# Optimizing a Trainium2 kernel written in Bass

```python
import math
import jax, jax.numpy as jnp
from jax import lax
import numpy as np

D_MODEL = 1024
BATCH = 1
SEQ = 256
DEPTH = 2

HEAD_DIM = 64
EPS = 1e-6
Q_BLOCK = 128
MOBA_HEADS = D_MODEL // 2 // HEAD_DIM
FOX_HEADS = D_MODEL // 2 // HEAD_DIM
MOBA_BLOCK = 256
MOBA_TOPK = 3
MOBA_Q_CHUNK = 16
DIFF_V_DIM = 2 * HEAD_DIM
DIFF_HEADS = D_MODEL // 2 // DIFF_V_DIM
SWA_Q_HEADS = D_MODEL // 2 // HEAD_DIM
SWA_KV_HEADS = SWA_Q_HEADS // 4
SWA_WINDOW = 128

N_AB = (DEPTH + 1) // 2
N_CD = DEPTH // 2

MOBA_W = MOBA_HEADS * HEAD_DIM
FOX_W = FOX_HEADS * HEAD_DIM
AB_SIZES = [MOBA_W, MOBA_W, MOBA_W, MOBA_W, FOX_W, FOX_W, FOX_W, FOX_W, FOX_HEADS]
AB_IN = sum(AB_SIZES)
DIFF_QK_W = DIFF_HEADS * 2 * HEAD_DIM
DIFF_W = DIFF_HEADS * DIFF_V_DIM
SWA_W = SWA_Q_HEADS * HEAD_DIM
SWA_KV_W = SWA_KV_HEADS * HEAD_DIM
CD_SIZES = [DIFF_QK_W, DIFF_QK_W, DIFF_W, DIFF_W, SWA_W, SWA_KV_W, SWA_KV_W, SWA_W]
CD_IN = sum(CD_SIZES)
MIX_W = D_MODEL


def rmsnorm(x, gain):
    xf = x.astype(jnp.float32)
    y = xf * lax.rsqrt(jnp.mean(xf * xf, axis=-1, keepdims=True) + EPS)
    return (y * gain.astype(jnp.float32)).astype(x.dtype)

def alibi_slopes(n):
    return jnp.asarray(2.0 ** (-8.0 * np.arange(1, n + 1) / n), dtype=jnp.float32)

def split_cols(t, sizes):
    idx = np.cumsum(sizes)[:-1].tolist()
    return jnp.split(t, idx, axis=-1)

def to_heads(t, n):
    b, s, _ = t.shape
    return t.reshape(b, s, n, -1).transpose(0, 2, 1, 3)

def from_heads(t):
    b, h, s, d = t.shape
    return t.transpose(0, 2, 1, 3).reshape(b, s, h * d)

def moba_attention(q, k, v, slopes):
    B, H, S, Dh = q.shape
    L = MOBA_BLOCK
    nb = -(-S // L)
    pad = nb * L - S
    kp = jnp.pad(k, ((0, 0), (0, 0), (0, pad), (0, 0)))
    vp = jnp.pad(v, ((0, 0), (0, 0), (0, pad), (0, 0)))
    kb = kp.reshape(B, H, nb, L, Dh)
    vb = vp.reshape(B, H, nb, L, Dh)
    kmean = jnp.mean(kb.astype(jnp.float32), axis=3)
    pos = jnp.arange(S)
    qblk = pos // L
    gate = jnp.einsum('bhsd,bhnd->bhsn', q.astype(jnp.float32), kmean)
    past = jnp.arange(nb)[None, :] < qblk[:, None]
    gate = jnp.where(past, gate, -jnp.inf)
    topk = min(MOBA_TOPK, nb)
    _, sel = lax.top_k(gate, topk)
    sel_valid = sel < qblk[None, None, :, None]
    scale = Dh ** -0.5
    bi = jnp.arange(B)[:, None, None, None]
    hi = jnp.arange(H)[None, :, None, None]
    C = MOBA_Q_CHUNK

    def chunk(c):
        start = c * C
        qc = lax.dynamic_slice_in_dim(q, start, C, axis=2)
        selc = lax.dynamic_slice_in_dim(sel, start, C, axis=2)
        validc = lax.dynamic_slice_in_dim(sel_valid, start, C, axis=2)
        tpos = start + jnp.arange(C)
        kg = kb[bi, hi, selc]
        vg = vb[bi, hi, selc]
        s_past = jnp.einsum('bhqd,bhqnld->bhqnl', qc, kg).astype(jnp.float32) * scale
        spos = selc[..., None] * L + jnp.arange(L)
        rel_p = (tpos[None, None, :, None, None] - spos).astype(jnp.float32)
        s_past = jnp.where(validc[..., None],
                           s_past - slopes[None, :, None, None, None] * rel_p, -jnp.inf)
        s_past = s_past.reshape(B, H, C, topk * L)
        own_start = (start // L) * L
        ko = lax.dynamic_slice_in_dim(kp, own_start, L, axis=2)
        vo = lax.dynamic_slice_in_dim(vp, own_start, L, axis=2)
        s_own = jnp.einsum('bhqd,bhld->bhql', qc, ko).astype(jnp.float32) * scale
        rel_o = tpos[:, None] - (own_start + jnp.arange(L))[None, :]
        s_own = jnp.where(rel_o >= 0,
                          s_own - slopes[None, :, None, None] * rel_o.astype(jnp.float32),
                          -jnp.inf)
        p = jax.nn.softmax(jnp.concatenate([s_past, s_own], axis=-1), axis=-1).astype(v.dtype)
        p_past = p[..., :topk * L].reshape(B, H, C, topk, L)
        p_own = p[..., topk * L:]
        return (jnp.einsum('bhqnl,bhqnld->bhqd', p_past, vg)
                + jnp.einsum('bhql,bhld->bhqd', p_own, vo))

    outs = lax.map(chunk, jnp.arange(S // C))
    return outs.transpose(1, 2, 0, 3, 4).reshape(B, H, S, Dh)

def fox_attention(q, k, v, log_f):
    B, H, S, Dh = q.shape
    c = jnp.cumsum(log_f, axis=-1)
    scale = Dh ** -0.5
    kpos = jnp.arange(S)

    def block(i):
        start = i * Q_BLOCK
        qb = lax.dynamic_slice_in_dim(q, start, Q_BLOCK, axis=2)
        cb = lax.dynamic_slice_in_dim(c, start, Q_BLOCK, axis=2)
        s = (jnp.einsum('bhqd,bhsd->bhqs', qb, k).astype(jnp.float32) * scale
             + cb[..., None] - c[:, :, None, :])
        tpos = start + jnp.arange(Q_BLOCK)
        s = jnp.where(tpos[:, None] >= kpos[None, :], s, -jnp.inf)
        p = jax.nn.softmax(s, axis=-1).astype(v.dtype)
        return jnp.einsum('bhqs,bhsd->bhqd', p, v)

    outs = lax.map(block, jnp.arange(S // Q_BLOCK))
    return outs.transpose(1, 2, 0, 3, 4).reshape(B, H, S, Dh)

def diff_attention(q, k, v, lam, slopes):
    B, H, S, _, Dh = q.shape
    scale = Dh ** -0.5
    kpos = jnp.arange(S)

    def block(i):
        start = i * Q_BLOCK
        qb = lax.dynamic_slice_in_dim(q, start, Q_BLOCK, axis=2)
        s = jnp.einsum('bhqcd,bhscd->bhcqs', qb, k).astype(jnp.float32) * scale
        rel = (start + jnp.arange(Q_BLOCK))[:, None] - kpos[None, :]
        s = jnp.where(rel >= 0,
                      s - slopes[None, :, None, None, None] * rel.astype(jnp.float32),
                      -jnp.inf)
        p = jax.nn.softmax(s, axis=-1)
        a = (p[:, :, 0] - lam * p[:, :, 1]).astype(v.dtype)
        return jnp.einsum('bhqs,bhse->bhqe', a, v)

    outs = lax.map(block, jnp.arange(S // Q_BLOCK))
    return outs.transpose(1, 2, 0, 3, 4).reshape(B, H, S, v.shape[-1])

def swa_attention(q, k, v, sinks, slopes):
    B, S, Hq, Dh = q.shape
    Hkv = k.shape[2]
    G = Hq // Hkv
    nb = S // Q_BLOCK
    qb = q.reshape(B, nb, Q_BLOCK, Hkv, G, Dh)
    kb = k.reshape(B, nb, Q_BLOCK, Hkv, Dh)
    vb = v.reshape(B, nb, Q_BLOCK, Hkv, Dh)
    pad = ((0, 0), (1, 0), (0, 0), (0, 0), (0, 0))
    kband = jnp.concatenate([jnp.pad(kb, pad)[:, :-1], kb], axis=2)
    vband = jnp.concatenate([jnp.pad(vb, pad)[:, :-1], vb], axis=2)
    s = jnp.einsum('bnqgrd,bnkgd->bngrqk', qb, kband).astype(jnp.float32) * (Dh ** -0.5)
    qi = jnp.arange(Q_BLOCK)
    ki = jnp.arange(2 * Q_BLOCK)
    rel = (Q_BLOCK + qi)[:, None] - ki[None, :]
    in_win = (rel >= 0) & (rel < SWA_WINDOW)
    has_prev = (jnp.arange(nb) > 0)[:, None, None] | (ki >= Q_BLOCK)[None, None, :]
    mask = in_win[None] & has_prev
    bias = -slopes.reshape(Hkv, G)[:, :, None, None] * rel.astype(jnp.float32)
    s = jnp.where(mask[None, :, None, None], s + bias, -jnp.inf)
    sink = jnp.broadcast_to(
        sinks.astype(jnp.float32).reshape(Hkv, G)[None, None, :, :, None, None],
        s.shape[:-1] + (1,))
    p = jax.nn.softmax(jnp.concatenate([s, sink], axis=-1), axis=-1)[..., :-1]
    out = jnp.einsum('bngrqk,bnkgd->bnqgrd', p.astype(v.dtype), vband)
    return out.reshape(B, S, Hq * Dh)

def first_inputs(seed: int = 0) -> dict:
    key = jax.random.key(seed)
    ks = jax.random.split(key, 20)
    f32 = jnp.float32
    nrm = lambda k, shp: jax.random.normal(k, shp, f32)
    gain = lambda k, shp: 1.0 + 0.05 * nrm(k, shp)
    return {
        "x": nrm(ks[0], (BATCH, SEQ, D_MODEL)),
        "norm_gain": gain(ks[1], (DEPTH, D_MODEL)),
        "w_in_ab": nrm(ks[2], (N_AB, D_MODEL, AB_IN)) * D_MODEL ** -0.5,
        "b_forget": 3.0 + 0.3 * nrm(ks[3], (N_AB, FOX_HEADS)),
        "moba_q_gain": gain(ks[4], (N_AB, HEAD_DIM)),
        "moba_k_gain": gain(ks[5], (N_AB, HEAD_DIM)),
        "fox_q_gain": gain(ks[6], (N_AB, HEAD_DIM)),
        "fox_k_gain": gain(ks[7], (N_AB, HEAD_DIM)),
        "w_out_ab": nrm(ks[8], (N_AB, MIX_W, D_MODEL)) * MIX_W ** -0.5,
        "w_in_cd": nrm(ks[9], (N_CD, D_MODEL, CD_IN)) * D_MODEL ** -0.5,
        "diff_q_gain": gain(ks[10], (N_CD, HEAD_DIM)),
        "diff_k_gain": gain(ks[11], (N_CD, HEAD_DIM)),
        "diff_lambda": 0.1 * nrm(ks[12], (N_CD, 4, HEAD_DIM)),
        "diff_subln_gain": gain(ks[13], (N_CD, DIFF_V_DIM)),
        "swa_q_gain": gain(ks[14], (N_CD, HEAD_DIM)),
        "swa_k_gain": gain(ks[15], (N_CD, HEAD_DIM)),
        "swa_sinks": nrm(ks[16], (N_CD, SWA_Q_HEADS)),
        "w_out_cd": nrm(ks[17], (N_CD, MIX_W, D_MODEL)) * MIX_W ** -0.5,
    }

def first_block(x, norm_gain, w_in_ab, b_forget, moba_q_gain, moba_k_gain, fox_q_gain,
              fox_k_gain, w_out_ab, w_in_cd, diff_q_gain, diff_k_gain, diff_lambda,
              diff_subln_gain, swa_q_gain, swa_k_gain, swa_sinks, w_out_cd):
    B, S, _ = x.shape
    moba_slopes = alibi_slopes(MOBA_HEADS)
    diff_slopes = alibi_slopes(DIFF_HEADS)
    swa_slopes = alibi_slopes(SWA_Q_HEADS)
    for layer in range(DEPTH):
        h = rmsnorm(x, norm_gain[layer])
        j = layer // 2
        if layer % 2 == 0:
            proj = h @ w_in_ab[j]
            qa, ka, va, ga, qb, kb_, vb_, gb, fb = split_cols(proj, AB_SIZES)
            qa = rmsnorm(to_heads(qa, MOBA_HEADS), moba_q_gain[j])
            ka = rmsnorm(to_heads(ka, MOBA_HEADS), moba_k_gain[j])
            ya = from_heads(moba_attention(qa, ka, to_heads(va, MOBA_HEADS), moba_slopes))
            qb = rmsnorm(to_heads(qb, FOX_HEADS), fox_q_gain[j])
            kb_ = rmsnorm(to_heads(kb_, FOX_HEADS), fox_k_gain[j])
            log_f = jax.nn.log_sigmoid(fb.astype(jnp.float32)
                                       + b_forget[j].astype(jnp.float32)).transpose(0, 2, 1)
            yb = from_heads(fox_attention(qb, kb_, to_heads(vb_, FOX_HEADS), log_f))
            y = jnp.concatenate([ya * jax.nn.silu(ga), yb * jax.nn.silu(gb)], axis=-1)
            x = x + y @ w_out_ab[j]
        else:
            proj = h @ w_in_cd[j]
            qc, kc, vc, gc, qd, kd, vd, gd = split_cols(proj, CD_SIZES)
            qc = rmsnorm(qc.reshape(B, S, DIFF_HEADS, 2, HEAD_DIM).transpose(0, 2, 1, 3, 4),
                         diff_q_gain[j])
            kc = rmsnorm(kc.reshape(B, S, DIFF_HEADS, 2, HEAD_DIM).transpose(0, 2, 1, 3, 4),
                         diff_k_gain[j])
            lam_init = 0.8 - 0.6 * math.exp(-0.3 * layer)
            lp = diff_lambda[j].astype(jnp.float32)
            lam = (jnp.exp(jnp.sum(lp[0] * lp[1])) - jnp.exp(jnp.sum(lp[2] * lp[3]))
                   + lam_init)
            oc = diff_attention(qc, kc, to_heads(vc, DIFF_HEADS), lam, diff_slopes)
            oc = rmsnorm(oc, diff_subln_gain[j]) * (1.0 - lam_init)
            yc = from_heads(oc)
            qd = rmsnorm(qd.reshape(B, S, SWA_Q_HEADS, HEAD_DIM), swa_q_gain[j])
            kd = rmsnorm(kd.reshape(B, S, SWA_KV_HEADS, HEAD_DIM), swa_k_gain[j])
            vd = vd.reshape(B, S, SWA_KV_HEADS, HEAD_DIM)
            yd = swa_attention(qd, kd, vd, swa_sinks[j], swa_slopes)
            y = jnp.concatenate([yc * jax.nn.silu(gc), yd * jax.nn.silu(gd)], axis=-1)
            x = x + y @ w_out_cd[j]
    return x


N_MIXERS = 2
N_MLA_LAYERS = (DEPTH + 1) // 2
N_SB_LAYERS = DEPTH // 2
BLOCK_Q = 128
MLA_HEADS = 8
MLA_Q_LORA = 384
MLA_KV_LORA = 256
MLA_NOPE = 128
MLA_ROPE = 64
MLA_V = 128
ROPE_THETA = 10000.0
POS_OFFSET_MAX = 4096
SB_HEADS = 8
SB_HEAD_DIM = D_MODEL // SB_HEADS
MEM_LEN = 256
MEM_HEADS = 4
MEM_HEAD_DIM = 128
D_FF = 4 * D_MODEL


NEG_BIG = -1e30

def rmsnorm_2(x, g):
    xf = x.astype(jnp.float32)
    y = xf * lax.rsqrt(jnp.mean(xf * xf, axis=-1, keepdims=True) + EPS)
    return (y * g.astype(jnp.float32)).astype(x.dtype)

def rope_tables(positions):
    inv_freq = ROPE_THETA ** (-jnp.arange(0, MLA_ROPE, 2, dtype=jnp.float32) / MLA_ROPE)
    ang = positions.astype(jnp.float32)[..., None] * inv_freq
    return jnp.cos(ang)[:, :, None, :], jnp.sin(ang)[:, :, None, :]

def apply_rope(x, cos, sin):
    half = x.shape[-1] // 2
    x1, x2 = x[..., :half], x[..., half:]
    c = cos.astype(x.dtype)
    s = sin.astype(x.dtype)
    return jnp.concatenate([x1 * c - x2 * s, x1 * s + x2 * c], axis=-1)

def blocked_causal_softmax_attn(q, k, v, scale):
    S = q.shape[1]
    outs = []
    for i in range(S // BLOCK_Q):
        lo, hi = i * BLOCK_Q, (i + 1) * BLOCK_Q
        s = jnp.einsum('bqhd,bkhd->bhqk', q[:, lo:hi], k[:, :hi]).astype(jnp.float32) * scale
        causal = (lo + jnp.arange(BLOCK_Q))[:, None] >= jnp.arange(hi)[None, :]
        p = jax.nn.softmax(jnp.where(causal, s, NEG_BIG), axis=-1).astype(v.dtype)
        outs.append(jnp.einsum('bhqk,bkhd->bqhd', p, v[:, :hi]))
    return jnp.concatenate(outs, axis=1)

def mla_mixer(h, cos, sin, w_dkv, g_q, g_kv, w_uq, w_ukv, w_o):
    B, S, _ = h.shape
    lat = h @ w_dkv
    c_q = rmsnorm_2(lat[..., :MLA_Q_LORA], g_q)
    c_kv = rmsnorm_2(lat[..., MLA_Q_LORA:MLA_Q_LORA + MLA_KV_LORA], g_kv)
    k_pe = lat[..., MLA_Q_LORA + MLA_KV_LORA:][:, :, None, :]
    q = (c_q @ w_uq).reshape(B, S, MLA_HEADS, MLA_NOPE + MLA_ROPE)
    kv = (c_kv @ w_ukv).reshape(B, S, MLA_HEADS, MLA_NOPE + MLA_V)
    q_pe = apply_rope(q[..., MLA_NOPE:], cos, sin)
    k_pe = apply_rope(k_pe, cos, sin)
    q = jnp.concatenate([q[..., :MLA_NOPE], q_pe], axis=-1)
    k = jnp.concatenate([kv[..., :MLA_NOPE],
                         jnp.broadcast_to(k_pe, (B, S, MLA_HEADS, MLA_ROPE))], axis=-1)
    v = kv[..., MLA_NOPE:]
    o = blocked_causal_softmax_attn(q, k, v, (MLA_NOPE + MLA_ROPE) ** -0.5)
    return o.reshape(B, S, MLA_HEADS * MLA_V) @ w_o

def stick_breaking_mixer(h, w_qkv, w_o):
    B, S, _ = h.shape
    qkv = (h @ w_qkv).reshape(B, S, 3, SB_HEADS, SB_HEAD_DIM)
    q, k, v = qkv[:, :, 0], qkv[:, :, 1], qkv[:, :, 2]
    scale = SB_HEAD_DIM ** -0.5
    outs = []
    for i in range(S // BLOCK_Q):
        lo, hi = i * BLOCK_Q, (i + 1) * BLOCK_Q
        z = jnp.einsum('bqhd,bkhd->bhqk', q[:, lo:hi], k[:, :hi]).astype(jnp.float32) * scale
        strict = jnp.arange(hi)[None, :] < (lo + jnp.arange(BLOCK_Q))[:, None]
        log_fail = jnp.where(strict, -jax.nn.softplus(z), 0.0)
        excl = lax.cumsum(log_fail, axis=3, reverse=True) - log_fail
        a = jnp.where(strict, jnp.exp(jax.nn.log_sigmoid(z) + excl), 0.0)
        outs.append(jnp.einsum('bhqk,bkhd->bqhd', a.astype(v.dtype), v[:, :hi]))
    o = jnp.concatenate(outs, axis=1)
    return o.reshape(B, S, SB_HEADS * SB_HEAD_DIM) @ w_o

def mem_cross_attn(h, m, w_q, w_kv, w_o):
    B, S, _ = h.shape
    q = (h @ w_q).reshape(B, S, MEM_HEADS, MEM_HEAD_DIM)
    kv = (m @ w_kv).reshape(B, m.shape[1], 2, MEM_HEADS, MEM_HEAD_DIM)
    s = jnp.einsum('bqhd,bmhd->bhqm', q, kv[:, :, 0]).astype(jnp.float32) * MEM_HEAD_DIM ** -0.5
    p = jax.nn.softmax(s, axis=-1).astype(h.dtype)
    o = jnp.einsum('bhqm,bmhd->bqhd', p, kv[:, :, 1])
    return o.reshape(B, S, MEM_HEADS * MEM_HEAD_DIM) @ w_o

def sq_relu_mlp(h, w_in, w_out):
    return jnp.square(jax.nn.relu(h @ w_in)) @ w_out

def second_inputs(seed: int = 0) -> dict:
    key = jax.random.key(seed)
    ks = iter(jax.random.split(key, 32))
    f32 = jnp.float32

    def w(shape, fan_in):
        return jax.random.normal(next(ks), shape, f32) * (fan_in ** -0.5)

    def gain(shape):
        return 1.0 + 0.02 * jax.random.normal(next(ks), shape, f32)

    x = jax.random.normal(next(ks), (BATCH, SEQ, D_MODEL), f32)
    mem = jax.random.normal(next(ks), (BATCH, MEM_LEN, D_MODEL), f32)
    offset = jax.random.randint(next(ks), (BATCH, 1), 0, POS_OFFSET_MAX, dtype=jnp.int32)
    positions = (offset + jnp.arange(SEQ, dtype=jnp.int32)[None, :]).astype(jnp.int32)
    return {
        "x": x,
        "mem": mem,
        "positions": positions,
        "norm_mix": gain((DEPTH, D_MODEL)),
        "norm_cross": gain((DEPTH, D_MODEL)),
        "norm_mem": gain((DEPTH, D_MODEL)),
        "norm_mlp": gain((DEPTH, D_MODEL)),
        "norm_final": gain((D_MODEL,)),
        "mla_w_dkv": w((N_MLA_LAYERS, D_MODEL, MLA_Q_LORA + MLA_KV_LORA + MLA_ROPE), D_MODEL),
        "mla_g_q": gain((N_MLA_LAYERS, MLA_Q_LORA)),
        "mla_g_kv": gain((N_MLA_LAYERS, MLA_KV_LORA)),
        "mla_w_uq": w((N_MLA_LAYERS, MLA_Q_LORA, MLA_HEADS * (MLA_NOPE + MLA_ROPE)), MLA_Q_LORA),
        "mla_w_ukv": w((N_MLA_LAYERS, MLA_KV_LORA, MLA_HEADS * (MLA_NOPE + MLA_V)), MLA_KV_LORA),
        "mla_w_o": w((N_MLA_LAYERS, MLA_HEADS * MLA_V, D_MODEL), MLA_HEADS * MLA_V),
        "sb_w_qkv": w((N_SB_LAYERS, D_MODEL, 3 * SB_HEADS * SB_HEAD_DIM), D_MODEL),
        "sb_w_o": w((N_SB_LAYERS, SB_HEADS * SB_HEAD_DIM, D_MODEL), SB_HEADS * SB_HEAD_DIM),
        "xa_w_q": w((DEPTH, D_MODEL, MEM_HEADS * MEM_HEAD_DIM), D_MODEL),
        "xa_w_kv": w((DEPTH, D_MODEL, 2 * MEM_HEADS * MEM_HEAD_DIM), D_MODEL),
        "xa_w_o": w((DEPTH, MEM_HEADS * MEM_HEAD_DIM, D_MODEL), MEM_HEADS * MEM_HEAD_DIM),
        "mlp_w_in": w((DEPTH, D_MODEL, D_FF), D_MODEL),
        "mlp_w_out": w((DEPTH, D_FF, D_MODEL), D_FF),
    }

def second_block(x, mem, positions, norm_mix, norm_cross, norm_mem, norm_mlp, norm_final,
              mla_w_dkv, mla_g_q, mla_g_kv, mla_w_uq, mla_w_ukv, mla_w_o,
              sb_w_qkv, sb_w_o, xa_w_q, xa_w_kv, xa_w_o, mlp_w_in, mlp_w_out):
    cos, sin = rope_tables(positions)
    h = x
    for i in range(DEPTH):
        a = rmsnorm_2(h, norm_mix[i])
        j = i // N_MIXERS
        if i % N_MIXERS == 0:
            h = h + mla_mixer(a, cos, sin, mla_w_dkv[j], mla_g_q[j], mla_g_kv[j],
                              mla_w_uq[j], mla_w_ukv[j], mla_w_o[j])
        else:
            h = h + stick_breaking_mixer(a, sb_w_qkv[j], sb_w_o[j])
        h = h + mem_cross_attn(rmsnorm_2(h, norm_cross[i]), rmsnorm_2(mem, norm_mem[i]),
                               xa_w_q[i], xa_w_kv[i], xa_w_o[i])
        h = h + sq_relu_mlp(rmsnorm_2(h, norm_mlp[i]), mlp_w_in[i], mlp_w_out[i])
    return rmsnorm_2(h, norm_final)


def setup_inputs(seed=0):
    out = dict(first_inputs(seed))
    for name, value in second_inputs(seed + 1).items():
        if name != "x":
            out[name + "_2"] = value
    return out


def reference(
    x, norm_gain, w_in_ab, b_forget, moba_q_gain, moba_k_gain, fox_q_gain, fox_k_gain, w_out_ab,
    w_in_cd, diff_q_gain, diff_k_gain, diff_lambda, diff_subln_gain, swa_q_gain, swa_k_gain,
    swa_sinks, w_out_cd, mem_2, positions_2, norm_mix_2, norm_cross_2, norm_mem_2, norm_mlp_2,
    norm_final_2, mla_w_dkv_2, mla_g_q_2, mla_g_kv_2, mla_w_uq_2, mla_w_ukv_2, mla_w_o_2,
    sb_w_qkv_2, sb_w_o_2, xa_w_q_2, xa_w_kv_2, xa_w_o_2, mlp_w_in_2, mlp_w_out_2,
):
    x = first_block(
        x, norm_gain, w_in_ab, b_forget, moba_q_gain, moba_k_gain, fox_q_gain, fox_k_gain,
        w_out_ab, w_in_cd, diff_q_gain, diff_k_gain, diff_lambda, diff_subln_gain, swa_q_gain,
        swa_k_gain, swa_sinks, w_out_cd,
    )
    return second_block(
        x, mem_2, positions_2, norm_mix_2, norm_cross_2, norm_mem_2, norm_mlp_2, norm_final_2,
        mla_w_dkv_2, mla_g_q_2, mla_g_kv_2, mla_w_uq_2, mla_w_ukv_2, mla_w_o_2, sb_w_qkv_2,
        sb_w_o_2, xa_w_q_2, xa_w_kv_2, xa_w_o_2, mlp_w_in_2, mlp_w_out_2,
    )


_drawn_inputs = setup_inputs


def setup_inputs(seed=0):
    import zlib

    import numpy as np

    out = dict(_drawn_inputs(seed))
    spreads = {}
    factors = {'moba_q_gain': 8.0,
     'moba_k_gain': 7.174,
     'fox_q_gain': 7.262,
     'fox_k_gain': 7.674,
     'diff_q_gain': 3.411,
     'diff_k_gain': 3.775,
     'diff_subln_gain': 3.5,
     'swa_q_gain': 8.0,
     'swa_k_gain': 8.0,
     'swa_sinks': 2.7,
     'norm_mix_2': 4.729,
     'norm_cross_2': 8.0,
     'norm_mem_2': 8.0,
     'norm_final_2': 7.863,
     'mla_g_q_2': 8.0,
     'mla_g_kv_2': 8.0,
     'norm_mlp_2': 3.301}
    for name, (base, spread) in spreads.items():
        noise = np.random.default_rng([zlib.crc32(name.encode()), seed]).standard_normal(out[name].shape)
        drawn = base * np.exp(spread * noise) if base else spread * noise
        out[name] = __import__('jax').numpy.asarray(drawn.astype(out[name].dtype))
    for name, factor in factors.items():
        out[name] = (out[name] * factor).astype(out[name].dtype)
    return out
```

```python
import math
from contextlib import ExitStack

import numpy as np

import concourse.bass as bass
from concourse import mybir

ALU = mybir.AluOpType
ACT = mybir.ActivationFunctionType
AX_X = mybir.AxisListType.X
F32 = mybir.dt.float32
F32R = mybir.dt.float32r
I32 = mybir.dt.int32

P = 128
D = 1024
S = 256
T = S // P
KC = D // P
PANEL = 512
UNIT = 2048
RAW = 2
RING = 4
EPS = 1e-6
BIG = 1e30
HD = 64
HEADS = 8
DFF = 4 * D
BLK = 512
NBLK = DFF // BLK
MLA_QL, MLA_KVL, NOPE, ROPE, MLA_V = 384, 256, 128, 64, 128
LAM_INIT = 0.8 - 0.6 * math.exp(-0.3)
TWO_PI_HI = 6.28125
GATE_ROWS = (0, 32, 64, 96)
ROWS = 104
MLA_PANELS = (4, 5, 7)


def two_pi_parts():
    hi = TWO_PI_HI
    rest = 2 * math.pi - hi
    mid = math.floor(rest * 2 ** 20) / 2 ** 20
    return hi, mid, rest - mid


class Order:

    def __init__(self, eng, chain):
        self.eng, self.chain, self.counts, self.last = eng, chain, {}, None

    def sig(self, ins, sem=None, value=None, loop=0):
        sem = self.chain if sem is None else sem
        ins.then_inc(sem, 1)
        if value is None:
            self.counts[sem.name] = self.counts.get(sem.name, 0) + 1
            value = self.counts[sem.name] + loop
        self.last = (sem, value)
        return value

    def settle(self):
        self.eng.wait_ge(*self.last)


def weight_units(A):
    names, units = {}, []

    def rows(w):
        return w.rearrange("(c p) n -> p c n", p=P)

    def add(name, width, *pieces):
        names[name] = len(units)
        units.append((width, pieces))

    def panel(name, w, c0, cols, chunks, per):
        for n in range(chunks // per):
            add((name, n), per * cols, (0, per, cols, cols, rows(w)[:, n * per:(n + 1) * per, c0:c0 + cols]))

    ab, cd = A["w_in_ab"][0], A["w_in_cd"][0]
    for n, c in (("qa", 0), ("ka", 1), ("va", 2), ("ga", 3), ("qb", 4), ("kb", 5)):
        panel(n, ab, c * PANEL, PANEL, KC, 4)
    f0 = 8 * PANEL
    add(("f", 0), KC * P, (0, KC, 8, P, rows(ab)[:, :, f0:f0 + 8]),
        *((c, KC, 32, P, rows(ab)[:, :, f0 - 24:f0 + 8]) for c in (8, 40, 72)), (104, KC, 24, P, rows(ab)[:, :, 0:24]))
    for n, c in (("vb", 6), ("gb", 7)):
        panel(n, ab, c * PANEL, PANEL, KC, 4)

    def memory(i):
        for n in range(4):
            panel(("xkv", i, n), A["xa_w_kv_2"][i], n * 256, 256, KC, KC)

    for n in range(2):
        panel(("oab", n), A["w_out_ab"][0], n * PANEL, PANEL, KC, 4)
    for n, c in (("qc", 0), ("kc", 1), ("vc", 2), ("gc", 3), ("qd", 4)):
        panel(n, cd, c * PANEL, PANEL, KC, 4)
    panel("kvd", cd, 5 * PANEL, 256, KC, KC)
    panel("gd", cd, 5 * PANEL + 256, PANEL, KC, 4)
    memory(0)
    for n in range(2):
        panel(("ocd", n), A["w_out_cd"][0], n * PANEL, PANEL, KC, 4)
    dkv = A["mla_w_dkv_2"][0]
    panel("dq", dkv, 0, MLA_QL, KC, 4)
    panel("dk", dkv, MLA_QL, MLA_KVL, KC, KC)
    pe0 = MLA_QL + MLA_KVL
    add(("dp", 0), KC * P, (0, KC, 64, P, rows(dkv)[:, :, pe0:pe0 + 64]),
        (64, KC, 32, P, rows(dkv)[:, :, pe0 + 32:pe0 + 64]), (96, KC, 32, P, rows(dkv)[:, :, pe0:pe0 + 32]))
    uq, ukv = rows(A["mla_w_uq_2"][0]), rows(A["mla_w_ukv_2"][0])
    for h in range(HEADS):
        c, k = h * (NOPE + ROPE), h * (NOPE + MLA_V)
        add(("uh", h), 3 * 256 + 2 * 256,
            (0, 3, 192, 256, uq[:, :, c:c + 192]), (192, 3, 32, 256, uq[:, :, c + 160:c + 192]),
            (224, 3, 32, 256, uq[:, :, c + 128:c + 160]), (768, 2, 256, 256, ukv[:, :, k:k + 256]))
    for n in range(2):
        panel(("omla", n), A["mla_w_o_2"][0], n * PANEL, PANEL, KC, 4)

    def cross(i):
        for n in range(2):
            panel(("xq", i, n), A["xa_w_q_2"][i], n * 256, 256, KC, KC)
        for n in range(2):
            panel(("xo", i, n), A["xa_w_o_2"][i], n * PANEL, PANEL, 4, 4)

    def mlp(i):
        names[("mlp", i)] = len(units)
        win, wout = rows(A["mlp_w_in_2"][i]), rows(A["mlp_w_out_2"][i])

        def up(b):
            for n in range(2):
                add(("up", i, b, n), UNIT, (0, 4, BLK, BLK, win[:, 4 * n:4 * n + 4, b * BLK:(b + 1) * BLK]))

        def down(b):
            for n in range(2):
                add(("down", i, b, n), UNIT, (0, 4, PANEL, PANEL, wout[:, 4 * b:4 * b + 4, n * PANEL:(n + 1) * PANEL]))
        up(0)
        for b in range(1, NBLK):
            up(b)
            down(b - 1)
        down(NBLK - 1)

    cross(0)
    mlp(0)
    sb = A["sb_w_qkv_2"][0]
    for n in range(4):
        panel(("sv", n), sb, 2 * D + n * 256, 256, KC, KC)
    for h in range(HEADS):
        add(("sqk", h), UNIT, (0, KC, P, 256, rows(sb)[:, :, h * P:(h + 1) * P]),
            (P, KC, P, 256, rows(sb)[:, :, D + h * P:D + (h + 1) * P]))
    for n in range(2):
        panel(("osb", n), A["sb_w_o_2"][0], n * PANEL, PANEL, KC, 4)
    memory(1)
    cross(1)
    mlp(1)
    return names, units


def build(nc, A, out):
    names, units = weight_units(A)
    loaded, per_slot = [], [0] * RAW
    for u, (_, pieces) in enumerate(units):
        per_slot[u % RAW] += 16 * len(pieces)
        loaded.append(per_slot[u % RAW])

    with ExitStack() as ctx:
        def sb(name, shape, dt=F32):
            return ctx.enter_context(nc.sbuf_tensor(name, shape, dt))

        def sem(name):
            return ctx.enter_context(nc.semaphore(name))

        raw = sb("raw", [P, RAW, UNIT])
        w_hi = sb("w_hi", [P, RING, UNIT], F32R)
        w_lo = sb("w_lo", [P, RING, UNIT], F32R)
        xT_hi = sb("xT_hi", [P, KC, S], F32R)
        xT_lo = sb("xT_lo", [P, KC, S], F32R)
        hT_hi = sb("hT_hi", [P, KC, S], F32R)
        hT_lo = sb("hT_lo", [P, KC, S], F32R)
        x = sb("x", [P, T, D])
        xn = sb("xn", [P, T, D])
        arena = sb("arena", [P, 12, 1024])
        ident = sb("ident", [P, P])
        rel = sb("rel", [P, 384])
        causal = sb("causal", [P, 384])
        alibi = sb("alibi", [P, 2, 384])
        gains = sb("gains", [P, P])
        rope = sb("rope", [P, S])
        nl3 = sb("nl3", [P, 2, 384])
        pb3 = sb("pb3", [P, 2, 384])
        pt3 = sb("pt3", [P, 2, 384])
        mem = sb("mem", [P, T, D])
        mem_k = mem[:, 0, :].rearrange("p (h s) -> p h s", h=4)
        mem_v = mem[:, 1, :].rearrange("p (t n) -> p t n", t=T)
        NST = 160
        ssq, var, lnv, guess, tmp, rstd = (sb(n, [P, NST]) for n in ("ssq", "var", "lnv", "guess", "tmp", "rstd"))
        NH = 2 * 64
        nmax, esum, rsum = (sb(n, [P, NH]) for n in ("nmax", "esum", "rsum"))
        small = sb("small", [P, 64])
        banks = [ctx.enter_context(nc.psum_tensor(f"bank{b}", [P, PANEL], F32)) for b in range(8)]

        SINK, NSINK, LAM, NLAM, BF, INVF, PHASE, TURN, NLR, ESINK = 0, 8, 16, 18, 20, 21, 22, 23, 24, 32
        col = lambda c, n=1: small[:, c:c + n]

        def pan(n, t=None):
            a = arena[:, n, :]
            return a if t is None else a[:, t * PANEL:(t + 1) * PANEL]

        w_in = [sem(f"w_in{n}") for n in range(RAW)]
        hi_ready, lo_ready = sem("hi_ready"), sem("lo_ready")
        units_used = sem("units_used")
        written = [sem(f"written{b}") for b in range(8)]
        read = [sem(f"read{b}") for b in range(8)]
        dve_chain, act_chain, pool_chain = sem("dve_chain"), sem("act_chain"), sem("pool_chain")
        x_in, stage_in, small_in, mem_in, final_in = (sem(n) for n in ("x_in", "stage_in", "small_in", "mem_in", "final_in"))
        x_ready, squares_ready, var_ready, guess_ready = (sem(n) for n in ("x_ready", "squares_ready", "var_ready", "guess_ready"))
        xn_ready, hiT_ready, loT_ready = sem("xn_ready"), sem("hiT_ready"), sem("loT_ready")
        scratch_ready = sem("scratch_ready")
        tok_ready = sem("tok_ready")
        qkT_ready = sem("qkT_ready")
        copied, roped = sem("copied"), sem("roped")
        logits_ready, probs_ready, probsT_ready, y_ready = (sem(n) for n in ("logits_ready", "probs_ready", "probsT_ready", "y_ready"))
        norm_ready = sem("norm_ready")
        table_ready = sem("table_ready")
        fox_const, fox_gate, fox_log, fox_ready = sem("fox_const"), sem("fox_gate"), sem("fox_log"), sem("fox_ready")
        sb_log, sb_w, angle_ready, sine_ready, lam_sum, lam_exp, gains_ready = (sem(n) for n in ("sb_log", "sb_w", "angle_ready", "sine_ready", "lam_sum", "lam_exp", "gains_ready"))
        relu_ready, h_ready, hhi_ready, hT_ready = (sem(n) for n in ("relu_ready", "h_ready", "hhi_ready", "hT_ready"))
        setup_ready, out_ready, out_done = sem("setup_ready"), sem("out_ready"), sem("out_done")

        stage = arena[:, 11, 0:P]
        gain_of, stage_rows = {}, 0
        gain_loads = []
        for key, ap in (("norm", A["norm_gain"]), ("mix", A["norm_mix_2"]), ("cross", A["norm_cross_2"]),
                        ("mem", A["norm_mem_2"]), ("mlp", A["norm_mlp_2"])):
            for i in range(2):
                gain_of[key, i] = stage_rows
                gain_loads.append((stage_rows, KC, 0, P, ap[i].rearrange("(c p) -> c p", p=P)))
                stage_rows += KC
        for key, ap, n in (("gq", A["mla_g_q_2"], 3), ("gkv", A["mla_g_kv_2"], 2), ("sub", A["diff_subln_gain"], 1)):
            gain_of[key] = stage_rows
            gain_loads.append((stage_rows, n, 0, P, ap[0].rearrange("(c p) -> c p", p=P)))
            stage_rows += n
        for key in ("moba_q", "moba_k", "fox_q", "fox_k", "diff_q", "diff_k", "swa_q", "swa_k"):
            gain_of[key] = stage_rows
            for half in range(2):
                gain_loads.append((stage_rows, 1, half * HD, HD, A[key + "_gain"]))
            stage_rows += 1
        assert stage_rows <= P

        def gain(key, n=0):
            c = gain_of[key] + n
            return gains[:, c:c + 1]

        CAUSAL = [(0, 0, 0), (1, 0, P), (1, 1, 2 * P)]
        FULL = [(0, 0, 0), (1, 0, 256), (0, 1, 128), (1, 1, 384)]
        heads = []

        def head(kind, h, **k):
            k.update(kind=kind, h=h, g=len(heads), blocks=CAUSAL, spans=[(0, P), (P, 384)])
            n = len(heads) % 2
            k.update(nl=nl3[:, n], pb=pb3[:, n], pt=pt3[:, n])
            if kind == "xa":
                k.update(blocks=FULL, spans=[(0, 256), (256, 512)])
                k.update(nl=pan(1, n), pb=pan(2, n), pt=pan(3, n))
            heads.append(k)

        def chunked(panel, chunk, part, a, b):
            return arena[part * HD:(part + 1) * HD, panel, chunk * S + a:chunk * S + b]

        tables = []

        def slope(h):
            return 2.0 ** -(h + 1)

        for h in range(HEADS):
            tables.append((len(heads), -slope(h), "rel"))
            head("moba", h, scale=1.0, table=len(tables) - 1, v=lambda kt, h=h: arena[:, 2, kt * PANEL + h * HD:kt * PANEL + (h + 1) * HD], vd=HD,
                 parts=[lambda a, b, h=h: chunked(8, h // 2, h % 2, a, b)], keys=[lambda a, b, h=h: chunked(9, h // 2, h % 2, a, b)],
                 gate=lambda t, h=h: arena[:, 3, t * PANEL + h * HD:t * PANEL + (h + 1) * HD])
        foxL = arena[0:ROWS, 10:12, :].rearrange("p a n -> p (a n)").rearrange("p (h s) -> p h s", h=HEADS)
        foxR = arena[0:ROWS, 4:6, :].rearrange("p a n -> p (a n)").rearrange("p (h s) -> p h s", h=HEADS)
        for h in range(HEADS):
            head("fox", h, scale=1.0, table=None, v=lambda kt, h=h: arena[:, 6, kt * PANEL + h * HD:kt * PANEL + (h + 1) * HD], vd=HD,
                 parts=[lambda a, b, h=h: chunked(0, h // 2, h % 2, a, b), lambda a, b, h=h: foxL[HD * (h % 2):HD * (h % 2) + 40, h, a:b]],
                 keys=[lambda a, b, h=h: chunked(1, h // 2, h % 2, a, b), lambda a, b, h=h: foxR[HD * (h % 2):HD * (h % 2) + 40, h, a:b]],
                 gate=lambda t, h=h: arena[:, 7, t * PANEL + h * HD:t * PANEL + (h + 1) * HD])
        for h in range(4):
            tables.append((len(heads), -(2.0 ** -(2 * h + 2)), "rel"))
            for c in range(2):
                head("diff", h, c=c, scale=1.0, table=len(tables) - 1, v=lambda kt, h=h: arena[:, 2, kt * PANEL + h * P:kt * PANEL + (h + 1) * P], vd=P,
                     parts=[lambda a, b, h=h, c=c: chunked(8, h, c, a, b)], keys=[lambda a, b, h=h, c=c: chunked(9, h, c, a, b)],
                     gate=lambda t, h=h: arena[:, 3, t * PANEL + h * P:t * PANEL + (h + 1) * P])
        vd_tok = arena[:, 5, 512:768].rearrange("p (t n) -> p t n", t=T)
        for h in range(HEADS):
            tables.append((len(heads), -slope(h), "window"))
            head("swa", h, scale=1.0, table=len(tables) - 1, v=lambda kt, n=h // 4: vd_tok[:, kt, n * HD:(n + 1) * HD], vd=HD,
                 parts=[lambda a, b, h=h: chunked(10, h // 2, h % 2, a, b)], keys=[lambda a, b, h=h: chunked(7, h // 4, h % 2, a, b)],
                 gate=lambda t, h=h: arena[:, 6, t * PANEL + h * HD:t * PANEL + (h + 1) * HD])

        def mla_buf(h, n):
            return arena[:, MLA_PANELS[h % 3], n * S:(n + 1) * S]
        krope = arena[:, 6, 0:S]
        ksum_in = arena[:, 6, S:2 * S]
        halves = arena[:, 6, 2 * S:2 * S + P]
        for h in range(HEADS):
            head("mla", h, scale=(NOPE + ROPE) ** -0.5, table=None, vd=P,
                 parts=[lambda a, b, h=h: mla_buf(h, 0)[:, a:b], lambda a, b, h=h: mla_buf(h, 1)[:, a:b]],
                 keys=[lambda a, b, h=h: mla_buf(h, 2)[:, a:b], lambda a, b: krope[:, a:b]],
                 v=lambda kt, h=h: mla_buf(h, 3)[:, kt * P:(kt + 1) * P])
        for i in range(2):
            if i == 1:
                for h in range(HEADS):
                    head("sb", h, scale=P ** -0.5, table=None, vd=P, parts=[], keys=[],
                         v=lambda kt, h=h: sb_v[:, kt, h * P:(h + 1) * P])
            for h in range(4):
                head("xa", h, layer=i, scale=P ** -0.5, table=None, vd=P,
                     parts=[lambda a, b, h=h: arena[:, 0, h * S + a:h * S + b]], keys=[lambda a, b, h=h: mem_k[:, h, a:b]],
                     v=lambda kt, h=h: mem_v[:, kt, h * P:(h + 1) * P])

        turns = outputs = norms = 0
        for k in heads:
            first_map = k["kind"] == "diff" and k["c"] == 0
            turns += not first_map
            outputs += k["kind"] in ("moba", "fox", "swa") or k["kind"] == "diff" and k["c"] == 1
            norms += k["kind"] in ("mla", "xa") or k["kind"] == "diff" and k["c"] == 1
            k.update(turn=turns, output=outputs, norm=norms)
        qkT_needed = {"moba": 4, "fox": 8, "diff": 12, "swa": 15}
        xcount = {k: 4 * n for n, k in enumerate(("oab", "ocd", "omla", ("xo", 0), ("mlp", 0), "osb", ("xo", 1), ("mlp", 1)))}
        copied_at = {"krope": 1}
        for h in range(HEADS):
            copied_at["q", h], copied_at["kv", h] = 2 * h + 2, 2 * h + 3
            copied_at["sqk", h] = 2 * HEADS + 4 + h
        for i in range(2):
            for n in range(2):
                copied_at["xq", i, n] = 2 * HEADS + 2 + n + i * (HEADS + 2)

        def heads_of(kind, **want):
            return [k for k in heads if k["kind"] == kind and all(k[a] == b for a, b in want.items())]

        for k in heads:
            k["tab"] = (lambda a, b: causal[:, a:b]) if k["table"] is None else (lambda a, b, n=k["table"]: alibi[:, n % 2, a:b])
            if k["kind"] == "xa":
                k["tab"] = lambda a, b: causal[:, P:2 * P].unsqueeze(1).to_broadcast([P, 2, P])

        sb_v = arena[:, 0:2, :]
        sb_qk = lambda h: pan(2, h % 2)
        strict = arena[:, 3, 0:384]
        sbuf_of = lambda n, h: arena[:, 4 + n, (h % 2) * 384:(h % 2) * 384 + 384]

        final_gain = pan(6)
        hT_blocks = lambda a: a[:, :, :].rearrange("p c s -> p (c s)").rearrange("p (b n) -> p b n", b=4)

        products = {}
        mlp_base = {}
        released = {}

        def flat(buf, u):
            return buf[:, u % RING, :]

        block = ctx.enter_context(nc.Block())

        @block.tensor
        def _(pe):
            uses = [0] * 8
            freed = [None] * 8
            reads = [0] * 8
            state = {"loT": 0, "xn": 0, "tok": 0, "act": 0, "dve": 0, "qkT": 0}

            def begin(name, b):
                for one in freed[b] or ():
                    pe.wait_ge(*one)
                freed[b] = None
                products[name] = b

            def end(name, ins, free=None):
                b = products[name]
                uses[b] += 1
                ins.then_inc(written[b], 1)
                products[name] = (b, written[b], uses[b])
                release(name, b, free)

            def end_with_unit(name, u, free=None):
                b = products[name]
                products[name] = (b, units_used, u + 1)
                release(name, b, free)

            def release(name, b, free):
                if free is None:
                    reads[b] += 1
                    free = (read[b], reads[b])
                freed[b] = released[name] = free if isinstance(free, list) else [free]

            def take(u):
                pe.wait_ge(lo_ready, u + 1)

            def three(o, w, i, s, start, stop):
                (wh, wl), (ih, il) = w, i
                pe.matmul(o, wh, ih, start=start, stop=False, skip_group_check=True)
                pe.matmul(o, wh, il, start=False, stop=False, skip_group_check=True)
                return pe.matmul(o, wl, ih, start=False, stop=stop, skip_group_check=True)

            def tokens(name, us, cols, chunks, lhs, ready, b0, free=(None, None), one_bank=False, width=None, c0=0):
                width = width or cols
                for n, u in enumerate(us):
                    take(u)
                    wh, wl = (flat(w, u)[:, c0:c0 + chunks * width].rearrange("p (c n) -> p c n", n=width) for w in (w_hi, w_lo))
                    for t in range(T):
                        b = b0 if one_bank else b0 + t
                        if n == 0:
                            if not one_bank or t == 0:
                                begin((name, t) if not one_bank else name, b)
                        o = banks[b][:, t * cols:(t + 1) * cols] if one_bank else banks[b][:, 0:cols]
                        for c in range(chunks):
                            k = n * chunks + c
                            if n == 0 and t == 0 or n and t == 0:
                                pe.wait_ge(*ready(k))
                            a = [v[:, k, t * P:(t + 1) * P] for v in lhs]
                            ins = three(o, a, (wh[:, c, 0:cols], wl[:, c, 0:cols]), u,
                                        n == 0 and c == 0, n == len(us) - 1 and c == chunks - 1)
                        if n == len(us) - 1 and t == 0 and not one_bank:
                            end((name, 0), ins, free[0])
                    ins.then_inc(units_used, 1)
                    if n == len(us) - 1:
                        end_with_unit(name if one_bank else (name, 1), u, free[-1])

            def features(name, o, u, chunks, width, c0, rhs, ready, last, free=None, m=P, start=True):
                wh, wl = (flat(w, u)[:, 0:].rearrange("p n -> p n") for w in (w_hi, w_lo))
                for c in range(chunks):
                    pe.wait_ge(*ready(c))
                    a = [v[:, c0 + c * width:c0 + c * width + m] for v in (wh, wl)]
                    ins = three(o, a, [v[:, c, :] for v in rhs], u, start and c == 0, c == chunks - 1)
                return ins

            def chunks_ready(base):
                return lambda c: (loT_ready, base + c + 1)

            def transposes(name, src, chunks, ready, b0=4):
                for t in range(T):
                    pe.wait_ge(*ready(t))
                    for c in range(chunks):
                        b = b0 + c // 2
                        if t == 0 and c % 2 == 0:
                            begin((name, c // 2), b)
                        o = banks[b][:, (c % 2) * S + t * P:(c % 2) * S + (t + 1) * P]
                        ins = pe.transpose(o, src(t, c), ident[:, :])
                        if t == T - 1 and (c % 2 == 1 or c == chunks - 1):
                            n = state["loT"] + c + 1
                            end((name, c // 2), ins, (loT_ready, n))
                base = state["loT"]
                state["loT"] += chunks
                return chunks_ready(base)

            def norm(name, chunks=KC, src=None, b0=4):
                n = state["xn"]
                state["xn"] += T
                src = src or (lambda t, c: xn[:, t, c * P:(c + 1) * P])
                return transposes(name, src, chunks, lambda t: (xn_ready, n + t + 1), b0)

            def qk_transposes(name, panel, chunks=4):
                state["tok"] += 1
                pe.wait_ge(tok_ready, state["tok"])
                for pair in range(chunks // 2):
                    begin((name, "T", pair), 6)
                    for c in range(2 * pair, 2 * pair + 2):
                        for t in range(T):
                            o = banks[6][:, (c % 2) * S + t * P:(c % 2) * S + (t + 1) * P]
                            w = PANEL * chunks // 4
                            ins = pe.transpose(o, arena[:, panel, t * w + c * P:t * w + (c + 1) * P], ident[:, :])
                    state["qkT"] += 1
                    end((name, "T", pair), ins, (qkT_ready, state["qkT"]))

            def scores(k):
                g = k["g"]
                b = 4 + g % 2
                begin(("S", g), b)
                if k["kind"] in ("moba", "fox", "diff", "swa"):
                    pe.wait_ge(qkT_ready, qkT_needed[k["kind"]])
                    if k["kind"] == "fox":
                        pe.wait_ge(fox_ready, 2)
                for t, (a, z) in enumerate(k["spans"]):
                    keys = z - a
                    for n, (q, kk) in enumerate(zip(k["parts"], k["keys"])):
                        ins = pe.matmul(banks[b][:, a:z], q(t * P, (t + 1) * P), kk(0, keys),
                                        start=n == 0, stop=n == len(k["parts"]) - 1)
                end(("S", g), ins, (logits_ready, g + 1))

            def turn_probs(k):
                g = k["g"]
                begin(("PT", g), 6)
                if k["kind"] in ("moba", "fox", "swa", "sb"):
                    pe.wait_ge(probs_ready, g + 1)
                else:
                    pe.wait_ge(norm_ready, k["norm"])
                src = k["nl"] if k["kind"] == "diff" else k["pb"]
                for n, (t, kt, a) in enumerate(k["blocks"]):
                    a = a if k["kind"] != "xa" else t * S + kt * P
                    ins = pe.transpose(banks[6][:, n * P:(n + 1) * P], src[:, a:a + P], ident[:, :])
                end(("PT", g), ins, (probsT_ready, k["turn"]))

            def values(k):
                g, vd = k["g"], k["vd"]
                begin(("Y", g), 7)
                pe.wait_ge(probsT_ready, k["turn"])
                for t in range(T):
                    mine = [(n, kt) for n, (tt, kt, _) in enumerate(k["blocks"]) if tt == t]
                    for m, (n, kt) in enumerate(mine):
                        ins = pe.matmul(banks[7][:, t * vd:(t + 1) * vd], k["pt"][:, n * P:(n + 1) * P], k["v"](kt),
                                        start=m == 0, stop=m == len(mine) - 1)
                end(("Y", g), ins, (y_ready, k["output"]))

            def values_T(k, name, pt, v, full=False):
                begin(name, 7)
                o = banks[7][:, 0:S]
                if full:
                    pe.matmul(o, v(0), pt[:, 0:S], start=True, stop=False)
                    ins = pe.matmul(o, v(1), pt[:, S:2 * S], start=False, stop=True)
                else:
                    pe.matmul(o[:, 0:P], v(0), pt[:, 0:P], start=True, stop=True)
                    pe.matmul(o[:, P:S], v(0), pt[:, P:S], start=True, stop=False)
                    ins = pe.matmul(o[:, P:S], v(1), pt[:, S:S + P], start=False, stop=True)
                state["loT"] += 1
                end(name, ins, (loT_ready, state["loT"]))

            X = (xT_hi, xT_lo)
            H = (hT_hi, hT_lo)

            def two(name):
                return [names[name, 0], names[name, 1]]

            tok_of = {"qa": 1, "ka": 2, "qb": 3, "kb": 4, "qc": 5, "kc": 6, "qd": 7, "kvd": 8}

            def second_free(name):
                return (tok_ready, tok_of[name]) if name in tok_of else None

            def plain(name, b0, ready, lhs=X):
                tokens(name, two(name), PANEL, 4, lhs, ready, b0, free=(None, second_free(name)))

            def project(name, lhs, ready, chunks=KC):
                for n in range(2):
                    us = two((name, n)) if chunks == KC else [names[(name[0], name[1], n), 0]]
                    tokens(("o", name, n), us, PANEL, 4, lhs, ready, 2 * n,
                           free=((x_ready, xcount[name] + 2 * n + 1), (x_ready, xcount[name] + 2 * n + 2)))

            pe.wait_ge(stage_in, 16 * len(gain_loads))
            pe.wait_ge(setup_ready, 1)
            begin("gains", 0)
            end("gains", pe.transpose(banks[0][:, 0:P], stage[:, :], ident[:, :]))
            begin("freq", 1)
            end("freq", pe.matmul(banks[1][:, 0:1], arena[0:1, 9, 0:P], arena[0:1, 9, P:P + 1], start=True, stop=True))

            r = norm(("n", 0))
            plain("qa", 0, r)
            plain("ka", 2, r)
            qk_transposes("qa", 0)
            plain("va", 0, r)
            qk_transposes("ka", 1)
            plain("ga", 2, r)
            fill = [lambda: tok_unit("qb", 0), lambda: tok_unit("qb", 1), lambda: tok_unit("kb", 0), lambda: tok_unit("kb", 1),
                    lambda: fgate(r), lambda: tok_unit("vb", 0), lambda: tok_unit("vb", 1)]
            where = {"qb": 0, "kb": 2, "vb": 0, "gb": 2, "gc": 2, "qd": 0, "gd": 0}

            def tok_unit(name, n):
                u = names[name, n]
                take(u)
                b0 = where[name]
                wh, wl = (flat(w, u).rearrange("p (c n) -> p c n", n=PANEL) for w in (w_hi, w_lo))
                for t in range(T):
                    if n == 0:
                        begin((name, t), b0 + t)
                    for c in range(4):
                        k = 4 * n + c
                        a = [v[:, k, t * P:(t + 1) * P] for v in X]
                        ins = three(banks[b0 + t][:, :], a, (wh[:, c, :], wl[:, c, :]), u, n == 0 and c == 0, n == 1 and c == 3)
                    if n == 1 and t == 0:
                        end((name, 0), ins)
                ins.then_inc(units_used, 1)
                if n == 1:
                    end_with_unit((name, 1), u, second_free(name))

            def fgate(ready):
                u = names["f", 0]
                take(u)
                begin("f", 0)
                ins = features("f", banks[0][:, 0:S], u, KC, P, 0, X, ready, True)
                ins.then_inc(units_used, 1)
                end_with_unit("f", u)

            def mem_unit(i, n, ready):
                u = names[("xkv", i, n), 0]
                b = n % 4
                if n < 2:
                    take(u)
                    begin(("mem", i, n), b)
                    for h in range(2):
                        ins = features("", banks[b][:, h * S:(h + 1) * S], u, KC, S, h * P, X, ready, True)
                    ins.then_inc(units_used, 1)
                    end_with_unit(("mem", i, n), u)
                else:
                    tokens(("mem", i, n), [u], 256, KC, X, ready, b, one_bank=True)

            def pipeline(ks, fill, extra={}, lag=1):
                fill = list(fill)
                for i in range(len(ks) + 2):
                    if 1 <= i <= len(ks):
                        turn_probs(ks[i - 1])
                    if 2 <= i:
                        values(ks[i - 2])
                    if i < len(ks):
                        scores(ks[i])
                    if fill:
                        fill.pop(0)()
                    for e in extra.get(i, []):
                        e()
                assert not fill

            pipeline(heads_of("moba"), fill, {4: [lambda: qk_transposes("qb", 4)], 6: [lambda: qk_transposes("kb", 5)]})

            def gated(name, panel, b0, need):
                return transposes(name, lambda t, c: arena[:, panel, t * PANEL + c * P:t * PANEL + (c + 1) * P],
                                  4, lambda t: (y_ready, need), b0)

            yr = []
            pipeline(heads_of("fox"), [lambda: tok_unit("gb", 0), lambda: tok_unit("gb", 1)],
                     {5: [lambda: yr.append(gated("yab0", 3, 0, heads_of("moba")[-1]["output"]))]})
            gated("yab1", 7, 2, heads_of("fox")[-1]["output"])
            project("oab", X, yr[0])

            r = norm(("n", 1))
            plain("qc", 0, r)
            plain("kc", 2, r)
            qk_transposes("qc", 0)
            plain("vc", 0, r)
            qk_transposes("kc", 1)
            plain("gc", 2, r)

            def kvd():
                tokens("kvd", [names["kvd", 0]], 256, KC, X, r, 2, one_bank=True, free=(second_free("kvd"),))

            dh = heads_of("diff")
            fill = [lambda: tok_unit("qd", 0), lambda: tok_unit("qd", 1), kvd, lambda: tok_unit("gd", 0), lambda: tok_unit("gd", 1)]
            for i in range(4 + 2):
                if 1 <= i <= 4:
                    turn_probs(dh[2 * i - 1])
                if 2 <= i:
                    values(dh[2 * i - 3])
                if i < 4:
                    scores(dh[2 * i])
                    scores(dh[2 * i + 1])
                if i < len(fill):
                    fill[i]()
                if i == 3:
                    qk_transposes("qd", 4)
            qk_transposes("kvd", 5, 2)
            rm = norm(("m", 0), src=lambda t, c: mem[:, t, c * P:(c + 1) * P])
            pipeline(heads_of("swa"), [lambda n=n: mem_unit(0, n, rm) for n in range(4)],
                     {6: [lambda: yr.append(gated("ycd0", 3, 0, heads_of("diff")[-1]["output"]))]})
            gated("ycd1", 6, 2, heads_of("swa")[-1]["output"])
            project("ocd", X, yr[1])

            r = norm(("x", 0))
            tokens("dq", two("dq"), MLA_QL, 4, X, r, 0)
            tokens("dk", [names["dk", 0]], MLA_KVL, KC, X, r, 2, one_bank=True)
            u = names["dp", 0]
            take(u)
            begin("dp", 3)
            features("dp", banks[3][:, 0:S], u, KC, P, 0, X, r, True).then_inc(units_used, 1)
            end_with_unit("dp", u, (roped, 1))
            lat = lambda o: (lambda t, c: xn[:, t, o + c * P:o + (c + 1) * P])
            rq = norm("cq", 3, lat(0))
            rk = norm("ckv", 2, lat(MLA_QL))
            begin("ksum", 3)
            end("ksum", pe.matmul(banks[3][:, 0:S], halves, ksum_in, start=True, stop=True), (copied, copied_at["krope"]))

            def mla_head(h):
                u = names["uh", h]
                take(u)
                b = 2 * (h % 2)
                begin(("q", h), b)
                q3 = [v[:, 0:3, :] for v in H]
                features("", banks[b][:, 0:S], u, 3, 256, 0, q3, rq, True)
                ins = features("", banks[b][:, S:2 * S], u, 3, 256, P, q3, rq, True)
                end(("q", h), ins, [(copied, copied_at["q", h]), (roped, h + 2)])
                begin(("kv", h), b + 1)
                kv2 = [v[:, 3:5, :] for v in H]
                features("", banks[b + 1][:, 0:S], u, 2, 256, 768, kv2, rk, True)
                wh, wl = (flat(w, u)[:, 768:1280].rearrange("p (c n) -> p c n", n=256) for w in (w_hi, w_lo))
                for t in range(T):
                    for c in range(2):
                        a = [v[:, 3 + c, t * P:(t + 1) * P] for v in H]
                        ins = three(banks[b + 1][:, S + t * P:S + (t + 1) * P], a, (wh[:, c, P:2 * P], wl[:, c, P:2 * P]), u, c == 0, c == 1)
                ins.then_inc(units_used, 1)
                end_with_unit(("kv", h), u, (copied, copied_at["kv", h]))

            def deep(ks, before, name, ready):
                first = state["loT"]
                for i in range(len(ks) + 2):
                    if 1 <= i <= len(ks):
                        turn_probs(ks[i - 1])
                    if 2 <= i:
                        k = ks[i - 2]
                        pe.wait_ge(probsT_ready, k["turn"])
                        values_T(k, ("Y", k["g"]), k["pt"], k["v"], full=k["kind"] == "xa")
                    if i < len(ks):
                        ready(i)
                        scores(ks[i])
                    before(i + 1)
                return chunks_ready(first)

            mh = heads_of("mla")
            mla_head(0)

            def mla_inputs(h):
                pe.wait_ge(copied, copied_at["kv", h])
                pe.wait_ge(roped, h + 2)

            r = deep(mh, lambda h: mla_head(h) if h < HEADS else None, "mla", mla_inputs)
            project("omla", X, r)

            def cross(i):
                r = norm(("c", i))
                def xq(n):
                    u = names[("xq", i, n), 0]
                    take(u)
                    begin(("xq", i, n), n)
                    for h in range(2):
                        ins = features("", banks[n][:, h * S:(h + 1) * S], u, KC, S, h * P, X, r, True)
                    ins.then_inc(units_used, 1)
                    end_with_unit(("xq", i, n), u, (copied, copied_at["xq", i, n]))

                xq(0)
                ks = heads_of("xa", layer=i)
                r2 = deep(ks, lambda h: xq(1) if h == 1 else None, "xa",
                          lambda h: pe.wait_ge(copied, copied_at["xq", i, h // 2]))
                project(("xo", i), H, r2, 4)

            def mlp(i):
                r = norm(("p", i))
                pe.wait_ge(*r(KC - 1))
                u0 = names["mlp", i]
                hb = [hT_blocks(v) for v in H]
                base = {b: uses[b] for b in (4, 5, 6, 7)}
                relu0, hT0 = 2 * NBLK * i, 2 * NBLK * i

                def up(odd, u, du, blk, first):
                    A_, B_ = 4 + 2 * odd, 5 + 2 * odd
                    for n in range(2):
                        pe.wait_ge(lo_ready, u + n + 1 + du)
                        if n == 0 and not first:
                            pe.wait_ge(relu_ready, relu0 + 2 * (blk - 2) + 2)
                        for f in range(4):
                            o = banks[A_ + f // 2][:, (f % 2) * S:(f % 2 + 1) * S]
                            for c in range(4):
                                a = [flat(w, u + n)[:, c * BLK + f * P:c * BLK + (f + 1) * P] for w in (w_hi, w_lo)]
                                ins = three(o, a, [v[:, 4 * n + c, :] for v in X], u, n == 0 and f % 2 == 0 and c == 0, n == 1 and c == 3)
                            if n == 1 and f == 1:
                                ins.then_inc(written[A_], 1)
                        ins.then_inc(units_used, 1)

                def down(odd, u, du, blk, first, last):
                    pe.wait_ge(hT_ready, hT0 + 2 * blk + 2)
                    for n in range(2):
                        pe.wait_ge(lo_ready, u + n + 1 + du)
                        wh, wl = (flat(w, u + n).rearrange("p (c n) -> p c n", n=PANEL) for w in (w_hi, w_lo))
                        for t in range(T):
                            b = 2 * n + t
                            if first:
                                begin(("d", i, n, t), b)
                            for c in range(4):
                                a = [v[:, 2 * odd + c // 2, (c % 2) * S + t * P:(c % 2) * S + (t + 1) * P] for v in hb]
                                ins = three(banks[b][:, :], a, (wh[:, c, :], wl[:, c, :]), u, first and c == 0, last and c == 3)
                            if last:
                                free = (x_ready, xcount["mlp", i] + 2 * n + t + 1)
                                if t == 0:
                                    products["d", i, n, t] = b
                                    end(("d", i, n, t), ins, free)
                                else:
                                    products["d", i, n, t] = b
                                    end_with_unit(("d", i, n, t), u + n, free)
                        ins.then_inc(units_used, 1)

                for b in (4, 5, 6, 7):
                    begin(("upbank", b), b)
                up(0, u0, 0, 0, True)
                up(1, u0 + 2, 0, 1, True)
                down(0, u0 + 4, 0, 0, True, False)
                loops = (NBLK - 2) // 2
                with pe.Fori(0, loops) as it:
                    for s in range(2):
                        u = u0 + 6 + 4 * s
                        up(s, u, it * 8, it * 2 + 2 + s, False)
                        down(1 - s, u + 2, it * 8, it * 2 + 1 + s, False, False)
                down(1, u0 + 6 + 8 * loops, 0, NBLK - 1, False, True)
                for b in (4, 6):
                    uses[b] += NBLK // 2
                for n, b in enumerate((4, 5, 6, 7)):
                    freed[b] = [(relu_ready, relu0 + 2 * NBLK)]
                mlp_base[i] = base

            cross(0)
            mlp(0)

            r = norm(("x", 1))
            for n in range(4):
                tokens(("sv", n), [names[("sv", n), 0]], 256, KC, X, r, n, one_bank=True)

            def sqk(h):
                if h >= HEADS:
                    return
                u = names["sqk", h]
                take(u)
                b = h % 4
                begin(("sqk", h), b)
                for n in range(2):
                    ins = features("", banks[b][:, n * S:(n + 1) * S], u, KC, 256, n * P, X, r, True)
                ins.then_inc(units_used, 1)
                end_with_unit(("sqk", h), u, (copied, copied_at["sqk", h]))

            sqk(0)
            first = state["loT"]
            ks = heads_of("sb")
            for i in range(HEADS + 2):
                if 1 <= i <= HEADS:
                    turn_probs(ks[i - 1])
                if 2 <= i:
                    k = ks[i - 2]
                    pe.wait_ge(probsT_ready, k["turn"])
                    values_T(k, ("Y", k["g"]), k["pt"], k["v"])
                if i < HEADS:
                    g = ks[i]["g"]
                    b = 4 + g % 2
                    begin(("S", g), b)
                    pe.wait_ge(copied, copied_at["sqk", i])
                    for t, (a, z) in enumerate(ks[i]["spans"]):
                        ins = pe.matmul(banks[b][:, a:z], sb_qk(i)[:, t * P:(t + 1) * P], sb_qk(i)[:, S:S + z - a], start=True, stop=True)
                    end(("S", g), ins, (logits_ready, g + 1))
                sqk(i + 1)
            rm = norm(("m", 1), src=lambda t, c: mem[:, t, c * P:(c + 1) * P])
            project("osb", H, chunks_ready(first))
            for n in range(4):
                mem_unit(1, n, rm)
            cross(1)
            mlp(1)

        def condition(eng, name):
            b, s, v = products[name]
            eng.wait_ge(s, v)
            return banks[b]

        def read_of(name):
            return released[name][-1]

        stat, n_stat = {}, 0
        for name, n in ([("mem", 2)] + [(("n", i), 2) for i in range(2)] + [(("x", 0), 2), ("cq", 2), ("ckv", 2), (("c", 0), 2), (("p", 0), 2),
                        (("x", 1), 2), (("c", 1), 2), (("p", 1), 2), ("final", 2)]
                        + [(q, 16) for q in ("qa", "ka", "qb", "kb", "qc", "kc", "qd")] + [("kvd", 4)]
                        + [(("sub", h), 2) for h in range(4)]):
            stat[name] = n_stat
            n_stat += n
        assert n_stat <= NST

        panel_of = {"qa": 0, "ka": 1, "va": 2, "ga": 3, "qb": 4, "kb": 5, "vb": 6, "gb": 7,
                    "qc": 0, "kc": 1, "vc": 2, "gc": 3, "qd": 4, "kvd": 5, "gd": 6}
        turned = {"qa": (8, "moba_q", HD ** -0.5), "ka": (9, "moba_k", 1.0), "qb": (0, "fox_q", HD ** -0.5), "kb": (1, "fox_k", 1.0),
                  "qc": (8, "diff_q", HD ** -0.5), "kc": (9, "diff_k", 1.0), "qd": (10, "swa_q", HD ** -0.5), "kvd": (7, "swa_k", 1.0)}
        scaled = {}
        for n, key in enumerate(("moba_q", "fox_q", "diff_q", "swa_q", "sub")):
            scaled[key] = 110 + n
        scale_of = {"sub": 1.0 - LAM_INIT}
        qk_gain = lambda key: gains[:, scaled[key]:scaled[key] + 1] if key in scaled else gain(key)
        scratch = lambda n: xn[:, n % 2, :].rearrange("p (t n) -> p t n", t=T)
        SMALL_LOADS = 7
        lat = arena[:, 0:2, :].rearrange("p a n -> p (a n)")[:, 0:T * (MLA_QL + MLA_KVL)].rearrange("p (t n) -> p t n", t=T)
        held_index = {name: n for n, name in enumerate(("qa", "ka", "ga", "qb", "kb", "gb", "qc", "kc", "gc", "qd", "kvd", "gd"))}
        act_at = {}
        pos_i = arena[:, 8, 0:S].bitcast(I32)
        lam_in = arena[:, 10, 0:4 * HD]
        fox_z, fox_l, fox_c, fox_one = (arena[0:ROWS, 7, n * S:(n + 1) * S] for n in range(4))
        norm_gains = {("n", 0): ("norm", 0), ("n", 1): ("norm", 1), ("m", 0): ("mem", 0), ("m", 1): ("mem", 1), ("x", 0): ("mix", 0),
                      ("x", 1): ("mix", 1), ("c", 0): ("cross", 0), ("c", 1): ("cross", 1), ("p", 0): ("mlp", 0), ("p", 1): ("mlp", 1),
                      "cq": "gq", "ckv": "gkv"}

        def evac_gain(name, c):
            if name == "ycd0":
                return qk_gain("sub")
            return gain(norm_gains[name], c) if name in norm_gains else None

        @block.scalar
        def _(act):
            own = Order(act, act_chain)
            done = [0]
            chains = [0]

            def split_one(u, du=0, dload=0):
                act.wait_ge(w_in[u % RAW], loaded[u] + dload)
                if u >= RING:
                    act.wait_ge(units_used, u - RING + 1 + du)
                n = units[u][0]
                nc.scalar.copy(w_hi[:, u % RING, 0:n], raw[:, u % RAW, 0:n]).then_inc(hi_ready, 1)
                own.last = (hi_ready, u + 1 + du)

            def splits(n):
                while done[0] < min(n, len(units)):
                    split_one(done[0])
                    done[0] += 1

            def used(u):
                splits(u + 1 + RING)

            def mark(name, ins, s=None):
                v = own.sig(ins, s)
                act_at[name] = (s or act_chain, v)

            def stats(name, src, w, junk, ready):
                for t in range(T):
                    if ready is not None:
                        act.wait_ge(*ready(t))
                    c = stat[name] + t
                    ins = nc.scalar.activation(junk(t)[:, 0:w], src(t), ACT.Square, accum_out=ssq[:, c:c + 1])
                    mark(("ssq", name, t), ins, squares_ready)

            def rsqrt(c, n):
                chains[0] += 1
                act.wait_ge(var_ready, chains[0])
                own.sig(nc.scalar.activation(lnv[:, c:c + n], var[:, c:c + n], ACT.Ln))
                own.settle()
                own.sig(nc.scalar.activation(guess[:, c:c + n], lnv[:, c:c + n], ACT.Exp, scale=-0.5), guess_ready)

            def hi_T(name, chunks, dst, base=0):
                for c in range(chunks):
                    ps = condition(act, (name, c // 2))
                    g = evac_gain(name, c)
                    o = dst[:, base + c, :]
                    i_ = ps[:, (c % 2) * S:(c % 2 + 1) * S]
                    ins = nc.scalar.copy(o, i_) if g is None else nc.scalar.activation(o, i_, ACT.Copy, scale=g)
                    own.sig(ins, hiT_ready)

            def x_norm(name, x0):
                ready = (lambda t: (x_in, 16)) if x0 is None else (lambda t: (x_ready, x0 + 3 + t))
                stats(name, lambda t: x[:, t, :], D, lambda t: xn[:, t, :], ready)
                rsqrt(stat[name], T)
                if name != "final":
                    hi_T(name, KC, xT_hi)

            scratches = [0]
            held = []

            def scratch_panel(name, func):
                n = scratches[0]
                scratches[0] += 1
                if n >= 2:
                    for c in released[(held[n - 2], 1)]:
                        act.wait_ge(*c)
                held.append(name)
                for t in range(T):
                    ps = condition(act, (name, t))
                    ins = nc.scalar.activation(scratch(n)[:, t, :], ps[:, :], func, scale=-1.0 if func == ACT.Exp else 1.0)
                    mark(("scratch", name, t), ins, scratch_ready)

            def qk_panel(name):
                scratch_panel(name, ACT.Square)
                rsqrt(stat[name], 16)

            def qk_turned(name, pairs=2):
                for p in range(pairs):
                    ps = condition(act, (name, "T", p))
                    panel, key, _ = turned[name]
                    ins = nc.scalar.activation(arena[:, panel, p * PANEL:(p + 1) * PANEL], ps[:, :], ACT.Copy, scale=qk_gain(key))
                    own.sig(ins, qkT_ready)

            def plain(name):
                ps = condition(act, (name, 0))
                nc.scalar.copy(pan(panel_of[name], 0), ps[:, :]).then_inc(read_of((name, 0))[0], 1)
                own.last = read_of((name, 0))

            def exps(k):
                g = k["g"]
                act.wait_ge(logits_ready, g + 1)
                if g >= 2:
                    last = [q for q in heads if q["g"] in (g - 2, g - 1) and q["pb"] is not None and ("PT", q["g"]) in products and q["g"] % 2 == g % 2 or q["g"] == g - 1 and q["kind"] == "diff" and q["c"] == 1]
                    for q in last:
                        if ("PT", q["g"]) in products:
                            condition(act, ("PT", q["g"]))
                if k["kind"] == "swa":
                    for t in range(T):
                        own.sig(nc.scalar.activation(col(ESINK + 2 * k["h"] + t), nmax[:, 2 * g + t:2 * g + t + 1], ACT.Exp, bias=col(SINK + k["h"])))
                for t, (a, z) in enumerate(k["spans"]):
                    ins = nc.scalar.activation(k["pb"][:, a:z], k["nl"][:, a:z], ACT.Exp, bias=nmax[:, 2 * g + t:2 * g + t + 1],
                                               scale=-1.0, accum_out=esum[:, 2 * g + t:2 * g + t + 1])
                    own.sig(ins, probs_ready if t == T - 1 else None)

            def turned_probs(k):
                ps = condition(act, ("PT", k["g"]))
                before = [q for q in heads if q["g"] == k["g"] - 2]
                for q in before:
                    if ("Y", q["g"]) in products:
                        condition(act, ("Y", q["g"]))
                n = len(k["blocks"]) * P
                own.sig(nc.scalar.copy(k["pt"][:, 0:n], ps[:, 0:n]), probsT_ready)

            def y_hi(k, dst):
                ps = condition(act, ("Y", k["g"]))
                own.sig(nc.scalar.copy(dst[:, k["h"], :], ps[:, 0:S]), hiT_ready)

            stats("mem", lambda t: mem[:, t, :], D, lambda t: xn[:, t, :], lambda t: (mem_in, 16))
            rsqrt(stat["mem"], T)
            own.settle()
            x_norm(("n", 0), None)
            splits(RING)
            act.wait_ge(lam_sum, 1)
            own.sig(nc.scalar.activation(col(LAM, 2), col(LAM, 2), ACT.Exp), lam_exp)
            act.wait_ge(angle_ready, 1)
            own.sig(nc.scalar.activation(rope[:, :], arena[:, 8, 3 * S:4 * S], ACT.Sin), sine_ready)

            used(names["qa", 1]); qk_panel("qa")
            used(names["ka", 1]); qk_panel("ka")
            qk_turned("qa")
            used(names["va", 1]); plain("va")
            qk_turned("ka")
            used(names["ga", 1]); scratch_panel("ga", ACT.Exp)

            def pipeline(ks, after={}):
                for i in range(len(ks) + 2):
                    if 1 <= i <= len(ks):
                        turned_probs(ks[i - 1])
                    if i < len(ks):
                        exps(ks[i])
                    for f in after.get(i, []):
                        f()

            def fox_gates():
                act.wait_ge(fox_gate, 1)
                own.sig(nc.scalar.activation(fox_l, fox_z, ACT.Abs)); own.settle()
                own.sig(nc.scalar.activation(fox_l, fox_l, ACT.Exp, scale=-1.0)); own.settle()
                own.sig(nc.scalar.activation(fox_l, fox_l, ACT.Ln, bias=1.0), fox_log)

            U = names
            pipeline(heads_of("moba"), {
                0: [lambda: used(U["qb", 0])], 1: [lambda: used(U["qb", 1]), lambda: qk_panel("qb")],
                2: [lambda: used(U["kb", 0])], 3: [lambda: used(U["kb", 1]), lambda: qk_panel("kb")],
                4: [lambda: used(U["f", 0]), lambda: qk_turned("qb"), fox_gates], 5: [lambda: used(U["vb", 0])],
                6: [lambda: used(U["vb", 1]), lambda: plain("vb"), lambda: qk_turned("kb")]})
            pipeline(heads_of("fox"), {
                0: [lambda: used(U["gb", 0])], 1: [lambda: used(U["gb", 1]), lambda: scratch_panel("gb", ACT.Exp)],
                5: [lambda: hi_T("yab0", 4, xT_hi)]})
            hi_T("yab1", 4, xT_hi, 4)
            used(U[("oab", 1), 1])
            x_norm(("n", 1), 0)

            used(names["qc", 1]); qk_panel("qc")
            used(names["kc", 1]); qk_panel("kc")
            qk_turned("qc")
            used(names["vc", 1]); plain("vc")
            qk_turned("kc")
            used(names["gc", 1]); scratch_panel("gc", ACT.Exp)

            def kvd():
                n = scratches[0]
                scratches[0] += 1
                for c in released[(held[n - 2], 1)]:
                    act.wait_ge(*c)
                held.append("kvd")
                released["kvd", 1] = released["kvd"]
                ps = condition(act, "kvd")
                v = ps[:, :].rearrange("p (t n) -> p t n", t=T)
                own.sig(nc.scalar.copy(vd_tok, v[:, :, P:2 * P]))
                mark(("scratch", "kvd", 1), nc.scalar.activation(scratch(n)[:, :, 0:P], v[:, :, 0:P], ACT.Square), scratch_ready)
                rsqrt(stat["kvd"], 4)

            dh = heads_of("diff")
            extra = {0: [lambda: used(U["qd", 0])], 1: [lambda: used(U["qd", 1]), lambda: qk_panel("qd")],
                     2: [lambda: used(U["kvd", 0]), kvd], 3: [lambda: used(U["gd", 0]), lambda: qk_turned("qd")],
                     4: [lambda: used(U["gd", 1]), lambda: scratch_panel("gd", ACT.Exp)]}
            for i in range(4 + 2):
                if 1 <= i <= 4:
                    turned_probs(dh[2 * i - 1])
                if i < 4:
                    exps(dh[2 * i])
                    exps(dh[2 * i + 1])
                if i >= 2:
                    h = i - 2
                    ps = condition(act, ("Y", dh[2 * h + 1]["g"]))
                    for t in range(T):
                        c = stat["sub", h] + t
                        ins = nc.scalar.activation(arena[:, 11, t * P:(t + 1) * P], ps[:, t * P:(t + 1) * P], ACT.Square, accum_out=ssq[:, c:c + 1])
                        mark(("ssq", ("sub", h), t), ins, squares_ready)
                    rsqrt(stat["sub", h], T)
                for f in extra.get(i, []):
                    f()
            qk_turned("kvd", 1)
            hi_T(("m", 0), KC, xT_hi)

            def mem_unit(i, n):
                used(U[("xkv", i, n), 0])
                ps = condition(act, ("mem", i, n))
                if n < 2:
                    o = mem_k[:, 2 * n:2 * n + 2, :]
                else:
                    o = mem_v[:, :, (n - 2) * S:(n - 1) * S]
                nc.scalar.copy(o, ps[:, :].rearrange("p (a b) -> p a b", a=2)).then_inc(read_of(("mem", i, n))[0], 1)
                own.last = read_of(("mem", i, n))

            pipeline(heads_of("swa"), {**{n: [lambda n=n: mem_unit(0, n)] for n in range(4)}, 6: [lambda: hi_T("ycd0", 4, xT_hi)]})
            hi_T("ycd1", 4, xT_hi, 4)
            used(U[("ocd", 1), 1])

            x_norm(("x", 0), 4)
            used(U["dq", 1])
            for t in range(T):
                ps = condition(act, ("dq", t))
                nc.scalar.copy(lat[:, t, 0:MLA_QL], ps[:, 0:MLA_QL]).then_inc(read_of(("dq", t))[0], 1)
                own.last = read_of(("dq", t))
            used(U["dk", 0])
            ps = condition(act, "dk")
            nc.scalar.copy(lat[:, :, MLA_QL:], ps[:, :].rearrange("p (t n) -> p t n", t=T)).then_inc(read_of("dk")[0], 1)
            own.last = read_of("dk")
            own.settle()
            stats("cq", lambda t: lat[:, t, 0:MLA_QL], MLA_QL, lambda t: xn[:, t, :], None)
            stats("ckv", lambda t: lat[:, t, MLA_QL:], MLA_KVL, lambda t: xn[:, t, MLA_QL:], None)
            rsqrt(stat["cq"], 4)
            used(U["dp", 0])
            hi_T("cq", 3, hT_hi)
            hi_T("ckv", 2, hT_hi, 3)
            ps = condition(act, "ksum")
            own.sig(nc.scalar.copy(krope, ps[:, 0:S]), copied)

            def mla_inputs(h):
                used(U["uh", h])
                ps = condition(act, ("q", h))
                own.sig(nc.scalar.copy(mla_buf(h, 0), ps[:, 0:S]), copied)
                ps = condition(act, ("kv", h))
                own.sig(nc.scalar.copy(arena[:, MLA_PANELS[h % 3], 2 * S:4 * S], ps[:, :]), copied)

            def deep(ks, inputs, dst):
                for i in range(len(ks) + 2):
                    if 1 <= i <= len(ks):
                        turned_probs(ks[i - 1])
                    if i < len(ks):
                        exps(ks[i])
                    inputs(i + 1)
                    if i >= 2:
                        y_hi(ks[i - 2], dst)

            mla_inputs(0)
            deep(heads_of("mla"), lambda h: mla_inputs(h) if h < HEADS else None, xT_hi)
            used(U[("omla", 1), 1])

            def cross(i, x0):
                x_norm(("c", i), x0)

                def xq(n):
                    used(U[("xq", i, n), 0])
                    ps = condition(act, ("xq", i, n))
                    own.sig(nc.scalar.copy(pan(0, n), ps[:, :]), copied)
                xq(0)
                deep(heads_of("xa", layer=i), lambda h: xq(1) if h == 1 else None, hT_hi)
                used(U[("xo", i, 1), 0])

            hb = hT_blocks(hT_hi)

            def mlp(i, x0):
                x_norm(("p", i), x0)
                u0 = names["mlp", i]
                h0 = 2 * NBLK * i

                def step(blk, u, it=None):
                    odd = blk % 2
                    du, db, dl = (0, 0, 0) if it is None else (it * 8, it * 2, it * (8 // RAW * 16))
                    if it is None:
                        splits(u + 6)
                    else:
                        split_one(u + 4, du, dl)
                        split_one(u + 5, du, dl)
                    for p in range(2):
                        b = 4 + 2 * odd + p
                        if p == 0:
                            act.wait_ge(written[b], mlp_base[i][b] + blk // 2 + 1 + (0 if it is None else it))
                        else:
                            act.wait_ge(units_used, u + 2 + du)
                        nc.scalar.activation(pan(4, p), banks[b][:, :], ACT.Relu).then_inc(relu_ready, 1)
                    for p in range(2):
                        act.wait_ge(h_ready, h0 + 2 * blk + p + 1 + 2 * db)
                        nc.scalar.copy(hb[:, 2 * odd + p, :], pan(5, p)).then_inc(hhi_ready, 1)
                    if it is not None:
                        split_one(u + 6, du, dl)
                        split_one(u + 7, du, dl)

                used(u0 - 1)
                step(0, u0)
                step(1, u0 + 2)
                splits(u0 + 10)
                with act.Fori(0, (NBLK - 4) // 2) as it:
                    step(2, u0 + 6, it)
                    step(3, u0 + 10, it)
                done[0] = u0 + 6 + 8 * ((NBLK - 4) // 2) + RING
                for blk in (NBLK - 2, NBLK - 1):
                    u = u0 + 6 + 4 * (blk - 2)
                    step(blk, u)
                    splits(u + 8)
                used(u0 + 4 * NBLK - 1)

            cross(0, 8)
            mlp(0, 12)

            x_norm(("x", 1), 16)
            for n in range(4):
                used(U[("sv", n), 0])
                ps = condition(act, ("sv", n))
                nc.scalar.copy(sb_v[:, :, n * S:(n + 1) * S], ps[:, :].rearrange("p (t n) -> p t n", t=T)).then_inc(read_of(("sv", n))[0], 1)
                own.last = read_of(("sv", n))

            def sqk(h):
                used(U["sqk", h])
                ps = condition(act, ("sqk", h))
                own.sig(nc.scalar.copy(sb_qk(h), ps[:, :]), copied)

            ks = heads_of("sb")
            sqk(0)
            for i in range(HEADS + 2):
                if 1 <= i <= HEADS:
                    turned_probs(ks[i - 1])
                if i < HEADS:
                    g = ks[i]["g"]
                    act.wait_ge(logits_ready, g + 1)
                    own.sig(nc.scalar.activation(sbuf_of(1, i), sbuf_of(0, i), ACT.Abs)); own.settle()
                    own.sig(nc.scalar.activation(sbuf_of(1, i), sbuf_of(1, i), ACT.Exp, scale=-1.0)); own.settle()
                    own.sig(nc.scalar.activation(sbuf_of(1, i), sbuf_of(1, i), ACT.Ln, bias=1.0), sb_log)
                if i >= 2:
                    y_hi(ks[i - 2], hT_hi)
                if i < HEADS:
                    act.wait_ge(sb_w, i + 1)
                    if i >= 2:
                        condition(act, ("PT", g - 2))
                    own.sig(nc.scalar.activation(pb3[:, i % 2, :], sbuf_of(2, i), ACT.Exp), probs_ready)
                if i + 1 < HEADS:
                    sqk(i + 1)
            hi_T(("m", 1), KC, xT_hi)
            used(U[("osb", 1), 1])
            for n in range(4):
                mem_unit(1, n)
            cross(1, 20)
            mlp(1, 24)
            x_norm("final", 28)

        @block.vector
        def _(dve):
            own = Order(dve, dve_chain)
            V = nc.vector
            done, chains, lo_T = [0], [0], [0]

            def split_one(u, du=0):
                dve.wait_ge(hi_ready, u + 1 + du)
                if u >= RING:
                    dve.wait_ge(units_used, u - RING + 1 + du)
                n = units[u][0]
                V.tensor_tensor(w_lo[:, u % RING, 0:n], raw[:, u % RAW, 0:n], w_hi[:, u % RING, 0:n].bitcast(F32),
                                ALU.subtract).then_inc(lo_ready, 1)
                own.last = (lo_ready, u + 1 + du)

            def splits(n):
                while done[0] < min(n, len(units)):
                    split_one(done[0])
                    done[0] += 1

            def used(u):
                splits(u + 1 + RING)

            def link(ins, s=None):
                own.sig(ins, s)
                own.settle()

            def rsqrt(name, segs):
                c0 = stat[segs[0][0]]
                n = sum(s[1] for s in segs)
                for m, (seg, k, w) in enumerate(segs):
                    c = stat[seg]
                    ins = V.tensor_scalar(var[:, c:c + k], ssq[:, c:c + k], 1.0 / w, EPS, ALU.mult, ALU.add)
                    own.sig(ins, var_ready if m == len(segs) - 1 else None)
                chains[0] += 1
                a = slice(c0, c0 + n)
                dve.wait_ge(guess_ready, chains[0])
                link(V.tensor_tensor(tmp[:, a], guess[:, a], guess[:, a], ALU.mult))
                link(V.tensor_tensor(tmp[:, a], tmp[:, a], var[:, a], ALU.mult))
                link(V.tensor_scalar(tmp[:, a], tmp[:, a], -0.5, 1.5, ALU.mult, ALU.add))
                link(V.tensor_tensor(rstd[:, a], guess[:, a], tmp[:, a], ALU.mult))

            def lo(o, ps, hi, g):
                if g is None:
                    ins = V.tensor_tensor(o, ps, hi.bitcast(F32), ALU.subtract)
                else:
                    ins = V.scalar_tensor_tensor(out=o, in0=ps, scalar=g, in1=hi.bitcast(F32), op0=ALU.mult, op1=ALU.subtract)
                lo_T[0] += 1
                own.sig(ins, loT_ready)

            def lo_chunks(name, chunks, dst, base=0):
                for c in range(chunks):
                    ps = condition(dve, (name, c // 2))
                    bank_left = 1 if c % 2 or c == chunks - 1 else 2
                    dve.wait_ge(hiT_ready, lo_T[0] + bank_left)
                    lo(dst[1][:, base + c, :], ps[:, (c % 2) * S:(c % 2 + 1) * S], dst[0][:, base + c, :], evac_gain(name, c))

            X, H = (xT_hi, xT_lo), (hT_hi, hT_lo)

            def scaled_rows(name, src, dst):
                for t in range(T):
                    c = stat[name] + t
                    own.sig(V.tensor_scalar(dst(t), src(t), rstd[:, c:c + 1], None, ALU.mult), xn_ready)

            def x_norm(name):
                dve.wait_ge(*act_at["ssq", name, T - 1])
                rsqrt(name, [(name, T, D)])
                scaled_rows(name, lambda t: x[:, t, :], lambda t: xn[:, t, :])
                lo_chunks(name, KC, X)

            def residual(name):
                for n in range(2):
                    for t in range(T):
                        key = (("d", name[1], n, t)) if name[0] == "mlp" else (("o", name, n), t)
                        ps = condition(dve, key)
                        o = x[:, t, n * PANEL:(n + 1) * PANEL]
                        own.sig(V.tensor_tensor(o, ps[:, :], o, ALU.add), x_ready)

            tok_n = [0]

            def qk_panel(name):
                kvd = name == "kvd"
                nh = 2 if kvd else 8
                n = held_index[name]
                dve.wait_ge(*act_at["scratch", name, 1])
                c = stat[name]
                if kvd:
                    i_ = scratch(n)[:, :, 0:P].rearrange("p t (h d) -> p t h d", d=HD)
                    o_ = ssq[:, c:c + 4].rearrange("p (t h) -> p t h", t=T)
                else:
                    i_ = xn[:, n % 2, :].rearrange("p (h d) -> p h d", d=HD)
                    o_ = ssq[:, c:c + 16]
                link(V.tensor_reduce(o_, i_, AX_X, ALU.add))
                rsqrt(name, [(name, T * nh, HD)])
                for t in range(T):
                    r = rstd[:, c + t * nh:c + (t + 1) * nh]
                    if kvd:
                        ps = condition(dve, "kvd")[:, t * S:t * S + P].rearrange("p (h d) -> p h d", d=HD)
                        for u in range(2):
                            o = arena[:, 5, t * S:(t + 1) * S].rearrange("p (h u d) -> p h u d", h=2, u=2)[:, :, u, :]
                            ins = V.tensor_tensor(o, ps, r.unsqueeze(2).to_broadcast([P, 2, HD]), ALU.mult)
                            if t == T - 1 and u == 1:
                                own.sig(ins, tok_ready)
                            else:
                                own.sig(ins)
                        continue
                    ps = condition(dve, (name, t))[:, :].rearrange("p (h d) -> p h d", d=HD)
                    o = pan(panel_of[name], t).rearrange("p (h d) -> p h d", d=HD)
                    ins = V.tensor_tensor(o, ps, r.unsqueeze(2).to_broadcast([P, nh, HD]), ALU.mult)
                    if t == T - 1:
                        own.sig(ins, tok_ready)
                    else:
                        ins.then_inc(read_of((name, t))[0], 1)
                        own.last = read_of((name, t))
                        own.settle()

            def plain(name):
                ps = condition(dve, (name, 1))
                V.tensor_copy(pan(panel_of[name], 1), ps[:, :]).then_inc(read_of((name, 1))[0], 1)
                own.last = read_of((name, 1))

            def gate_panel(name):
                n = held_index[name]
                e = xn[:, n % 2, :]
                dve.wait_ge(*act_at["scratch", name, 1])
                link(V.tensor_scalar(e, e, 1.0, None, ALU.add))
                link(V.reciprocal(e, e))
                for t in range(T):
                    ps = condition(dve, (name, t))
                    V.tensor_tensor(pan(panel_of[name], t), ps[:, :], e[:, t * PANEL:(t + 1) * PANEL], ALU.mult).then_inc(read_of((name, t))[0], 1)
                    own.last = read_of((name, t))
                own.settle()

            tables_of = {}

            def logits(k):
                g = k["g"]
                ps = condition(dve, ("S", g))
                if k["table"] is not None:
                    dve.wait_ge(table_ready, k["table"] + 1)
                if g >= 2:
                    dve.wait_ge(probs_ready, g - 1)
                for q in heads[max(0, g - 2):g]:
                    if q["kind"] == "diff" and q["c"] == 1 and k["c"] % 2 == 1 if k["kind"] == "diff" else q["kind"] == "diff" and q["c"] == 1:
                        condition(dve, ("PT", q["g"]))
                for t, (a, z) in enumerate(k["spans"]):
                    tab, o, i_ = k["tab"](a, z), k["nl"][:, a:z], ps[:, a:z]
                    if k["kind"] == "xa":
                        o, i_ = (v.rearrange("p (a b) -> p a b", a=2) for v in (o, i_))
                    ins = V.tensor_tensor_reduce(o, i_, tab, -k["scale"], BIG * 1e8, ALU.add, ALU.min, nmax[:, 2 * g + t:2 * g + t + 1])
                    if k["kind"] == "swa":
                        own.sig(ins)
                    else:
                        own.sig(ins, logits_ready if t == T - 1 else None)
                if k["kind"] == "swa":
                    own.settle()
                    m = nmax[:, 2 * g:2 * g + 2]
                    own.sig(V.tensor_scalar(m, m, col(NSINK + k["h"]), None, ALU.min), logits_ready)

            def recip(k):
                g = k["g"]
                e = esum[:, 2 * g:2 * g + 2]
                dve.wait_ge(probs_ready, g + 1)
                if k["kind"] == "swa":
                    link(V.tensor_tensor(e, e, col(ESINK + 2 * k["h"], 2), ALU.add))
                link(V.reciprocal(rsum[:, 2 * g:2 * g + 2], e))

            def outputs(k):
                recip(k)
                g, vd = k["g"], k["vd"]
                ps = condition(dve, ("Y", g))
                for t in range(T):
                    o = k["gate"](t)
                    ins = V.scalar_tensor_tensor(out=o, in0=ps[:, t * vd:(t + 1) * vd], scalar=rsum[:, 2 * g + t:2 * g + t + 1],
                                                 in1=o, op0=ALU.mult, op1=ALU.mult)
                    own.sig(ins, y_ready if t == T - 1 else None)

            def normalise(k):
                recip(k)
                g = k["g"]
                for t, (a, z) in enumerate(k["spans"]):
                    o = k["pb"][:, a:z]
                    ins = V.tensor_scalar(o, o, rsum[:, 2 * g + t:2 * g + t + 1], None, ALU.mult)
                    own.sig(ins, norm_ready if t == T - 1 else None)

            def y_lo(k, dst):
                ps = condition(dve, ("Y", k["g"]))
                dve.wait_ge(hiT_ready, lo_T[0] + 1)
                lo(dst[1][:, k["h"], :], ps[:, 0:S], dst[0][:, k["h"], :], None)

            dve.wait_ge(*act_at["ssq", "mem", T - 1])
            rsqrt("mem", [("mem", T, D)])
            for t in range(T):
                own.sig(V.tensor_scalar(mem[:, t, :], mem[:, t, :], rstd[:, stat["mem"] + t:stat["mem"] + t + 1], None, ALU.mult))
            ps = condition(dve, "gains")
            V.tensor_copy(gains[:, 0:stage_rows], ps[:, 0:stage_rows]).then_inc(read_of("gains")[0], 1)
            own.last = read_of("gains")
            own.settle()
            for key, c in scaled.items():
                own.sig(V.tensor_scalar(gains[:, c:c + 1], gain(key), scale_of.get(key, HD ** -0.5), None, ALU.mult), gains_ready)
            ps = condition(dve, "freq")
            V.tensor_copy(col(INVF), ps[:, 0:1]).then_inc(read_of("freq")[0], 1)
            own.last = read_of("freq")
            own.settle()
            x_norm(("n", 0))
            splits(RING)
            dve.wait_ge(small_in, 16 * SMALL_LOADS)
            own.sig(V.tensor_scalar(col(NSINK, 8), col(SINK, 8), -1.0, None, ALU.mult))
            for n in range(2):
                a = lam_in[:, 2 * n * HD:(2 * n + 1) * HD]
                ins = V.tensor_tensor_reduce(arena[:, 10, 256 + n * HD:256 + (n + 1) * HD], a, lam_in[:, (2 * n + 1) * HD:(2 * n + 2) * HD],
                                             1.0, 0.0, ALU.mult, ALU.add, col(LAM + n))
                own.sig(ins, lam_sum if n else None)
            ang, turn, red = (arena[:, 8, n * S:(n + 1) * S] for n in (1, 2, 3))
            link(V.tensor_copy(red, pos_i))
            link(V.tensor_scalar(ang, red, col(INVF), None, ALU.mult))
            link(V.tensor_scalar(turn, ang, 1.0 / (2 * math.pi), col(TURN), ALU.mult, ALU.add))
            magic = 1.5 * 2.0 ** 23
            link(V.tensor_scalar(turn, turn, magic, None, ALU.add))
            link(V.tensor_scalar(turn, turn, -magic, None, ALU.add))
            hi_, mid_, low_ = two_pi_parts()
            link(V.scalar_tensor_tensor(out=red, in0=turn, scalar=-hi_, in1=ang, op0=ALU.mult, op1=ALU.add))
            link(V.scalar_tensor_tensor(out=red, in0=turn, scalar=-mid_, in1=red, op0=ALU.mult, op1=ALU.add))
            link(V.scalar_tensor_tensor(out=red, in0=turn, scalar=-low_, in1=red, op0=ALU.mult, op1=ALU.add))
            link(V.tensor_scalar(red, red, col(PHASE), None, ALU.add))
            own.sig(V.tensor_scalar(red, red, 3.1415925, -3.1415925, ALU.min, ALU.max), angle_ready)
            dve.wait_ge(sine_ready, 1)
            own.sig(V.tensor_scalar(rope[64:96, :], rope[64:96, :], -1.0, None, ALU.mult))
            dve.wait_ge(lam_exp, 1)
            link(V.tensor_scalar(col(NLAM), col(LAM + 1), -LAM_INIT, None, ALU.add))
            link(V.tensor_tensor(col(NLAM), col(NLAM), col(LAM), ALU.subtract))

            used(names["qa", 1]); qk_panel("qa")
            used(names["ka", 1]); qk_panel("ka")
            used(names["va", 1]); plain("va")
            used(names["ga", 1]); gate_panel("ga")

            def pipeline(ks, after={}):
                for i in range(len(ks) + 2):
                    if i < len(ks):
                        logits(ks[i])
                    if i >= 2:
                        outputs(ks[i - 2])
                    for f in after.get(i, []):
                        f()

            def fox_z_():
                ps = condition(dve, "f")
                dve.wait_ge(small_in, 16 * SMALL_LOADS)
                V.tensor_scalar(fox_z, ps[0:ROWS, 0:S], col(BF)[0:ROWS], None, ALU.add).then_inc(read_of("f")[0], 1)
                own.last = read_of("f")
                own.settle()
                own.sig(V.memset(fox_one, 1.0), fox_gate)

            def fox_rows():
                dve.wait_ge(fox_log, 1)
                link(V.scalar_tensor_tensor(out=fox_l, in0=fox_z, scalar=0.0, in1=fox_l, op0=ALU.min, op1=ALU.subtract))
                link(V.tensor_tensor_scan(fox_c, fox_one, fox_l, 0.0, ALU.mult, ALU.add))

            def fox_tables():
                dve.wait_ge(fox_const, 2)
                b = lambda lo_: fox_c[lo_:lo_ + HEADS].unsqueeze(1).to_broadcast([HEADS, HEADS, S])
                for r in (32, 96):
                    own.sig(V.tensor_copy(foxL[r:r + HEADS], b(r)))
                for r in (0, 64):
                    own.sig(V.tensor_copy(foxR[r:r + HEADS], b(r)), fox_ready)

            U = names
            pipeline(heads_of("moba"), {
                0: [lambda: used(U["qb", 0])], 1: [lambda: used(U["qb", 1]), lambda: qk_panel("qb")],
                2: [lambda: used(U["kb", 0])], 3: [lambda: used(U["kb", 1]), lambda: qk_panel("kb")],
                4: [lambda: used(U["f", 0]), fox_z_], 5: [lambda: used(U["vb", 0]), fox_rows],
                6: [lambda: used(U["vb", 1]), lambda: plain("vb")], 9: [fox_tables]})
            pipeline(heads_of("fox"), {
                0: [lambda: used(U["gb", 0])], 1: [lambda: used(U["gb", 1]), lambda: gate_panel("gb")],
                5: [lambda: lo_chunks("yab0", 4, X)]})
            lo_chunks("yab1", 4, X, 4)
            used(U[("oab", 1), 1])
            residual("oab")
            x_norm(("n", 1))

            used(names["qc", 1]); qk_panel("qc")
            used(names["kc", 1]); qk_panel("kc")
            used(names["vc", 1]); plain("vc")
            used(names["gc", 1]); gate_panel("gc")
            dh = heads_of("diff")

            def combine(a, b):
                recip(a)
                recip(b)
                r = rsum[:, 2 * b["g"]:2 * b["g"] + 2]
                link(V.tensor_scalar(r, r, col(NLAM), None, ALU.mult))
                for t, (s, z) in enumerate(a["spans"]):
                    o = a["pb"][:, s:z]
                    own.sig(V.tensor_scalar(o, o, rsum[:, 2 * a["g"] + t:2 * a["g"] + t + 1], None, ALU.mult))
                own.settle()
                for t, (s, z) in enumerate(a["spans"]):
                    ins = V.scalar_tensor_tensor(out=b["nl"][:, s:z], in0=b["pb"][:, s:z], scalar=rsum[:, 2 * b["g"] + t:2 * b["g"] + t + 1],
                                                 in1=a["pb"][:, s:z], op0=ALU.mult, op1=ALU.add)
                    own.sig(ins, norm_ready if t == T - 1 else None)

            extra = {0: [lambda: used(U["qd", 0])], 1: [lambda: used(U["qd", 1]), lambda: qk_panel("qd")],
                     2: [lambda: used(U["kvd", 0]), lambda: qk_panel("kvd")], 3: [lambda: used(U["gd", 0])],
                     4: [lambda: used(U["gd", 1]), lambda: gate_panel("gd")]}
            for i in range(4 + 2):
                if i < 4:
                    logits(dh[2 * i])
                    logits(dh[2 * i + 1])
                    combine(dh[2 * i], dh[2 * i + 1])
                if i >= 2:
                    h = i - 2
                    k = dh[2 * h + 1]
                    dve.wait_ge(*act_at["ssq", ("sub", h), T - 1])
                    rsqrt(("sub", h), [(("sub", h), T, P)])
                    ps = condition(dve, ("Y", k["g"]))
                    for t in range(T):
                        c = stat["sub", h] + t
                        o = k["gate"](t)
                        ins = V.scalar_tensor_tensor(out=o, in0=ps[:, t * P:(t + 1) * P], scalar=rstd[:, c:c + 1], in1=o, op0=ALU.mult, op1=ALU.mult)
                        own.sig(ins, y_ready if t == T - 1 else None)
                for f in extra.get(i, []):
                    f()
            own.settle()
            for t in range(T):
                own.sig(V.tensor_copy(tmp[:, stat["mem"] + t:stat["mem"] + t + 1], rstd[:, stat["mem"] + t:stat["mem"] + t + 1]), xn_ready)
            lo_chunks(("m", 0), KC, X)
            pipeline(heads_of("swa"), {**{n: [lambda n=n: used(U[("xkv", 0, n), 0])] for n in range(4)}, 6: [lambda: lo_chunks("ycd0", 4, X)]})
            lo_chunks("ycd1", 4, X, 4)
            used(U[("ocd", 1), 1])
            residual("ocd")

            x_norm(("x", 0))
            used(U["dq", 1])
            used(U["dk", 0])
            dve.wait_ge(*act_at["ssq", "ckv", T - 1])
            rsqrt("lat", [("cq", T, MLA_QL), ("ckv", T, MLA_KVL)])
            scaled_rows("cq", lambda t: lat[:, t, 0:MLA_QL], lambda t: xn[:, t, 0:MLA_QL])
            scaled_rows("ckv", lambda t: lat[:, t, MLA_QL:], lambda t: xn[:, t, MLA_QL:MLA_QL + MLA_KVL])
            used(U["dp", 0])
            ps = condition(dve, "dp")
            own.sig(V.tensor_tensor(ksum_in, ps[:, 0:S], rope[:, :], ALU.mult))
            own.settle()
            for n, (r0, c0) in enumerate([(0, 0), (64, 64), (0, 64), (64, 0)]):
                ins = V.tensor_copy(halves[r0:r0 + 64, c0:c0 + 64], ident[r0:r0 + 64, r0:r0 + 64])
                own.sig(ins, roped if n == 3 else None)
            lo_chunks("cq", 3, H)
            lo_chunks("ckv", 2, H, 3)

            def mla_inputs(h):
                used(U["uh", h])
                ps = condition(dve, ("q", h))
                dve.wait_ge(copied, copied_at["q", h])
                own.sig(V.tensor_tensor(mla_buf(h, 1), ps[:, S:2 * S], rope[:, :], ALU.mult), roped)

            def deep(ks, inputs, dst):
                for i in range(len(ks) + 2):
                    if i < len(ks):
                        logits(ks[i])
                        normalise(ks[i])
                    inputs(i + 1)
                    if i >= 2:
                        y_lo(ks[i - 2], dst)

            mla_inputs(0)
            deep(heads_of("mla"), lambda h: mla_inputs(h) if h < HEADS else None, X)
            used(U[("omla", 1), 1])
            residual("omla")

            def cross(i):
                x_norm(("c", i))
                used(U[("xq", i, 0), 0])
                deep(heads_of("xa", layer=i), lambda h: used(U[("xq", i, 1), 0]) if h == 1 else None, H)
                used(U[("xo", i, 1), 0])
                residual(("xo", i))

            hb = hT_blocks(hT_hi), hT_blocks(hT_lo)

            def mlp(i):
                x_norm(("p", i))
                u0, h0 = names["mlp", i], 2 * NBLK * i

                def step(blk, u, it=None):
                    odd = blk % 2
                    du, db = (0, 0) if it is None else (it * 8, it * 2)
                    if it is None:
                        splits(u + 6)
                    else:
                        split_one(u + 4, du)
                        split_one(u + 5, du)
                    for p in range(2):
                        dve.wait_ge(relu_ready, h0 + 2 * blk + p + 1 + 2 * db)
                        if p == 0 and (blk > 0 or i > 0):
                            dve.wait_ge(hT_ready, h0 + 2 * blk + 2 * db)
                        V.tensor_tensor(pan(5, p), pan(4, p), pan(4, p), ALU.mult).then_inc(h_ready, 1)
                    for p in range(2):
                        dve.wait_ge(hhi_ready, h0 + 2 * blk + p + 1 + 2 * db)
                        V.tensor_tensor(hb[1][:, 2 * odd + p, :], pan(5, p), hb[0][:, 2 * odd + p, :].bitcast(F32),
                                        ALU.subtract).then_inc(hT_ready, 1)
                    if it is not None:
                        split_one(u + 6, du)
                        split_one(u + 7, du)

                used(u0 - 1)
                step(0, u0)
                step(1, u0 + 2)
                splits(u0 + 10)
                with dve.Fori(0, (NBLK - 4) // 2) as it:
                    step(2, u0 + 6, it)
                    step(3, u0 + 10, it)
                done[0] = u0 + 6 + 8 * ((NBLK - 4) // 2) + RING
                for blk in (NBLK - 2, NBLK - 1):
                    u = u0 + 6 + 4 * (blk - 2)
                    step(blk, u)
                    splits(u + 8)
                used(u0 + 4 * NBLK - 1)
                residual(("mlp", i))

            cross(0)
            mlp(0)

            x_norm(("x", 1))
            for n in range(4):
                used(U[("sv", n), 0])
            for a, z in ((0, P), (2 * P, 3 * P)):
                own.sig(V.scalar_tensor_tensor(out=strict[:, a:z], in0=ident[:, :], scalar=-BIG, in1=causal[:, a:z], op0=ALU.mult, op1=ALU.add))
            link(V.tensor_copy(strict[:, P:2 * P], causal[:, P:2 * P]))
            used(U["sqk", 0])
            ks = heads_of("sb")
            for i in range(HEADS + 2):
                if i < HEADS:
                    g = ks[i]["g"]
                    z, l, w, r = (sbuf_of(n, i) for n in range(4))
                    ps = condition(dve, ("S", g))
                    own.settle()
                    link(V.scalar_tensor_tensor(out=z, in0=ps[:, 0:384], scalar=ks[i]["scale"], in1=strict, op0=ALU.mult, op1=ALU.add), logits_ready)
                if i >= 2:
                    y_lo(ks[i - 2], H)
                if i < HEADS:
                    dve.wait_ge(sb_log, i + 1)
                    if i >= 2:
                        dve.wait_ge(probs_ready, g - 1)
                    link(V.scalar_tensor_tensor(out=w, in0=z, scalar=0.0, in1=l, op0=ALU.max, op1=ALU.add))
                    for a, e in ks[i]["spans"]:
                        own.sig(V.tensor_tensor_scan(r[:, a:e][:, ::-1], w[:, a:e][:, ::-1], w[:, a:e][:, ::-1], 0.0, ALU.add, ALU.bypass))
                    own.settle()
                    own.sig(V.tensor_tensor(w, z, r, ALU.subtract), sb_w)
                if i + 1 < HEADS:
                    used(U["sqk", i + 1])
            dve.wait_ge(mem_in, 32)
            for t in range(T):
                c = stat["mem"] + t
                own.sig(V.tensor_scalar(mem[:, t, :], mem[:, t, :], rstd[:, c:c + 1], None, ALU.mult), xn_ready)
            lo_chunks(("m", 1), KC, X)
            used(U[("osb", 1), 1])
            residual("osb")
            for n in range(4):
                used(U[("xkv", 1, n), 0])
            cross(1)
            mlp(1)

            dve.wait_ge(*act_at["ssq", "final", T - 1])
            rsqrt("final", [("final", T, D)])
            dve.wait_ge(final_in, 16)
            for t in range(T):
                c = stat["final"] + t
                own.sig(V.scalar_tensor_tensor(out=xn[:, t, :], in0=x[:, t, :], scalar=rstd[:, c:c + 1], in1=final_gain,
                                               op0=ALU.mult, op1=ALU.mult), out_ready)

        @block.gpsimd
        def _(pool):
            G = nc.gpsimd
            own = Order(pool, pool_chain)

            def link(ins, s=None):
                own.sig(ins, s)
                own.settle()

            link(G.memset(ident[:, :], 0.0))
            link(G.affine_select(out=ident[:, :], in_=ident[:, :], compare_op=ALU.not_equal, fill=1.0, base=0, pattern=[[-1, P]], channel_multiplier=1))
            link(G.memset(col(BF), 0.0))
            link(G.memset(col(PHASE), 0.0))
            link(G.memset(col(TURN), 0.0))
            link(G.memset(small[0:64, PHASE:PHASE + 1], math.pi / 2))
            link(G.memset(small[0:64, TURN:TURN + 1], 0.25))
            for j in range(32):
                f = float(np.float32(10000.0 ** (-2.0 * j / ROPE)))
                own.sig(G.memset(arena[0:1, 9, j:j + 97:32], f))
            link(G.memset(arena[0:1, 9, P:P + 1], 1.0), setup_ready)
            rel_i = arena[:, 10, 512:896].bitcast(I32)
            own.sig(G.iota(rel_i[:, 0:P], [[-1, P]], base=0, channel_multiplier=1))
            link(G.iota(rel_i[:, P:384], [[-1, S]], base=P, channel_multiplier=1))
            link(G.tensor_copy(rel[:, :], rel_i))
            link(G.memset(causal[:, :], 0.0))
            for a, base in ((0, 0), (2 * P, 0)):
                for buf, fill in ((rel, BIG), (causal, -BIG)):
                    link(G.affine_select(out=buf[:, a:a + P], in_=buf[:, a:a + P], compare_op=ALU.is_ge, fill=fill, base=base, pattern=[[-1, P]], channel_multiplier=1))
            own.sig(G.memset(small[:, NLR:NLR + 1], 0.0), setup_ready)
            done = []
            for n, (g, factor, kind) in enumerate(tables):
                if n == 8:
                    pool.wait_ge(qkT_ready, 8)
                    for buf, first, fill in ((foxL, 0, -1.0), (foxR, 32, 1.0)):
                        link(G.memset(buf, 0.0))
                        for half in range(2):
                            link(G.affine_select(out=buf, in_=buf, compare_op=ALU.not_equal, fill=fill, base=-first - HD * half,
                                                 pattern=[[-1, HEADS], [0, S]], channel_multiplier=1), fox_const if buf is foxR else None)
                if kind == "window" and "window" not in done:
                    done.append("window")
                    own.settle()
                    m = rel[:, P:2 * P]
                    link(G.affine_select(out=m, in_=m, compare_op=ALU.is_gt, fill=BIG, base=0, pattern=[[1, P]], channel_multiplier=-1))
                if n >= 2:
                    pool.wait_ge(logits_ready, tables[n - 1][0])
                own.sig(G.tensor_scalar(alibi[:, n % 2, :], rel[:, :], factor, None, ALU.mult), table_ready)

        @block.sync
        def _(sp):
            def weight(u, src=None, du=0):
                if u >= RAW:
                    sp.wait_ge(lo_ready, u - RAW + 1 + du)
                width, pieces = units[u]
                for c0, chunks, cols, pitch, ap in pieces:
                    if src is not None:
                        ap = src
                    o = raw[:, u % RAW, :]
                    if cols == pitch:
                        o = o[:, c0:c0 + chunks * cols].rearrange("p (c n) -> p c n", c=chunks)
                    else:
                        first = c0 - c0 % pitch
                        o = o[:, first:first + chunks * pitch].rearrange("p (c n) -> p c n", c=chunks)[:, :, c0 % pitch:c0 % pitch + cols]
                    sp.dma_start(o, ap).then_inc(w_in[u % RAW], 16)

            tok = lambda ap: ap[0].rearrange("(t p) n -> p t n", p=P)
            sp.dma_start(mem[:, :, :], tok(A["mem_2"])).then_inc(mem_in, 16)
            sp.dma_start(x[:, :, :], tok(A["x"])).then_inc(x_in, 16)
            for r0, n, c0, w, ap in gain_loads:
                sp.dma_start(stage[r0:r0 + n, c0:c0 + w], ap).then_inc(stage_in, 16)
            for u in range(RAW):
                weight(u)
            sp.wait_ge(setup_ready, 1)
            loads = [(pos_i, A["positions_2"].to_broadcast([P, S])), (col(SINK, 8), A["swa_sinks"].to_broadcast([P, HEADS])),
                     (lam_in, A["diff_lambda"].rearrange("a b c -> a (b c)").to_broadcast([P, 4 * HD])),
                     *((small[r:r + HEADS, BF:BF + 1], A["b_forget"].rearrange("a h -> h a")) for r in GATE_ROWS)]
            assert len(loads) == SMALL_LOADS
            for o, i_ in loads:
                sp.dma_start(o, i_).then_inc(small_in, 16)

            def mlp(i):
                u0 = names["mlp", i]
                for u in range(u0, u0 + 6):
                    weight(u)
                win = A["mlp_w_in_2"][i].rearrange("(c p) n -> p c n", p=P)
                wout = A["mlp_w_out_2"][i].rearrange("(c p) n -> p c n", p=P)
                loops = (NBLK - 2) // 2
                with sp.Fori(0, loops) as it:
                    for s in range(2):
                        u = u0 + 6 + 4 * s
                        for n in range(2):
                            weight(u + n, win[:, 4 * n:4 * n + 4, bass.ds(it * (2 * BLK) + (2 + s) * BLK, BLK)], it * 8)
                        for n in range(2):
                            weight(u + 2 + n, wout[:, bass.ds(it * 8 + 4 * (1 + s), 4), n * PANEL:(n + 1) * PANEL], it * 8)
                for u in range(u0 + 6 + 8 * loops, u0 + 4 * NBLK):
                    weight(u)

            for u in range(RAW, names["mlp", 0]):
                weight(u)
            mlp(0)
            sp.wait_ge(x_ready, 16)
            sp.dma_start(mem[:, :, :], tok(A["mem_2"])).then_inc(mem_in, 16)
            for u in range(names["mlp", 0] + 4 * NBLK, names["mlp", 1]):
                weight(u)
            mlp(1)
            sp.dma_start(final_gain, A["norm_final_2"].rearrange("(a n) -> a n", a=1).to_broadcast([P, D])).then_inc(final_in, 16)
            o = tok(out)
            for t in range(T):
                sp.wait_ge(out_ready, t + 1)
                sp.dma_start(o[:, t, :], xn[:, t, :]).then_inc(out_done, 16)
            sp.wait_ge(out_done, 16 * T)


_NAMES = ["x", "norm_gain", "w_in_ab", "b_forget", "moba_q_gain", "moba_k_gain", "fox_q_gain", "fox_k_gain", "w_out_ab",
          "w_in_cd", "diff_q_gain", "diff_k_gain", "diff_lambda", "diff_subln_gain", "swa_q_gain", "swa_k_gain", "swa_sinks",
          "w_out_cd", "mem_2", "positions_2", "norm_mix_2", "norm_cross_2", "norm_mem_2", "norm_mlp_2", "norm_final_2",
          "mla_w_dkv_2", "mla_g_q_2", "mla_g_kv_2", "mla_w_uq_2", "mla_w_ukv_2", "mla_w_o_2", "sb_w_qkv_2", "sb_w_o_2",
          "xa_w_q_2", "xa_w_kv_2", "xa_w_o_2", "mlp_w_in_2", "mlp_w_out_2"]


def kernel(**inputs):
    import concourse.bacc as bacc
    from concourse.bass_utils import run_bass_kernel_spmd

    nc = bacc.Bacc("TRN2", target_bir_lowering=False, num_devices=1)
    arrays, aps = {}, {}
    for name in _NAMES:
        a = np.ascontiguousarray(inputs[name])
        arrays[f"in_{name}"] = a
        aps[name] = nc.dram_tensor(f"in_{name}", a.shape, mybir.dt.from_np(a.dtype), kind="ExternalInput").ap()
    out = nc.dram_tensor("out", (1, S, D), F32, kind="ExternalOutput").ap()
    build(nc, aps, out)
    result = run_bass_kernel_spmd(nc, [arrays], core_ids=[0])
    return result.results[0]["out"]
```

```python
import math
from contextlib import ExitStack

import numpy as np

import concourse.bass as bass
from concourse import mybir

ALU = mybir.AluOpType
ACT = mybir.ActivationFunctionType
AX_X = mybir.AxisListType.X
F32 = mybir.dt.float32
F32R = mybir.dt.float32r
I32 = mybir.dt.int32

P = 128
D = 1024
S = 256
T = S // P
KC = D // P
PANEL = 512
UNIT = 2048
RAW = 2
RING = 4
EPS = 1e-6
BIG = 1e30
HD = 64
HEADS = 8
DFF = 4 * D
BLK = 512
NBLK = DFF // BLK
MLA_QL, MLA_KVL, NOPE, ROPE, MLA_V = 384, 256, 128, 64, 128
LAM_INIT = 0.8 - 0.6 * math.exp(-0.3)
TWO_PI_HI = 6.28125
GATE_ROWS = (0, 32, 64, 96)
ROWS = 104
MLA_PANELS = (4, 5, 7, 8, 9)


def two_pi_parts():
    hi = TWO_PI_HI
    rest = 2 * math.pi - hi
    mid = math.floor(rest * 2 ** 20) / 2 ** 20
    return hi, mid, rest - mid


class Order:

    def __init__(self, eng, chain):
        self.eng, self.chain, self.counts, self.last = eng, chain, {}, None

    def sig(self, ins, sem=None, value=None, loop=0):
        sem = self.chain if sem is None else sem
        ins.then_inc(sem, 1)
        if value is None:
            self.counts[sem.name] = self.counts.get(sem.name, 0) + 1
            value = self.counts[sem.name] + loop
        self.last = (sem, value)
        return value

    def settle(self):
        self.eng.wait_ge(*self.last)


def weight_units(A):
    names, units = {}, []

    def rows(w):
        return w.rearrange("(c p) n -> p c n", p=P)

    def add(name, width, *pieces):
        names[name] = len(units)
        units.append((width, pieces))

    def panel(name, w, c0, cols, chunks, per):
        for n in range(chunks // per):
            add((name, n), per * cols, (0, per, cols, cols, rows(w)[:, n * per:(n + 1) * per, c0:c0 + cols]))

    ab, cd = A["w_in_ab"][0], A["w_in_cd"][0]
    def pair(w, a, b):
        for half in range(2):
            for name, c in (a, b):
                add((name, half), UNIT, (0, 4, PANEL, PANEL, rows(w)[:, 4 * half:4 * half + 4, c * PANEL:(c + 1) * PANEL]))

    pair(ab, ("qa", 0), ("ka", 1))
    for n, c in (("va", 2), ("ga", 3), ("qb", 4), ("kb", 5)):
        panel(n, ab, c * PANEL, PANEL, KC, 4)
    f0 = 8 * PANEL
    add(("f", 0), KC * P, (0, KC, 8, P, rows(ab)[:, :, f0:f0 + 8]),
        *((c, KC, 32, P, rows(ab)[:, :, f0 - 24:f0 + 8]) for c in (8, 40, 72)), (104, KC, 24, P, rows(ab)[:, :, 0:24]))
    for n, c in (("vb", 6), ("gb", 7)):
        panel(n, ab, c * PANEL, PANEL, KC, 4)

    def memory(i):
        for n in range(4):
            panel(("xkv", i, n), A["xa_w_kv_2"][i], n * 256, 256, KC, KC)

    def output(name, w):
        for half in range(2):
            for n in range(2):
                add((name, n, half), UNIT, (0, 4, PANEL, PANEL, rows(w)[:, 4 * half:4 * half + 4, n * PANEL:(n + 1) * PANEL]))

    output("oab", A["w_out_ab"][0])
    pair(cd, ("qc", 0), ("kc", 1))
    for n, c in (("vc", 2), ("gc", 3), ("qd", 4)):
        panel(n, cd, c * PANEL, PANEL, KC, 4)
    panel("kvd", cd, 5 * PANEL, 256, KC, KC)
    panel("gd", cd, 5 * PANEL + 256, PANEL, KC, 4)
    memory(0)
    output("ocd", A["w_out_cd"][0])
    dkv = A["mla_w_dkv_2"][0]
    dq = [(("dq", n), 4 * MLA_QL, (0, 4, MLA_QL, MLA_QL, rows(dkv)[:, 4 * n:4 * n + 4, 0:MLA_QL])) for n in range(2)]
    add(*dq[0])
    panel("dk", dkv, MLA_QL, MLA_KVL, KC, KC)
    pe0 = MLA_QL + MLA_KVL
    add(("dp", 0), KC * P, (0, KC, 64, P, rows(dkv)[:, :, pe0:pe0 + 64]),
        (64, KC, 32, P, rows(dkv)[:, :, pe0 + 32:pe0 + 64]), (96, KC, 32, P, rows(dkv)[:, :, pe0:pe0 + 32]))
    add(*dq[1])
    uq, ukv = rows(A["mla_w_uq_2"][0]), rows(A["mla_w_ukv_2"][0])
    for h in range(HEADS):
        c, k = h * (NOPE + ROPE), h * (NOPE + MLA_V)
        add(("uh", h), 3 * 256 + 2 * 256,
            (0, 3, 192, 256, uq[:, :, c:c + 192]), (192, 3, 32, 256, uq[:, :, c + 160:c + 192]),
            (224, 3, 32, 256, uq[:, :, c + 128:c + 160]), (768, 2, 256, 256, ukv[:, :, k:k + 256]))
    output("omla", A["mla_w_o_2"][0])

    def cross(i):
        for n in range(2):
            panel(("xq", i, n), A["xa_w_q_2"][i], n * 256, 256, KC, KC)
        for n in range(2):
            panel(("xo", i, n), A["xa_w_o_2"][i], n * PANEL, PANEL, 4, 4)

    def mlp(i):
        names[("mlp", i)] = len(units)
        win, wout = rows(A["mlp_w_in_2"][i]), rows(A["mlp_w_out_2"][i])

        def up(b, halves=(0, 1)):
            for n in halves:
                add(("up", i, b, n), UNIT, (0, 4, BLK, BLK, win[:, 4 * n:4 * n + 4, b * BLK:(b + 1) * BLK]))

        def down(b):
            for n in range(2):
                add(("down", i, b, n), UNIT, (0, 4, PANEL, PANEL, wout[:, 4 * b:4 * b + 4, n * PANEL:(n + 1) * PANEL]))
        for n in range(2):
            up(0, (n,))
            up(1, (n,))
        down(0)
        for b in range(2, NBLK):
            up(b)
            down(b - 1)
        down(NBLK - 1)

    cross(0)
    mlp(0)
    sb = A["sb_w_qkv_2"][0]
    for n in range(4):
        panel(("sv", n), sb, 2 * D + n * 256, 256, KC, KC)
    for h in range(HEADS):
        add(("sqk", h), UNIT, (0, KC, P, 256, rows(sb)[:, :, h * P:(h + 1) * P]),
            (P, KC, P, 256, rows(sb)[:, :, D + h * P:D + (h + 1) * P]))
    memory(1)
    output("osb", A["sb_w_o_2"][0])
    cross(1)
    mlp(1)
    return names, units


def build(nc, A, out):
    names, units = weight_units(A)
    loaded, per_slot = [], [0] * RAW
    for u, (_, pieces) in enumerate(units):
        per_slot[u % RAW] += 16 * len(pieces)
        loaded.append(per_slot[u % RAW])

    with ExitStack() as ctx:
        def sb(name, shape, dt=F32):
            return ctx.enter_context(nc.sbuf_tensor(name, shape, dt))

        def sem(name):
            return ctx.enter_context(nc.semaphore(name))

        raw = sb("raw", [P, RAW, UNIT])
        w_hi = sb("w_hi", [P, RING, UNIT], F32R)
        w_lo = sb("w_lo", [P, RING, UNIT], F32R)
        xT_hi = sb("xT_hi", [P, KC, S], F32R)
        xT_lo = sb("xT_lo", [P, KC, S], F32R)
        hT_hi = sb("hT_hi", [P, KC, S], F32R)
        hT_lo = sb("hT_lo", [P, KC, S], F32R)
        x = sb("x", [P, T, D])
        xn = sb("xn", [P, T, D])
        arena = sb("arena", [P, 12, 1024])
        ident = sb("ident", [P, P])
        rel = sb("rel", [P, 384])
        causal = sb("causal", [P, 384])
        alibi = sb("alibi", [P, 2, 384])
        gains = sb("gains", [P, P])
        rope = sb("rope", [P, S])
        row = sb("row", [P, S])
        nl3 = sb("nl3", [P, 2, 384])
        pb3 = sb("pb3", [P, 2, 384])
        pt3 = sb("pt3", [P, 2, 384])
        mem = sb("mem", [P, T, D])
        mem_k = mem[:, 0, :].rearrange("p (h s) -> p h s", h=4)
        mem_v = mem[:, 1, :].rearrange("p (t n) -> p t n", t=T)
        NST = 160
        ssq, var, lnv, guess, rstd = (sb(n, [P, NST]) for n in ("ssq", "var", "lnv", "guess", "rstd"))
        tmp = lnv
        NH = 2 * 64
        nmax, esum, rsum = (sb(n, [P, NH]) for n in ("nmax", "esum", "rsum"))
        small = sb("small", [P, 64])
        banks = [ctx.enter_context(nc.psum_tensor(f"bank{b}", [P, PANEL], F32)) for b in range(8)]

        SINK, NSINK, LAM, NLAM, BF, INVF, PHASE, TURN, ONE, ESINK = 0, 8, 16, 18, 20, 21, 22, 23, 24, 32
        col = lambda c, n=1: small[:, c:c + n]

        def pan(n, t=None):
            a = arena[:, n, :]
            return a if t is None else a[:, t * PANEL:(t + 1) * PANEL]

        w_in = [sem(f"w_in{n}") for n in range(RAW)]
        hi_ready, lo_ready = sem("hi_ready"), sem("lo_ready")
        units_used = sem("units_used")
        written = [sem(f"written{b}") for b in range(8)]
        read = [sem(f"read{b}") for b in range(8)]
        dve_chain, act_chain, pool_chain = sem("dve_chain"), sem("act_chain"), sem("pool_chain")
        first_gains_in = sem("first_gains_in")
        x_in, stage_in, small_in, mem_in, final_in = (sem(n) for n in ("x_in", "stage_in", "small_in", "mem_in", "final_in"))
        x_ready, squares_ready, var_ready, guess_ready = (sem(n) for n in ("x_ready", "squares_ready", "var_ready", "guess_ready"))
        scale_ready, row_ready, mem_ready = sem("scale_ready"), sem("row_ready"), sem("mem_ready")
        xq_ready, krope_ready, q_ready, v_ready = sem("xq_ready"), sem("krope_ready"), sem("q_ready"), sem("v_ready")
        lat_squares, lat_scales, v_scales = sem("lat_squares"), sem("lat_scales"), sem("v_scales")
        sqk_ready, hiT_ready, loT_ready = sem("sqk_ready"), sem("hiT_ready"), sem("loT_ready")
        scratch_ready = sem("scratch_ready")
        tok_ready = sem("tok_ready")
        qkT_ready = sem("qkT_ready")
        copied, roped = sem("copied"), sem("roped")
        logits_ready, probs_ready, probsT_ready, y_ready = (sem(n) for n in ("logits_ready", "probs_ready", "probsT_ready", "y_ready"))
        norm_ready = sem("norm_ready")
        table_ready = sem("table_ready")
        fox_const, fox_gate, fox_log, fox_ready = sem("fox_const"), sem("fox_gate"), sem("fox_log"), sem("fox_ready")
        sb_log, sb_w, angle_ready, sine_ready, lam_sum, lam_exp, gains_ready = (sem(n) for n in ("sb_log", "sb_w", "angle_ready", "sine_ready", "lam_sum", "lam_exp", "gains_ready"))
        relu_ready, h_ready, hhi_ready, hT_ready = (sem(n) for n in ("relu_ready", "h_ready", "hhi_ready", "hT_ready"))
        setup_ready, out_ready, out_done = sem("setup_ready"), sem("out_ready"), sem("out_done")

        stage = arena[:, 11, 0:P]
        gain_of, stage_rows = {}, 0
        gain_loads = []
        for key, ap in (("norm", A["norm_gain"]), ("mix", A["norm_mix_2"]), ("cross", A["norm_cross_2"]),
                        ("mem", A["norm_mem_2"]), ("mlp", A["norm_mlp_2"])):
            for i in range(2):
                gain_of[key, i] = stage_rows + i * KC
            gain_loads.append((stage_rows, 2 * KC, ap.rearrange("i (c p) -> (i c) p", p=P)))
            stage_rows += 2 * KC
        first_rows = 2 * KC
        for key, ap, n in (("gq", A["mla_g_q_2"], 3), ("gkv", A["mla_g_kv_2"], 2), ("sub", A["diff_subln_gain"], 1)):
            gain_of[key] = stage_rows
            gain_loads.append((stage_rows, n, ap[0].rearrange("(c p) -> c p", p=P)))
            stage_rows += n
        for key in ("moba_q", "moba_k", "fox_q", "fox_k", "diff_q", "diff_k", "swa_q", "swa_k"):
            gain_of[key] = stage_rows
            gain_loads.append((stage_rows, 1, A[key + "_gain"].unsqueeze(1).to_broadcast([1, 2, HD])))
            stage_rows += 1
        assert stage_rows <= P

        def gain(key, n=0):
            c = gain_of[key] + n
            return gains[:, c:c + 1]

        CAUSAL = [(0, 0, 0), (1, 0, P), (1, 1, 2 * P)]
        FULL = [(0, 0, 0), (1, 0, 256), (0, 1, 128), (1, 1, 384)]
        heads = []

        def head(kind, h, **k):
            k.update(kind=kind, h=h, g=len(heads), blocks=CAUSAL, spans=[(0, P), (P, 384)])
            n = len(heads) % 2
            k.update(nl=nl3[:, n], pb=pb3[:, n], pt=pt3[:, n])
            if kind == "xa":
                k.update(blocks=FULL, spans=[(0, 256), (256, 512)])
                k.update(nl=pan(1, n), pb=pan(2, n), pt=pan(3, n))
            heads.append(k)

        def chunked(panel, chunk, part, a, b):
            return arena[part * HD:(part + 1) * HD, panel, chunk * S + a:chunk * S + b]

        tables = []

        def slope(h):
            return 2.0 ** -(h + 1)

        for h in range(HEADS):
            tables.append((len(heads), -slope(h), "rel"))
            head("moba", h, scale=1.0, table=len(tables) - 1, v=lambda kt, h=h: arena[:, 2, kt * PANEL + h * HD:kt * PANEL + (h + 1) * HD], vd=HD,
                 parts=[lambda a, b, h=h: chunked(8, h // 2, h % 2, a, b)], keys=[lambda a, b, h=h: chunked(9, h // 2, h % 2, a, b)],
                 gate=lambda t, h=h: arena[:, 3, t * PANEL + h * HD:t * PANEL + (h + 1) * HD])
        foxL = arena[0:ROWS, 10:12, :].rearrange("p a n -> p (a n)").rearrange("p (h s) -> p h s", h=HEADS)
        foxR = arena[0:ROWS, 4:6, :].rearrange("p a n -> p (a n)").rearrange("p (h s) -> p h s", h=HEADS)
        for h in range(HEADS):
            head("fox", h, scale=1.0, table=None, v=lambda kt, h=h: arena[:, 6, kt * PANEL + h * HD:kt * PANEL + (h + 1) * HD], vd=HD,
                 parts=[lambda a, b, h=h: chunked(0, h // 2, h % 2, a, b), lambda a, b, h=h: foxL[HD * (h % 2):HD * (h % 2) + 40, h, a:b]],
                 keys=[lambda a, b, h=h: chunked(1, h // 2, h % 2, a, b), lambda a, b, h=h: foxR[HD * (h % 2):HD * (h % 2) + 40, h, a:b]],
                 gate=lambda t, h=h: arena[:, 7, t * PANEL + h * HD:t * PANEL + (h + 1) * HD])
        for h in range(4):
            tables.append((len(heads), -(2.0 ** -(2 * h + 2)), "rel"))
            for c in range(2):
                head("diff", h, c=c, scale=1.0, table=len(tables) - 1, v=lambda kt, h=h: arena[:, 2, kt * PANEL + h * P:kt * PANEL + (h + 1) * P], vd=P,
                     parts=[lambda a, b, h=h, c=c: chunked(8, h, c, a, b)], keys=[lambda a, b, h=h, c=c: chunked(9, h, c, a, b)],
                     gate=lambda t, h=h: arena[:, 3, t * PANEL + h * P:t * PANEL + (h + 1) * P])
        vd_tok = arena[:, 5, 512:768].rearrange("p (t n) -> p t n", t=T)
        for h in range(HEADS):
            tables.append((len(heads), -slope(h), "window"))
            head("swa", h, scale=1.0, table=len(tables) - 1, v=lambda kt, n=h // 4: vd_tok[:, kt, n * HD:(n + 1) * HD], vd=HD,
                 parts=[lambda a, b, h=h: chunked(10, h // 2, h % 2, a, b)], keys=[lambda a, b, h=h: chunked(7, h // 4, h % 2, a, b)],
                 gate=lambda t, h=h: arena[:, 6, t * PANEL + h * HD:t * PANEL + (h + 1) * HD])

        def mla_buf(h, n):
            return arena[:, MLA_PANELS[h % 5], n * S:(n + 1) * S]
        krope = arena[:, 6, 0:S]
        ksum_in = arena[:, 6, S:2 * S]
        halves = arena[:, 6, 2 * S:2 * S + P]
        for h in range(HEADS):
            head("mla", h, scale=(NOPE + ROPE) ** -0.5, table=None, vd=P,
                 parts=[lambda a, b, h=h: mla_buf(h, 0)[:, a:b], lambda a, b, h=h: mla_buf(h, 1)[:, a:b]],
                 keys=[lambda a, b, h=h: mla_buf(h, 2)[:, a:b], lambda a, b: krope[:, a:b]],
                 v=lambda kt, h=h: mla_buf(h, 3)[:, kt * P:(kt + 1) * P])
        for i in range(2):
            if i == 1:
                for h in range(HEADS):
                    head("sb", h, scale=P ** -0.5, table=None, vd=P, parts=[], keys=[],
                         v=lambda kt, h=h: sb_v[:, kt, h * P:(h + 1) * P])
            for h in range(4):
                head("xa", h, layer=i, scale=P ** -0.5, table=None, vd=P,
                     parts=[lambda a, b, h=h: arena[:, 0, h * S + a:h * S + b]], keys=[lambda a, b, h=h: mem_k[:, h, a:b]],
                     v=lambda kt, h=h: mem_v[:, kt, h * P:(h + 1) * P])

        turns = outputs = norms = 0
        for k in heads:
            first_map = k["kind"] == "diff" and k["c"] == 0
            turns += not first_map
            outputs += k["kind"] in ("moba", "fox", "swa") or k["kind"] == "diff" and k["c"] == 1
            norms += k["kind"] in ("mla", "xa") or k["kind"] == "diff" and k["c"] == 1
            k.update(turn=turns, output=outputs, norm=norms)
        qkT_needed = {"moba": 4, "fox": 8, "diff": 12, "swa": 15}
        xcount = {k: 4 * n for n, k in enumerate(("oab", "ocd", "omla", ("xo", 0), ("mlp", 0), "osb", ("xo", 1), ("mlp", 1)))}
        def heads_of(kind, **want):
            return [k for k in heads if k["kind"] == kind and all(k[a] == b for a, b in want.items())]

        for k in heads:
            k["tab"] = (lambda a, b: causal[:, a:b]) if k["table"] is None else (lambda a, b, n=k["table"]: alibi[:, n % 2, a:b])
            if k["kind"] == "xa":
                k["tab"] = lambda a, b: causal[:, P:2 * P].unsqueeze(1).to_broadcast([P, 2, P])

        sb_v = arena[:, 0:2, :]
        sb_qk = lambda h: (pan(2, 0), pan(2, 1), pan(8, 0))[h % 3]
        strict = arena[:, 3, 0:384]
        sbuf_of = lambda n, h: arena[:, 4 + n, (h % 2) * 384:(h % 2) * 384 + 384]

        final_gain = pan(6)
        hT_blocks = lambda a: a[:, :, :].rearrange("p c s -> p (c s)").rearrange("p (b n) -> p b n", b=4)

        products = {}
        mlp_base = {}
        released = {}

        def flat(buf, u):
            return buf[:, u % RING, :]

        stat, n_stat = {}, 0
        for name, n in ([("mem", 2)] + [(("n", i), 2) for i in range(2)] + [(("x", 0), 2), ("latv", 2), (("c", 0), 2), (("p", 0), 2),
                        (("x", 1), 2), (("c", 1), 2), (("p", 1), 2), ("final", 2)]
                        + [(q, 16) for q in ("qa", "ka", "qb", "kb", "qc", "kc", "qd")] + [("kvd", 4)]
                        + [(("sub", h), 2) for h in range(4)]):
            stat[name] = n_stat
            n_stat += n
        assert n_stat <= NST

        order_of_norms = [("n", 0), ("n", 1), ("x", 0), ("c", 0), ("p", 0), ("x", 1), ("c", 1), ("p", 1)]
        norm_no = {name: n + 1 for n, name in enumerate(order_of_norms)}
        row_no = {name: n + 1 for n, name in enumerate([("n", 0), ("x", 0), ("c", 0), ("x", 1), ("c", 1)])}
        x_before = {name: 4 * n for n, name in enumerate(order_of_norms)}
        rs = lambda name, t: rstd[:, stat[name] + t:stat[name] + t + 1]
        rs2 = lambda name, t: ssq[:, stat[name] + t:stat[name] + t + 1]
        neg_rs = lambda name, t: var[:, stat[name] + t:stat[name] + t + 1]
        row2 = row[:, :].unsqueeze(1).to_broadcast([P, 2, S])
        two_halves = lambda v: v.rearrange("p (a b) -> p a b", a=2)
        lat_sq = arena[:, 0:2, :].rearrange("p a n -> p (a n)")[:, 0:5 * S]
        lat_var, lat_tmp, lat_guess = pan(2, 0), pan(2, 1), pan(3, 0)
        q_scale, k_scale = pan(10, 0), pan(10, 1)[:, 0:S]
        row_sq, row_rope = pan(11, 0)[:, 0:S], pan(11, 0)[:, S:2 * S]

        block = ctx.enter_context(nc.Block())

        @block.tensor
        def _(pe):
            uses = [0] * 8
            freed = [None] * 8
            reads = [0] * 8
            state = {"loT": 0, "xn": 0, "tok": 0, "act": 0, "dve": 0, "qkT": 0}

            def begin(name, b):
                for one in freed[b] or ():
                    pe.wait_ge(*one)
                freed[b] = None
                products[name] = b

            def end(name, ins, free=None):
                b = products[name]
                uses[b] += 1
                ins.then_inc(written[b], 1)
                products[name] = (b, written[b], uses[b])
                release(name, b, free)

            def end_with_unit(name, u, free=None):
                b = products[name]
                products[name] = (b, units_used, u + 1)
                release(name, b, free)

            def release(name, b, free):
                if free is None:
                    reads[b] += 1
                    free = (read[b], reads[b])
                freed[b] = released[name] = free if isinstance(free, list) else [free]

            def take(u):
                pe.wait_ge(lo_ready, u + 1)

            def three(o, w, i, s, start, stop):
                (wh, wl), (ih, il) = w, i
                pe.matmul(o, wh, ih, start=start, stop=False, skip_group_check=True)
                pe.matmul(o, wh, il, start=False, stop=False, skip_group_check=True)
                return pe.matmul(o, wl, ih, start=False, stop=stop, skip_group_check=True)

            X = (xT_hi, xT_lo)
            H = (hT_hi, hT_lo)

            def tokens(name, us, cols, chunks, lhs, ready, b0, free=(None, None), one_bank=False, between=None):
                for n, u in enumerate(us):
                    take(u)
                    wh, wl = (flat(w, u)[:, 0:chunks * cols].rearrange("p (c n) -> p c n", n=cols) for w in (w_hi, w_lo))
                    for t in range(T):
                        b = b0 if one_bank else b0 + t
                        if n == 0:
                            if not one_bank or t == 0:
                                begin((name, t) if not one_bank else name, b)
                        o = banks[b][:, t * cols:(t + 1) * cols] if one_bank else banks[b][:, 0:cols]
                        for c in range(chunks):
                            k = n * chunks + c
                            if t == 0:
                                pe.wait_ge(*ready(k))
                            a = [v[:, k, t * P:(t + 1) * P] for v in lhs]
                            ins = three(o, a, (wh[:, c, 0:cols], wl[:, c, 0:cols]), u,
                                        n == 0 and c == 0, n == len(us) - 1 and c == chunks - 1)
                        if n == len(us) - 1 and t == 0 and not one_bank:
                            end((name, 0), ins, free[0])
                        if between and t == 0:
                            between()
                    ins.then_inc(units_used, 1)
                    if n == len(us) - 1:
                        end_with_unit(name if one_bank else (name, 1), u, free[-1])

            def features(name, o, u, chunks, width, c0, rhs, ready, last, free=None, m=P, start=True):
                wh, wl = (flat(w, u)[:, 0:].rearrange("p n -> p n") for w in (w_hi, w_lo))
                for c in range(chunks):
                    pe.wait_ge(*ready(c))
                    a = [v[:, c0 + c * width:c0 + c * width + m] for v in (wh, wl)]
                    ins = three(o, a, [v[:, c, :] for v in rhs], u, start and c == 0, c == chunks - 1)
                return ins

            def chunks_ready(base):
                return lambda c: (loT_ready, base + c + 1)

            def transposes(name, src, chunks, ready, b0=4):
                for t in range(T):
                    pe.wait_ge(*ready(t))
                    for c in range(chunks):
                        b = b0 + c // 2
                        if t == 0 and c % 2 == 0:
                            begin((name, c // 2), b)
                        o = banks[b][:, (c % 2) * S + t * P:(c % 2) * S + (t + 1) * P]
                        ins = pe.transpose(o, src(t, c), ident[:, :])
                        if t == T - 1 and (c % 2 == 1 or c == chunks - 1):
                            n = state["loT"] + c + 1
                            end((name, c // 2), ins, (loT_ready, n))
                base = state["loT"]
                state["loT"] += chunks
                return chunks_ready(base)

            norms = {}

            def turn_x(name, half, b0):
                if name == ("n", 0):
                    ready = lambda t: (x_in, 16 * T)
                else:
                    ready = lambda t: (x_ready, x_before[name] - 4 + 2 * half + t + 1)
                norms[name, half] = transposes((name, half), lambda t, c: x[:, t, (4 * half + c) * P:(4 * half + c + 1) * P], 4, ready, b0)

            def normed(name):
                return lambda k: norms[name, k // 4](k % 4)

            def turn_mem(i):
                return transposes(("m", i), lambda t, c: mem[:, t, c * P:(c + 1) * P], KC, lambda t: (mem_ready, T * i + t + 1), 0)

            def row_scales(name, b):
                begin(("R", name), b)
                pe.wait_ge(scale_ready, norm_no[name])
                for t in range(T):
                    ins = pe.matmul(banks[b][:, t * P:(t + 1) * P], rs(name, t).to_broadcast([P, P]), ident[:, :], start=True, stop=True)
                end(("R", name), ins, (row_ready, row_no[name]))

            def part(key, u, b, first, token_layout, r):
                if first:
                    take(u)
                    begin(key, b)
                wh, wl = (flat(w, u) for w in (w_hi, w_lo))
                for i in range(2):
                    for c in range(0 if first else 4, 4 if first else KC):
                        if i == 0:
                            pe.wait_ge(*r(c))
                        if token_layout:
                            a, m = [v[:, c, i * P:(i + 1) * P] for v in X], [v[:, c * S:(c + 1) * S] for v in (wh, wl)]
                        else:
                            a, m = [v[:, c * S + i * P:c * S + (i + 1) * P] for v in (wh, wl)], [v[:, c, :] for v in X]
                        ins = three(banks[b][:, i * S:(i + 1) * S], a, m, u, first and i == 0 and c == 0, c == KC - 1)
                if not first:
                    ins.then_inc(units_used, 1)
                return ins

            def qk_transposes(name, panel, chunks=4):
                state["tok"] += 1
                pe.wait_ge(tok_ready, state["tok"])
                for pair in range(chunks // 2):
                    b = 6 + pair
                    begin((name, "T", pair), b)
                    for c in range(2 * pair, 2 * pair + 2):
                        for t in range(T):
                            o = banks[b][:, (c % 2) * S + t * P:(c % 2) * S + (t + 1) * P]
                            w = PANEL * chunks // 4
                            ins = pe.transpose(o, arena[:, panel, t * w + c * P:t * w + (c + 1) * P], ident[:, :])
                    state["qkT"] += 1
                    end((name, "T", pair), ins, (qkT_ready, state["qkT"]))

            def scores(k):
                g = k["g"]
                b = 4 + g % 2
                begin(("S", g), b)
                if k["kind"] in ("moba", "fox", "diff", "swa"):
                    pe.wait_ge(qkT_ready, qkT_needed[k["kind"]])
                    if k["kind"] == "fox":
                        pe.wait_ge(fox_ready, 2)
                for t, (a, z) in enumerate(k["spans"]):
                    keys = z - a
                    for n, (q, kk) in enumerate(zip(k["parts"], k["keys"])):
                        ins = pe.matmul(banks[b][:, a:z], q(t * P, (t + 1) * P), kk(0, keys),
                                        start=n == 0, stop=n == len(k["parts"]) - 1)
                end(("S", g), ins, (logits_ready, g + 1))

            def turn_probs(k):
                g = k["g"]
                begin(("PT", g), 6)
                if k["kind"] in ("moba", "fox", "swa", "sb"):
                    pe.wait_ge(probs_ready, g + 1)
                else:
                    pe.wait_ge(norm_ready, k["norm"])
                src = k["nl"] if k["kind"] == "diff" else k["pb"]
                for n, (t, kt, a) in enumerate(k["blocks"]):
                    a = a if k["kind"] != "xa" else t * S + kt * P
                    ins = pe.transpose(banks[6][:, n * P:(n + 1) * P], src[:, a:a + P], ident[:, :])
                end(("PT", g), ins, (probsT_ready, k["turn"]))

            def values(k):
                g, vd = k["g"], k["vd"]
                begin(("Y", g), 7)
                pe.wait_ge(probsT_ready, k["turn"])
                for t in range(T):
                    mine = [(n, kt) for n, (tt, kt, _) in enumerate(k["blocks"]) if tt == t]
                    for m, (n, kt) in enumerate(mine):
                        ins = pe.matmul(banks[7][:, t * vd:(t + 1) * vd], k["pt"][:, n * P:(n + 1) * P], k["v"](kt),
                                        start=m == 0, stop=m == len(mine) - 1)
                end(("Y", g), ins, (y_ready, k["output"]))

            def values_T(k, name, pt, v, full=False):
                begin(name, 7)
                o = banks[7][:, 0:S]
                if full:
                    pe.matmul(o, v(0), pt[:, 0:S], start=True, stop=False)
                    ins = pe.matmul(o, v(1), pt[:, S:2 * S], start=False, stop=True)
                else:
                    pe.matmul(o[:, 0:P], v(0), pt[:, 0:P], start=True, stop=True)
                    pe.matmul(o[:, P:S], v(0), pt[:, P:S], start=True, stop=False)
                    ins = pe.matmul(o[:, P:S], v(1), pt[:, S:S + P], start=False, stop=True)
                state["loT"] += 1
                end(name, ins, (loT_ready, state["loT"]))

            tok_of = {"qa": 1, "ka": 2, "qb": 3, "kb": 4, "qc": 5, "kc": 6, "qd": 7, "kvd": 8}

            def second_free(name):
                return (tok_ready, tok_of[name]) if name in tok_of else None

            def project_half(name, half, n, lhs, ready, between=None):
                u = names[name, n, half]
                take(u)
                wh, wl = (flat(w, u).rearrange("p (c n) -> p c n", n=PANEL) for w in (w_hi, w_lo))
                for t in range(T):
                    key, b = (("o", name, n), t), 2 * n + t
                    if half == 0:
                        begin(key, b)
                    for c in range(4):
                        k = 4 * half + c
                        if t == 0:
                            pe.wait_ge(*ready(k))
                        ins = three(banks[b][:, :], [v[:, k, t * P:(t + 1) * P] for v in lhs], (wh[:, c, :], wl[:, c, :]), u,
                                    k == 0, k == KC - 1)
                    if half == 1 and t == 0:
                        end(key, ins, (x_ready, xcount[name] + 2 * n + 1))
                    if between and t == 0:
                        between()
                ins.then_inc(units_used, 1)
                if half == 1:
                    end_with_unit(key, u, (x_ready, xcount[name] + 2 * n + 2))

            def project_heads(name, lhs, ready, between):
                for n in range(2):
                    tokens(("o", name, n), [names[(name[0], name[1], n), 0]], PANEL, 4, lhs, ready, 2 * n,
                           free=((x_ready, xcount[name] + 2 * n + 1), (x_ready, xcount[name] + 2 * n + 2)), between=between if n else None)

            begin("gains0", 0)
            pe.wait_ge(first_gains_in, 16)
            pe.wait_ge(setup_ready, 1)
            end("gains0", pe.transpose(banks[0][:, 0:first_rows], stage[0:first_rows, :], ident[0:first_rows, 0:first_rows]))

            def constants():
                begin("gains", 6)
                pe.wait_ge(stage_in, 16 * (len(gain_loads) - 1))
                end("gains", pe.transpose(banks[6][:, 0:P], stage[:, :], ident[:, :]))
                begin("freq", 7)
                pe.wait_ge(setup_ready, 2)
                end("freq", pe.matmul(banks[7][:, 0:1], arena[0:1, 9, 0:P], arena[0:1, 9, P:P + 1], start=True, stop=True))

            where = {"qa": 0, "ka": 2, "va": 0, "ga": 2, "qc": 0, "kc": 2, "vc": 0, "qb": 0, "kb": 2, "vb": 0, "gb": 2, "gc": 2, "qd": 0, "gd": 0}

            def tok_unit(name, n):
                u = names[name, n]
                take(u)
                b0 = where[name]
                wh, wl = (flat(w, u).rearrange("p (c n) -> p c n", n=PANEL) for w in (w_hi, w_lo))
                for t in range(T):
                    if n == 0:
                        begin((name, t), b0 + t)
                    for c in range(4):
                        k = 4 * n + c
                        if t == 0:
                            pe.wait_ge(*r(k))
                        a = [v[:, k, t * P:(t + 1) * P] for v in X]
                        ins = three(banks[b0 + t][:, :], a, (wh[:, c, :], wl[:, c, :]), u, n == 0 and c == 0, n == 1 and c == 3)
                    if n == 1 and t == 0:
                        end((name, 0), ins)
                ins.then_inc(units_used, 1)
                if n == 1:
                    end_with_unit((name, 1), u, second_free(name))

            def front(name, q, k, v, g):
                tok_unit(q, 0)
                turn_x(name, 1, 4)
                tok_unit(k, 0)
                tok_unit(q, 1)
                tok_unit(k, 1)
                if q == "qa":
                    constants()
                tok_unit(v, 0)
                qk_transposes(q, 0)
                tok_unit(v, 1)
                qk_transposes(k, 1)
                tok_unit(g, 0)
                tok_unit(g, 1)

            turn_x(("n", 0), 0, 6)
            r = normed(("n", 0))
            front(("n", 0), "qa", "ka", "va", "ga")
            def fgate(ready):
                u = names["f", 0]
                take(u)
                begin("f", 0)
                ins = features("f", banks[0][:, 0:S], u, KC, P, 0, X, ready, True)
                ins.then_inc(units_used, 1)
                end_with_unit("f", u)

            def mem_unit(i, n, ready):
                u = names[("xkv", i, n), 0]
                b = n % 4
                if n < 2:
                    take(u)
                    begin(("mem", i, n), b)
                    for h in range(2):
                        ins = features("", banks[b][:, h * S:(h + 1) * S], u, KC, S, h * P, X, ready, True)
                    ins.then_inc(units_used, 1)
                    end_with_unit(("mem", i, n), u)
                else:
                    tokens(("mem", i, n), [u], 256, KC, X, ready, b, one_bank=True)

            def pipeline(ks, extra, v=values):
                for i in range(len(ks) + 3):
                    if 3 <= i:
                        v(ks[i - 3])
                    if i < len(ks):
                        scores(ks[i])
                    if 2 <= i <= len(ks) + 1:
                        turn_probs(ks[i - 2])
                    for e in extra.get(i, []):
                        e()

            def gated(name, panel, b0, need):
                return transposes(name, lambda t, c: arena[:, panel, t * PANEL + c * P:t * PANEL + (c + 1) * P],
                                  4, lambda t: (y_ready, need), b0)

            yr = {}

            def gate(key, *a):
                yr[key] = gated(key, *a)

            unit = lambda name, n: lambda: tok_unit(name, n)
            turn = lambda name, panel, chunks=4: lambda: qk_transposes(name, panel, chunks)
            half = lambda name, m, n, lhs, key: lambda: project_half(name, m, n, lhs, yr[key])
            pipeline(heads_of("moba") + heads_of("fox"), {
                0: [unit("qb", 0)], 1: [unit("qb", 1)], 2: [unit("kb", 0)], 3: [turn("qb", 4), unit("kb", 1)], 4: [lambda: row_scales(("n", 0), 1), lambda: fgate(r)],
                5: [turn("kb", 5), unit("vb", 0)], 6: [unit("vb", 1)], 8: [unit("gb", 0)], 10: [unit("gb", 1)],
                12: [lambda: gate("yab0", 3, 0, heads_of("moba")[-1]["output"])],
                14: [half("oab", 0, 0, X, "yab0")], 17: [half("oab", 0, 1, X, "yab0")]})
            gate("yab1", 7, 4, heads_of("fox")[-1]["output"])
            for n in range(2):
                project_half("oab", 1, n, X, lambda k: yr["yab1"](k - 4), (lambda: turn_x(("n", 1), 0, 6)) if n else None)

            r = normed(("n", 1))
            front(("n", 1), "qc", "kc", "vc", "gc")

            def kvd():
                tokens("kvd", [names["kvd", 0]], 256, KC, X, r, 2, one_bank=True, free=(second_free("kvd"),))

            dh = heads_of("diff")
            fill = [lambda: tok_unit("qd", 0), lambda: tok_unit("qd", 1), kvd, lambda: tok_unit("gd", 0), lambda: tok_unit("gd", 1)]
            for i in range(4 + 2):
                if 1 <= i <= 4:
                    turn_probs(dh[2 * i - 1])
                if 2 <= i:
                    values(dh[2 * i - 3])
                if i < 4:
                    scores(dh[2 * i])
                    scores(dh[2 * i + 1])
                if i < len(fill):
                    fill[i]()
                if i == 3:
                    qk_transposes("qd", 4)
            qk_transposes("kvd", 5, 2)
            def memory(i):
                yr["m", i] = turn_mem(i)

            pipeline(heads_of("swa"), {0: [lambda: memory(0)], **{n + 2: [lambda n=n: mem_unit(0, n, yr["m", 0])] for n in range(4)},
                                       7: [lambda: gate("ycd0", 3, 0, heads_of("diff")[-1]["output"])],
                                       8: [half("ocd", 0, 0, X, "ycd0")], 9: [half("ocd", 0, 1, X, "ycd0")]})
            gate("ycd1", 6, 4, heads_of("swa")[-1]["output"])
            for n in range(2):
                project_half("ocd", 1, n, X, lambda k: yr["ycd1"](k - 4), (lambda: turn_x(("x", 0), 0, 6)) if n else None)

            r = normed(("x", 0))

            def latents(half):
                u = names["dq", half]
                take(u)
                if half == 0:
                    begin(("lat", 0), 0)
                    begin(("lat", 1), 1)
                wh, wl = (flat(w, u) for w in (w_hi, w_lo))
                for f in range(3):
                    for c in range(4):
                        if f == 0:
                            pe.wait_ge(*r(4 * half + c))
                        a = [v[:, c * MLA_QL + f * P:c * MLA_QL + (f + 1) * P] for v in (wh, wl)]
                        ins = three(banks[f // 2][:, f % 2 * S:(f % 2 + 1) * S], a, [v[:, 4 * half + c, :] for v in X], u,
                                    half == 0 and c == 0 and f != 1, half == 1 and c == 3)
                    if half == 1 and f == 1:
                        end(("lat", 0), ins, (loT_ready, state["loT"] + 2))
                ins.then_inc(units_used, 1)
                if half == 1:
                    end_with_unit(("lat", 1), u, (loT_ready, state["loT"] + 3))

            def rope_keys(first):
                u = names["dp", 0]
                if first:
                    take(u)
                    begin("dp", 3)
                for c in range(0 if first else 4, 4 if first else KC):
                    pe.wait_ge(*r(c))
                    ins = three(banks[3][:, 0:S], [flat(w, u)[:, c * P:(c + 1) * P] for w in (w_hi, w_lo)], [v[:, c, :] for v in X], u,
                                c == 0, c == KC - 1)
                if not first:
                    ins.then_inc(units_used, 1)
                    end_with_unit("dp", u, (roped, 1))

            latents(0)
            turn_x(("x", 0), 1, 4)
            part(("lat", 2), names["dk", 0], 2, True, False, r)
            rope_keys(True)
            part(("lat", 2), names["dk", 0], 2, False, False, r)
            end_with_unit(("lat", 2), names["dk", 0], (loT_ready, state["loT"] + 2))
            rope_keys(False)
            base = state["loT"]
            state["loT"] += 2
            latents(1)
            state["loT"] += 3
            rk, rq = chunks_ready(base), chunks_ready(base + 2)
            row_scales(("x", 0), 5)
            begin("lat_ss", 4)
            pe.wait_ge(lat_squares, 3)
            ones = col(ONE).to_broadcast([P, P])
            for c in range(5):
                o = banks[4][:, 0:S] if c < 3 else banks[4][:, S:2 * S]
                ins = pe.matmul(o, ones, lat_sq[:, c * S:(c + 1) * S], start=c in (0, 3), stop=c in (2, 4))
            end("lat_ss", ins)

            def rope_key_sum():
                begin("ksum", 7)
                pe.wait_ge(roped, 2)
                end("ksum", pe.matmul(banks[7][:, 0:S], halves, ksum_in, start=True, stop=True), (krope_ready, 1))

            def value_scales():
                begin("v_scales", 6)
                pe.wait_ge(lat_scales, 1)
                for t in range(T):
                    ins = pe.matmul(banks[6][:, t:t + 1], k_scale[:, t * P:(t + 1) * P], ident[:, 0:1], start=True, stop=True)
                end("v_scales", ins, (v_scales, 1))

            def mla_head(h):
                u = names["uh", h]
                take(u)
                b = 2 * (h % 2)
                begin(("q", h), b)
                q3 = [v[:, 0:3, :] for v in H]
                features("", banks[b][:, 0:S], u, 3, 256, 0, q3, rq, True)
                ins = features("", banks[b][:, S:2 * S], u, 3, 256, P, q3, rq, True)
                end(("q", h), ins, (q_ready, 2 * h + 1))
                begin(("kv", h), b + 1)
                kv2 = [v[:, 3:5, :] for v in H]
                features("", banks[b + 1][:, 0:S], u, 2, 256, 768, kv2, rk, True)
                wh, wl = (flat(w, u)[:, 768:1280].rearrange("p (c n) -> p c n", n=256) for w in (w_hi, w_lo))
                for t in range(T):
                    for c in range(2):
                        a = [v[:, 3 + c, t * P:(t + 1) * P] for v in H]
                        ins = three(banks[b + 1][:, S + t * P:S + (t + 1) * P], a, (wh[:, c, P:2 * P], wl[:, c, P:2 * P]), u, c == 0, c == 1)
                ins.then_inc(units_used, 1)
                end_with_unit(("kv", h), u, [(v_ready, 2 * h + 2), (q_ready, 2 * h + 2)])

            def deep(ks, before, ready, extra={}):
                for i in range(len(ks) + 3):
                    if 3 <= i:
                        k = ks[i - 3]
                        pe.wait_ge(probsT_ready, k["turn"])
                        values_T(k, ("Y", k["g"]), k["pt"], k["v"], full=k["kind"] == "xa")
                    if i < len(ks):
                        ready(i)
                        scores(ks[i])
                    if 2 <= i <= len(ks) + 1:
                        turn_probs(ks[i - 2])
                    before(i + 2)
                    for e in extra.get(i, []):
                        e()

            mh = heads_of("mla")
            mla_head(0)
            rope_key_sum()
            mla_head(1)
            value_scales()

            def mla_inputs(h):
                pe.wait_ge(q_ready, 2 * h + 2)
                pe.wait_ge(v_ready, 2 * h + 2)
                pe.wait_ge(krope_ready, 1)

            r = chunks_ready(state["loT"])
            deep(mh, lambda h: mla_head(h) if h < HEADS else None, mla_inputs,
                 {8: [lambda: project_half("omla", 0, 0, X, r)], 9: [lambda: project_half("omla", 0, 1, X, r)]})
            for n in range(2):
                project_half("omla", 1, n, X, r, (lambda: turn_x(("c", 0), 0, 6)) if n else None)

            def cross(i):
                r = normed(("c", i))
                us = [names[("xq", i, n), 0] for n in range(2)]
                part(("xq", i, 0), us[0], 0, True, False, r)
                turn_x(("c", i), 1, 4)
                part(("xq", i, 1), us[1], 1, True, False, r)
                for n in range(2):
                    part(("xq", i, n), us[n], n, False, False, r)
                    end_with_unit(("xq", i, n), us[n], (xq_ready, 2 * i + n + 1))
                row_scales(("c", i), 3)
                ks = heads_of("xa", layer=i)
                r2 = chunks_ready(state["loT"])
                deep(ks, lambda h: None, lambda h: pe.wait_ge(xq_ready, 2 * i + h // 2 + 1))
                project_heads(("xo", i), H, r2, lambda: turn_x(("p", i), 0, 6))

            def mlp(i):
                r = normed(("p", i))
                u0 = names["mlp", i]
                hb = [hT_blocks(v) for v in H]
                base = {}
                relu0, hT0 = 2 * NBLK * i, 2 * NBLK * i

                def up_half(odd, n, u, du, blk):
                    A_ = 4 + 2 * odd
                    pe.wait_ge(lo_ready, u + 1 + du)
                    for f in range(4):
                        o = banks[A_ + f // 2][:, (f % 2) * S:(f % 2 + 1) * S]
                        for c in range(4):
                            a = [flat(w, u)[:, c * BLK + f * P:c * BLK + (f + 1) * P] for w in (w_hi, w_lo)]
                            ins = three(o, a, [v[:, 4 * n + c, :] for v in X], u, n == 0 and f % 2 == 0 and c == 0, n == 1 and c == 3)
                        if n == 1 and f == 1:
                            ins.then_inc(written[A_], 1)
                    ins.then_inc(units_used, 1)

                def up(odd, u, du, blk):
                    pe.wait_ge(relu_ready, relu0 + 2 * (blk - 2) + 2)
                    for n in range(2):
                        up_half(odd, n, u + n, du, blk)

                def down(odd, u, du, blk, first, last):
                    pe.wait_ge(hT_ready, hT0 + 2 * blk + 2)
                    for n in range(2):
                        pe.wait_ge(lo_ready, u + n + 1 + du)
                        wh, wl = (flat(w, u + n).rearrange("p (c n) -> p c n", n=PANEL) for w in (w_hi, w_lo))
                        for t in range(T):
                            b = 2 * n + t
                            if first:
                                begin(("d", i, n, t), b)
                            for c in range(4):
                                a = [v[:, 2 * odd + c // 2, (c % 2) * S + t * P:(c % 2) * S + (t + 1) * P] for v in hb]
                                ins = three(banks[b][:, :], a, (wh[:, c, :], wl[:, c, :]), u, first and c == 0, last and c == 3)
                            if last:
                                free = (x_ready, xcount["mlp", i] + 2 * n + t + 1)
                                if t == 0:
                                    products["d", i, n, t] = b
                                    end(("d", i, n, t), ins, free)
                                    if n == 1 and i == 0:
                                        turn_x(("x", 1), 0, 6)
                                else:
                                    products["d", i, n, t] = b
                                    end_with_unit(("d", i, n, t), u + n, free)
                        ins.then_inc(units_used, 1)

                for odd in range(2):
                    for b in (4 + 2 * odd, 5 + 2 * odd):
                        begin(("upbank", b), b)
                        base[b] = uses[b]
                    pe.wait_ge(*r(3))
                    up_half(odd, 0, u0 + odd, 0, odd)
                    if odd == 0:
                        turn_x(("p", i), 1, 0)
                pe.wait_ge(*r(KC - 1))
                for odd in range(2):
                    up_half(odd, 1, u0 + 2 + odd, 0, odd)
                down(0, u0 + 4, 0, 0, True, False)
                loops = (NBLK - 2) // 2
                with pe.Fori(0, loops) as it:
                    for s in range(2):
                        u = u0 + 6 + 4 * s
                        up(s, u, it * 8, it * 2 + 2 + s)
                        down(1 - s, u + 2, it * 8, it * 2 + 1 + s, False, False)
                for b in (4, 6):
                    uses[b] += NBLK // 2
                for b in (4, 5, 6, 7):
                    freed[b] = [(relu_ready, relu0 + 2 * NBLK)]
                down(1, u0 + 6 + 8 * loops, 0, NBLK - 1, False, True)
                mlp_base[i] = base

            cross(0)
            mlp(0)

            r = normed(("x", 1))
            sv = [names[("sv", n), 0] for n in range(4)]
            part(("sv", 0), sv[0], 0, True, True, r)
            turn_x(("x", 1), 1, 4)
            part(("sv", 1), sv[1], 1, True, True, r)
            for n in range(2):
                part(("sv", n), sv[n], n, False, True, r)
                end_with_unit(("sv", n), sv[n])
            for n in (2, 3):
                tokens(("sv", n), [sv[n]], 256, KC, X, r, n, one_bank=True)
            row_scales(("x", 1), 5)

            def sqk(h):
                if h >= HEADS:
                    return
                u = names["sqk", h]
                take(u)
                b = h % 4
                begin(("sqk", h), b)
                for n in range(2):
                    ins = features("", banks[b][:, n * S:(n + 1) * S], u, KC, 256, n * P, X, r, True)
                ins.then_inc(units_used, 1)
                end_with_unit(("sqk", h), u, (sqk_ready, h + 1))

            sqk(0)
            sqk(1)
            ks = heads_of("sb")
            y0 = state["loT"]
            MEM_STEP = 6
            ry = lambda c: (loT_ready, y0 + c + 1 + (KC if c > MEM_STEP - 3 else 0))
            for i in range(HEADS + 3):
                if 3 <= i:
                    k = ks[i - 3]
                    pe.wait_ge(probsT_ready, k["turn"])
                    values_T(k, ("Y", k["g"]), k["pt"], k["v"])
                if i < HEADS:
                    g = ks[i]["g"]
                    b = 4 + g % 2
                    begin(("S", g), b)
                    pe.wait_ge(sqk_ready, i + 1)
                    for t, (a, z) in enumerate(ks[i]["spans"]):
                        ins = pe.matmul(banks[b][:, a:z], sb_qk(i)[:, t * P:(t + 1) * P], sb_qk(i)[:, S:S + z - a], start=True, stop=True)
                    end(("S", g), ins, (logits_ready, g + 1))
                if 2 <= i <= HEADS + 1:
                    turn_probs(ks[i - 2])
                sqk(i + 2)
                if i == MEM_STEP:
                    rm = turn_mem(1)
                if i >= 7:
                    mem_unit(1, i - 7, rm)
            for half in range(2):
                for n in range(2):
                    project_half("osb", half, n, H, ry, (lambda: turn_x(("c", 1), 0, 6)) if half and n else None)
            cross(1)
            mlp(1)

        def condition(eng, name):
            b, s, v = products[name]
            eng.wait_ge(s, v)
            return banks[b]

        def read_of(name):
            return released[name][-1]

        panel_of = {"qa": 0, "ka": 1, "va": 2, "ga": 3, "qb": 4, "kb": 5, "vb": 6, "gb": 7,
                    "qc": 0, "kc": 1, "vc": 2, "gc": 3, "qd": 4, "kvd": 5, "gd": 6}
        turned = {"qa": (8, "moba_q", HD ** -0.5), "ka": (9, "moba_k", 1.0), "qb": (0, "fox_q", HD ** -0.5), "kb": (1, "fox_k", 1.0),
                  "qc": (8, "diff_q", HD ** -0.5), "kc": (9, "diff_k", 1.0), "qd": (10, "swa_q", HD ** -0.5), "kvd": (7, "swa_k", 1.0)}
        scaled = {}
        for n, key in enumerate(("moba_q", "fox_q", "diff_q", "swa_q", "sub")):
            scaled[key] = 110 + n
        scale_of = {"sub": 1.0 - LAM_INIT}
        qk_gain = lambda key: gains[:, scaled[key]:scaled[key] + 1] if key in scaled else gain(key)
        scratch = lambda n: xn[:, n % 2, :].rearrange("p (t n) -> p t n", t=T)
        SMALL_LOADS = 7
        lat = arena[:, 0:2, :].rearrange("p a n -> p (a n)")[:, 0:T * (MLA_QL + MLA_KVL)].rearrange("p (t n) -> p t n", t=T)
        held_index = {name: n for n, name in enumerate(("qa", "ka", "ga", "qb", "kb", "gb", "qc", "kc", "gc", "qd", "kvd", "gd"))}
        norm_of = {name: ("n", n) for n, ns in enumerate((("qa", "ka", "va", "ga", "qb", "kb", "vb", "gb"), ("qc", "kc", "vc", "gc", "qd", "kvd", "gd")))
                   for name in ns}
        act_at = {}
        pos_i = arena[:, 4, 0:S].bitcast(I32)
        lam_in = arena[:, 5, 0:4 * HD]
        fox_z, fox_l, fox_c, fox_one = (arena[0:ROWS, 7, n * S:(n + 1) * S] for n in range(4))
        norm_gains = {("n", 0): ("norm", 0), ("n", 1): ("norm", 1), ("m", 0): ("mem", 0), ("m", 1): ("mem", 1), ("x", 0): ("mix", 0),
                      ("x", 1): ("mix", 1), ("c", 0): ("cross", 0), ("c", 1): ("cross", 1), ("p", 0): ("mlp", 0), ("p", 1): ("mlp", 1),
                      }

        def evac_gain(name, c):
            if name == "ycd0":
                return qk_gain("sub")
            if name in [("lat", 0), ("lat", 1)]:
                return gain("gq", c + 2 * name[1])
            if name == ("lat", 2):
                return gain("gkv", c)
            if name[0] in x_before:
                return gain(norm_gains[name[0]], c + 4 * name[1])
            return gain(norm_gains[name], c) if name in norm_gains else None

        @block.scalar
        def _(act):
            own = Order(act, act_chain)
            done = [0]
            chains = [0]

            def split_one(u, du=0, dload=0):
                act.wait_ge(w_in[u % RAW], loaded[u] + dload)
                if u >= RING:
                    act.wait_ge(units_used, u - RING + 1 + du)
                n = units[u][0]
                nc.scalar.copy(w_hi[:, u % RING, 0:n], raw[:, u % RAW, 0:n]).then_inc(hi_ready, 1)
                own.last = (hi_ready, u + 1 + du)

            def splits(n):
                while done[0] < min(n, len(units)):
                    split_one(done[0])
                    done[0] += 1

            def used(u):
                splits(u + 1 + RING)

            def mark(name, ins, s=None):
                v = own.sig(ins, s)
                act_at[name] = (s or act_chain, v)

            def stats(name, src, w, junk, ready):
                for t in range(T):
                    if ready is not None:
                        act.wait_ge(*ready(t))
                    c = stat[name] + t
                    ins = nc.scalar.activation(junk(t)[:, 0:w], src(t), ACT.Square, accum_out=ssq[:, c:c + 1])
                    mark(("ssq", name, t), ins, squares_ready)

            def rsqrt(c, n):
                chains[0] += 1
                act.wait_ge(var_ready, chains[0])
                own.sig(nc.scalar.activation(lnv[:, c:c + n], var[:, c:c + n], ACT.Ln))
                own.settle()
                own.sig(nc.scalar.activation(guess[:, c:c + n], lnv[:, c:c + n], ACT.Exp, scale=-0.5), guess_ready)

            def hi_T(name, chunks, dst, base=0):
                for c in range(chunks):
                    ps = condition(act, (name, c // 2))
                    g = evac_gain(name, c)
                    o = dst[:, base + c, :]
                    i_ = ps[:, (c % 2) * S:(c % 2 + 1) * S]
                    ins = nc.scalar.copy(o, i_) if g is None else nc.scalar.activation(o, i_, ACT.Copy, scale=g)
                    own.sig(ins, hiT_ready)

            def x_turned(name, before=None, after=None):
                for half in range(2):
                    if half and before is not None:
                        used(before)
                    if half and after is not None:
                        used(after)
                    hi_T((name, half), 4, xT_hi, 4 * half)
                    for t in range(T):
                        act.wait_ge(*((x_in, 16 * T) if name == ("n", 0) else (x_ready, x_before[name] - 4 + 2 * half + t + 1)))
                        c = stat[name] + t
                        a = slice(half * PANEL, (half + 1) * PANEL)
                        ins = nc.scalar.activation(xn[:, t, a], x[:, t, a], ACT.Square, accum_out=(guess if half else ssq)[:, c:c + 1])
                        mark(("ssq", name, 2 * half + t), ins, squares_ready)
                rsqrt(stat[name], T)

            scratches = [0]
            held = []

            def scratch_panel(name, func):
                n = scratches[0]
                scratches[0] += 1
                if n >= 2:
                    for c in released[(held[n - 2], 1)]:
                        act.wait_ge(*c)
                held.append(name)
                for t in range(T):
                    ps = condition(act, (name, t))
                    if func == ACT.Exp:
                        act.wait_ge(scale_ready, norm_no[norm_of[name]])
                    ins = nc.scalar.activation(scratch(n)[:, t, :], ps[:, :], func,
                                               scale=neg_rs(norm_of[name], t) if func == ACT.Exp else HD ** -0.5)
                    mark(("scratch", name, t), ins, scratch_ready)

            def qk_squares(name):
                return lambda: scratch_panel(name, ACT.Square)

            def qk_rsqrt(name):
                return lambda: rsqrt(stat[name], 16)

            def qk_turned(name, pairs=2):
                for p in range(pairs):
                    ps = condition(act, (name, "T", p))
                    panel, key, _ = turned[name]
                    ins = nc.scalar.activation(arena[:, panel, p * PANEL:(p + 1) * PANEL], ps[:, :], ACT.Copy, scale=qk_gain(key))
                    own.sig(ins, qkT_ready)

            def plain(name):
                ps = condition(act, (name, 0))
                act.wait_ge(scale_ready, norm_no[norm_of[name]])
                nc.scalar.activation(pan(panel_of[name], 0), ps[:, :], ACT.Copy, scale=rs(norm_of[name], 0)).then_inc(read_of((name, 0))[0], 1)
                own.last = read_of((name, 0))

            def gate_scratch(name):
                n = scratches[0]
                scratch_panel(name, ACT.Exp)
                e = xn[:, n % 2, :]
                own.settle()
                own.sig(nc.scalar.activation(e, e, ACT.Ln, bias=1.0)); own.settle()
                mark(("gate", name), nc.scalar.activation(e, e, ACT.Exp, scale=-1.0), scratch_ready)

            def exps(k):
                g = k["g"]
                act.wait_ge(logits_ready, g + 1)
                if g >= 2:
                    last = [q for q in heads if q["g"] in (g - 2, g - 1) and q["pb"] is not None and ("PT", q["g"]) in products and q["g"] % 2 == g % 2 or q["g"] == g - 1 and q["kind"] == "diff" and q["c"] == 1]
                    for q in last:
                        if ("PT", q["g"]) in products:
                            condition(act, ("PT", q["g"]))
                if k["kind"] == "swa":
                    for t in range(T):
                        own.sig(nc.scalar.activation(col(ESINK + 2 * k["h"] + t), nmax[:, 2 * g + t:2 * g + t + 1], ACT.Exp, bias=col(SINK + k["h"])))
                for t, (a, z) in enumerate(k["spans"]):
                    ins = nc.scalar.activation(k["pb"][:, a:z], k["nl"][:, a:z], ACT.Exp, bias=nmax[:, 2 * g + t:2 * g + t + 1],
                                               scale=-1.0, accum_out=esum[:, 2 * g + t:2 * g + t + 1])
                    own.sig(ins, probs_ready if t == T - 1 else None)

            def turned_probs(k):
                ps = condition(act, ("PT", k["g"]))
                before = [q for q in heads if q["g"] == k["g"] - 2]
                for q in before:
                    if ("Y", q["g"]) in products:
                        condition(act, ("Y", q["g"]))
                n = len(k["blocks"]) * P
                own.sig(nc.scalar.copy(k["pt"][:, 0:n], ps[:, 0:n]), probsT_ready)

            def y_hi(k, dst):
                ps = condition(act, ("Y", k["g"]))
                own.sig(nc.scalar.copy(dst[:, k["h"], :], ps[:, 0:S]), hiT_ready)

            def front(q, k, v, g):
                used(names[k, 0])
                qk_squares(q)()
                used(names[q, 1])
                qk_rsqrt(q)()
                qk_squares(k)()
                used(names[k, 1])
                qk_rsqrt(k)()
                used(names[v, 0])
                act.wait_ge(gains_ready, len(scaled))
                qk_turned(q)
                plain(v)
                if q == "qa":
                    position_tables()
                used(names[v, 1])
                qk_turned(k)
                gate_scratch(g)
                used(names[g, 1])

            def row_copy(name):
                ps = condition(act, ("R", name))
                own.sig(nc.scalar.copy(row[:, :], ps[:, 0:S]), row_ready)

            nc.scalar.preload_act_table_set("natural_log_exp_and_others")
            act.wait_ge(*read_of("gains0"))
            splits(2)
            x_turned(("n", 0), None, names["qa", 0])

            def position_tables():
                act.wait_ge(lam_sum, 1)
                own.sig(nc.scalar.activation(col(LAM, 2), col(LAM, 2), ACT.Exp), lam_exp)
                act.wait_ge(angle_ready, 1)
                own.sig(nc.scalar.activation(rope[:, :], arena[:, 4, 3 * S:4 * S], ACT.Sin), sine_ready)
                nc.scalar.preload_act_table_set("natural_log_exp_and_others")

            def memory_rows():
                for c in released["gb", 1]:
                    act.wait_ge(*c)
                stats("mem", lambda t: mem[:, t, :], D, lambda t: xn[:, t, :], lambda t: (mem_in, 16))
                rsqrt(stat["mem"], T)

            front("qa", "ka", "va", "ga")

            def pipeline(ks, after={}):
                for i in range(len(ks) + 3):
                    if 2 <= i <= len(ks) + 1:
                        turned_probs(ks[i - 2])
                    if i < len(ks):
                        exps(ks[i])
                    for f in after.get(i, []):
                        f()

            def fox_gates():
                act.wait_ge(fox_gate, 1)
                own.sig(nc.scalar.activation(fox_l, fox_z, ACT.Abs)); own.settle()
                own.sig(nc.scalar.activation(fox_l, fox_l, ACT.Exp, scale=-1.0)); own.settle()
                own.sig(nc.scalar.activation(fox_l, fox_l, ACT.Ln, bias=1.0), fox_log)

            U = names
            split_to = lambda *key: lambda: used(U[key])
            pipeline(heads_of("moba") + heads_of("fox"), {
                0: [split_to("qb", 0)], 1: [qk_squares("qb"), split_to("qb", 1)],
                2: [qk_rsqrt("qb"), split_to("kb", 0)], 3: [lambda: qk_turned("qb"), qk_squares("kb"), split_to("kb", 1)],
                4: [lambda: row_copy(("n", 0)), qk_rsqrt("kb"), split_to("f", 0)], 5: [fox_gates, lambda: qk_turned("kb"), split_to("vb", 0)],
                6: [lambda: plain("vb"), split_to("vb", 1)], 8: [split_to("gb", 0)], 10: [lambda: gate_scratch("gb"), split_to("gb", 1)],
                11: [memory_rows], 12: [lambda: hi_T("yab0", 4, xT_hi)], 14: [split_to("oab", 0, 0)], 17: [split_to("oab", 1, 0)]})
            hi_T("yab1", 4, xT_hi, 4)
            used(U["oab", 0, 1])
            x_turned(("n", 1), U["oab", 1, 1], U["qc", 0])

            front("qc", "kc", "vc", "gc")

            def kvd():
                n = scratches[0]
                scratches[0] += 1
                for c in released[(held[n - 2], 1)]:
                    act.wait_ge(*c)
                held.append("kvd")
                released["kvd", 1] = released["kvd"]
                ps = condition(act, "kvd")
                v = ps[:, :].rearrange("p (t n) -> p t n", t=T)
                for t in range(T):
                    own.sig(nc.scalar.activation(vd_tok[:, t, :], v[:, t, P:2 * P], ACT.Copy, scale=rs(("n", 1), t)))
                mark(("scratch", "kvd", 1), nc.scalar.activation(scratch(n)[:, :, 0:P], v[:, :, 0:P], ACT.Square, scale=HD ** -0.5), scratch_ready)

            dh = heads_of("diff")
            extra = {0: [lambda: used(U["qd", 0])], 1: [qk_squares("qd"), split_to("qd", 1)],
                     2: [kvd, split_to("kvd", 0)], 3: [lambda: qk_turned("qd"), split_to("gd", 0)],
                     4: [lambda: gate_scratch("gd"), split_to("gd", 1)]}
            for i in range(4 + 2):
                if 1 <= i <= 4:
                    turned_probs(dh[2 * i - 1])
                if i < 4:
                    exps(dh[2 * i])
                    exps(dh[2 * i + 1])
                if i in (2, 3):
                    rsqrt(*((stat["qd"], 16), (stat["kvd"], 4))[i - 2])
                if i >= 2:
                    h = i - 2
                    ps = condition(act, ("Y", dh[2 * h + 1]["g"]))
                    for t in range(T):
                        c = stat["sub", h] + t
                        ins = nc.scalar.activation(arena[:, 11, t * P:(t + 1) * P], ps[:, t * P:(t + 1) * P], ACT.Square, accum_out=ssq[:, c:c + 1])
                        mark(("ssq", ("sub", h), t), ins, squares_ready)
                    rsqrt(stat["sub", h], T)
                for f in extra.get(i, []):
                    f()
            qk_turned("kvd", 1)
            def mem_unit(i, n):
                ps = condition(act, ("mem", i, n))
                if n < 2:
                    o = mem_k[:, 2 * n:2 * n + 2, :]
                else:
                    o = mem_v[:, :, (n - 2) * S:(n - 1) * S]
                nc.scalar.copy(o, ps[:, :].rearrange("p (a b) -> p a b", a=2)).then_inc(read_of(("mem", i, n))[0], 1)
                own.last = read_of(("mem", i, n))
                used(U[("xkv", i, n), 0])

            pipeline(heads_of("swa"), {0: [lambda: hi_T(("m", 0), KC, xT_hi)], **{n + 2: [lambda n=n: mem_unit(0, n)] for n in range(4)},
                                       7: [lambda: hi_T("ycd0", 4, xT_hi)], 8: [split_to("ocd", 0, 0)], 9: [split_to("ocd", 1, 0)]})
            hi_T("ycd1", 4, xT_hi, 4)
            used(U["ocd", 0, 1])

            x_turned(("x", 0), U["ocd", 1, 1], U["dq", 0])
            used(U["dk", 0])
            used(U["dp", 0])
            lat_bank = {0: (0, 2), 1: (2, 1), 2: (3, 2)}

            def latent(n):
                c, chunks = lat_bank[n]
                ps = condition(act, ("lat", n))
                own.sig(nc.scalar.activation(lat_sq[:, c * S:(c + chunks) * S], ps[:, 0:chunks * S], ACT.Square), lat_squares)
                for k in range(chunks):
                    own.sig(nc.scalar.activation(hT_hi[:, c + k, :], ps[:, k * S:(k + 1) * S], ACT.Copy, scale=evac_gain(("lat", n), k)), hiT_ready)

            latent(2)
            latent(0)
            latent(1)
            used(U["dq", 1])
            row_copy(("x", 0))
            chains[0] += 1
            act.wait_ge(var_ready, chains[0])
            own.sig(nc.scalar.activation(lat_tmp, lat_var, ACT.Ln))
            own.settle()
            own.sig(nc.scalar.activation(lat_guess, lat_tmp, ACT.Exp, scale=-0.5), guess_ready)
            ps = condition(act, "ksum")
            own.sig(nc.scalar.copy(krope, ps[:, 0:S]), krope_ready)

            def mla_inputs(h):
                ps = condition(act, ("kv", h))
                act.wait_ge(v_scales, 1)
                for t in range(T):
                    own.sig(nc.scalar.activation(mla_buf(h, 3)[:, t * P:(t + 1) * P], ps[:, S + t * P:S + (t + 1) * P], ACT.Copy,
                                                 scale=rs("latv", t)), v_ready)
                used(U["uh", h])

            def deep(ks, inputs, dst, after={}):
                for i in range(len(ks) + 3):
                    if i >= 3:
                        y_hi(ks[i - 3], dst)
                    if 2 <= i <= len(ks) + 1:
                        turned_probs(ks[i - 2])
                    if i < len(ks):
                        exps(ks[i])
                    inputs(i + 2)
                    for f in after.get(i, []):
                        f()

            mla_inputs(0)
            mla_inputs(1)
            deep(heads_of("mla"), lambda h: mla_inputs(h) if h < HEADS else None, xT_hi,
                 {8: [split_to("omla", 0, 0)], 9: [split_to("omla", 1, 0)]})
            used(U["omla", 0, 1])

            def cross(i, before):
                x_turned(("c", i), before)
                used(U[("xq", i, 1), 0])
                row_copy(("c", i))
                deep(heads_of("xa", layer=i), lambda h: None, hT_hi)
                used(U[("xo", i, 0), 0])

            hb = hT_blocks(hT_hi)

            def mlp(i):
                x_turned(("p", i), U[("xo", i, 1), 0], U["mlp", i])
                u0 = names["mlp", i]
                h0 = 2 * NBLK * i

                def step(blk, u, it=None):
                    odd = blk % 2
                    du, db, dl = (0, 0, 0) if it is None else (it * 8, it * 2, it * (8 // RAW * 16))
                    if it is None:
                        splits(u + 6)
                    else:
                        split_one(u + 4, du, dl)
                        split_one(u + 5, du, dl)
                    for p in range(2):
                        b = 4 + 2 * odd + p
                        if p == 0:
                            act.wait_ge(written[b], mlp_base[i][b] + blk // 2 + 1 + (0 if it is None else it))
                        else:
                            act.wait_ge(units_used, max(u + 2, u0 + 3) + du)
                        nc.scalar.activation(pan(4, p), banks[b][:, :], ACT.Relu).then_inc(relu_ready, 1)
                    for p in range(2):
                        act.wait_ge(h_ready, h0 + 2 * blk + p + 1 + 2 * db)
                        nc.scalar.copy(hb[:, 2 * odd + p, :], pan(5, p)).then_inc(hhi_ready, 1)
                    if it is not None:
                        split_one(u + 6, du, dl)
                        split_one(u + 7, du, dl)

                used(u0 - 1)
                step(0, u0)
                step(1, u0 + 2)
                splits(u0 + 10)
                with act.Fori(0, (NBLK - 4) // 2) as it:
                    step(2, u0 + 6, it)
                    step(3, u0 + 10, it)
                done[0] = u0 + 6 + 8 * ((NBLK - 4) // 2) + RING
                for blk in (NBLK - 2, NBLK - 1):
                    u = u0 + 6 + 4 * (blk - 2)
                    step(blk, u)
                    splits(u + 8)
                used(u0 + 4 * NBLK - 2)

            cross(0, U["omla", 1, 1])
            mlp(0)

            x_turned(("x", 1), U["mlp", 0] + 4 * NBLK - 1)
            act.wait_ge(scale_ready, norm_no["x", 1])
            for n in range(4):
                ps = condition(act, ("sv", n))
                for t in range(T):
                    ins = nc.scalar.activation(sb_v[:, t, n * S:(n + 1) * S], ps[:, t * S:(t + 1) * S], ACT.Copy, scale=rs(("x", 1), t))
                    if t == 0:
                        own.sig(ins)
                ins.then_inc(read_of(("sv", n))[0], 1)
                own.last = read_of(("sv", n))
                used(U[("sv", n), 0])
            row_copy(("x", 1))

            def sqk(h):
                used(U["sqk", h])

            ks = heads_of("sb")
            sqk(0)
            sqk(1)
            for i in range(HEADS + 3):
                if i >= 3:
                    y_hi(ks[i - 3], hT_hi)
                if 2 <= i <= HEADS + 1:
                    turned_probs(ks[i - 2])
                if 1 <= i <= HEADS:
                    g = ks[i - 1]["g"]
                    act.wait_ge(sb_w, i)
                    if i >= 3:
                        condition(act, ("PT", g - 2))
                    own.sig(nc.scalar.activation(pb3[:, (i - 1) % 2, :], sbuf_of(2, i - 1), ACT.Exp), probs_ready)
                if i < HEADS:
                    g = ks[i]["g"]
                    act.wait_ge(logits_ready, g + 1)
                    own.sig(nc.scalar.activation(sbuf_of(1, i), sbuf_of(0, i), ACT.Abs)); own.settle()
                    own.sig(nc.scalar.activation(sbuf_of(1, i), sbuf_of(1, i), ACT.Exp, scale=-1.0)); own.settle()
                    own.sig(nc.scalar.activation(sbuf_of(1, i), sbuf_of(1, i), ACT.Ln, bias=1.0), sb_log)
                if i + 2 < HEADS:
                    sqk(i + 2)
                if i == 6:
                    hi_T(("m", 1), KC, xT_hi)
                if i >= 7:
                    mem_unit(1, i - 7)
            used(U["osb", 0, 1])
            cross(1, U["osb", 1, 1])
            mlp(1)
            used(U["mlp", 1] + 4 * NBLK - 1)
            stats("final", lambda t: x[:, t, :], D, lambda t: xn[:, t, :], lambda t: (x_ready, 4 * len(order_of_norms) - 1 + t))
            rsqrt(stat["final"], T)

        @block.vector
        def _(dve):
            own = Order(dve, dve_chain)
            V = nc.vector
            done, chains, lo_T = [0], [0], [0]

            def split_one(u, du=0):
                dve.wait_ge(hi_ready, u + 1 + du)
                if u >= RING:
                    dve.wait_ge(units_used, u - RING + 1 + du)
                n = units[u][0]
                V.tensor_tensor(w_lo[:, u % RING, 0:n], raw[:, u % RAW, 0:n], w_hi[:, u % RING, 0:n].bitcast(F32),
                                ALU.subtract).then_inc(lo_ready, 1)
                own.last = (lo_ready, u + 1 + du)

            def splits(n):
                while done[0] < min(n, len(units)):
                    split_one(done[0])
                    done[0] += 1

            def used(u):
                splits(u + 1 + RING)

            def link(ins, s=None):
                own.sig(ins, s)
                own.settle()

            def mean_squares(segs):
                for m, (seg, k, w) in enumerate(segs):
                    c = stat[seg]
                    ins = V.tensor_scalar(var[:, c:c + k], ssq[:, c:c + k], 1.0 / w, EPS, ALU.mult, ALU.add)
                    own.sig(ins, var_ready if m == len(segs) - 1 else None)

            def newton(segs, of=None):
                c0 = stat[segs[0][0]]
                n = sum(s[1] for s in segs)
                chains[0] += 1
                a = slice(c0, c0 + n)
                dve.wait_ge(guess_ready, chains[0])
                link(V.tensor_tensor(tmp[:, a], guess[:, a], guess[:, a], ALU.mult))
                link(V.tensor_tensor(tmp[:, a], tmp[:, a], var[:, a], ALU.mult))
                link(V.tensor_scalar(tmp[:, a], tmp[:, a], -0.5, 1.5, ALU.mult, ALU.add))
                if of is None:
                    link(V.tensor_tensor(rstd[:, a], guess[:, a], tmp[:, a], ALU.mult))
                    return
                for t in range(T):
                    h = slice(c0 + t * n // T, c0 + (t + 1) * n // T)
                    own.sig(V.scalar_tensor_tensor(out=rstd[:, h], in0=guess[:, h], scalar=rs(of, t), in1=tmp[:, h], op0=ALU.mult, op1=ALU.mult))
                own.settle()

            def rsqrt(name, segs):
                mean_squares(segs)
                newton(segs)

            def lo(o, ps, hi, g):
                if g is None:
                    ins = V.tensor_tensor(o, ps, hi.bitcast(F32), ALU.subtract)
                else:
                    ins = V.scalar_tensor_tensor(out=o, in0=ps, scalar=g, in1=hi.bitcast(F32), op0=ALU.mult, op1=ALU.subtract)
                lo_T[0] += 1
                own.sig(ins, loT_ready)

            def lo_chunks(name, chunks, dst, base=0):
                for c in range(chunks):
                    ps = condition(dve, (name, c // 2))
                    bank_left = 1 if c % 2 or c == chunks - 1 else 2
                    dve.wait_ge(hiT_ready, lo_T[0] + bank_left)
                    lo(dst[1][:, base + c, :], ps[:, (c % 2) * S:(c % 2 + 1) * S], dst[0][:, base + c, :], evac_gain(name, c))

            X, H = (xT_hi, xT_lo), (hT_hi, hT_lo)

            def x_turned(name, last=None, before=None, after=None):
                for half in range(2):
                    if last is not None:
                        residual(last, half)
                    if before is not None:
                        used(before - 1 + half)
                    if half and after is not None:
                        used(after)
                    lo_chunks((name, half), 4, X, 4 * half)
                dve.wait_ge(*act_at["ssq", name, 3])
                c = slice(stat[name], stat[name] + T)
                link(V.tensor_tensor(ssq[:, c], ssq[:, c], guess[:, c], ALU.add))
                rsqrt(name, [(name, T, D)])
                link(V.tensor_tensor(ssq[:, c], rstd[:, c], rstd[:, c], ALU.mult))
                own.sig(V.tensor_scalar(var[:, c], rstd[:, c], -1.0, None, ALU.mult), scale_ready)
                own.settle()

            def residual(name, n):
                for t in range(T):
                    mlp_ = name[0] == "mlp"
                    key = ("d", name[1], n, t) if mlp_ else (("o", name, n), t)
                    ps = condition(dve, key)
                    o = x[:, t, n * PANEL:(n + 1) * PANEL]
                    if mlp_:
                        ins = V.scalar_tensor_tensor(out=o, in0=ps[:, :], scalar=rs2(("p", name[1]), t), in1=o, op0=ALU.mult, op1=ALU.add)
                    else:
                        ins = V.tensor_tensor(o, ps[:, :], o, ALU.add)
                    own.sig(ins, x_ready)

            def qk_sums(name):
                kvd = name == "kvd"
                nh = 2 if kvd else 8
                n = held_index[name]
                dve.wait_ge(*act_at["scratch", name, 1])
                c = stat[name]
                if kvd:
                    i_ = scratch(n)[:, :, 0:P].rearrange("p t (h d) -> p t h d", d=HD)
                    o_ = ssq[:, c:c + 4].rearrange("p (t h) -> p t h", t=T)
                else:
                    i_ = xn[:, n % 2, :].rearrange("p (h d) -> p h d", d=HD)
                    o_ = ssq[:, c:c + 16]
                link(V.tensor_reduce(o_, i_, AX_X, ALU.add))
                for t in range(T):
                    a = slice(c + t * nh, c + (t + 1) * nh)
                    own.sig(V.tensor_scalar(var[:, a], ssq[:, a], rs2(norm_of[name], t), EPS, ALU.mult, ALU.add), var_ready if t else None)

            def qk_scale(name):
                kvd = name == "kvd"
                nh = 2 if kvd else 8
                c = stat[name]
                newton([(name, T * nh, HD)], norm_of[name])
                for t in range(T):
                    r = rstd[:, c + t * nh:c + (t + 1) * nh]
                    if kvd:
                        ps = condition(dve, "kvd")[:, t * S:t * S + P].rearrange("p (h d) -> p h d", d=HD)
                        for u in range(2):
                            o = arena[:, 5, t * S:(t + 1) * S].rearrange("p (h u d) -> p h u d", h=2, u=2)[:, :, u, :]
                            ins = V.tensor_tensor(o, ps, r.unsqueeze(2).to_broadcast([P, 2, HD]), ALU.mult)
                            if t == T - 1 and u == 1:
                                own.sig(ins, tok_ready)
                            else:
                                own.sig(ins)
                        continue
                    ps = condition(dve, (name, t))[:, :].rearrange("p (h d) -> p h d", d=HD)
                    o = pan(panel_of[name], t).rearrange("p (h d) -> p h d", d=HD)
                    ins = V.tensor_tensor(o, ps, r.unsqueeze(2).to_broadcast([P, nh, HD]), ALU.mult)
                    if t == T - 1:
                        own.sig(ins, tok_ready)
                    else:
                        ins.then_inc(read_of((name, t))[0], 1)
                        own.last = read_of((name, t))
                        own.settle()

            def plain(name):
                ps = condition(dve, (name, 1))
                V.tensor_scalar(pan(panel_of[name], 1), ps[:, :], rs(norm_of[name], 1), None, ALU.mult).then_inc(read_of((name, 1))[0], 1)
                own.last = read_of((name, 1))

            def gate_panel(name):
                n = held_index[name]
                e = xn[:, n % 2, :]
                dve.wait_ge(*act_at["gate", name])
                for t in range(T):
                    ps = condition(dve, (name, t))
                    V.scalar_tensor_tensor(out=pan(panel_of[name], t), in0=ps[:, :], scalar=rs(norm_of[name], t),
                                           in1=e[:, t * PANEL:(t + 1) * PANEL], op0=ALU.mult, op1=ALU.mult).then_inc(read_of((name, t))[0], 1)
                    own.last = read_of((name, t))
                own.settle()

            tables_of = {}

            def logits(k):
                g = k["g"]
                ps = condition(dve, ("S", g))
                if k["table"] is not None:
                    dve.wait_ge(table_ready, k["table"] + 1)
                if g >= 2:
                    dve.wait_ge(probs_ready, g - 1)
                for q in heads[max(0, g - 2):g]:
                    if q["kind"] == "diff" and q["c"] == 1 and k["c"] % 2 == 1 if k["kind"] == "diff" else q["kind"] == "diff" and q["c"] == 1:
                        condition(dve, ("PT", q["g"]))
                for t, (a, z) in enumerate(k["spans"]):
                    tab, o, i_ = k["tab"](a, z), k["nl"][:, a:z], ps[:, a:z]
                    if k["kind"] == "xa":
                        o, i_ = (v.rearrange("p (a b) -> p a b", a=2) for v in (o, i_))
                    ins = V.tensor_tensor_reduce(o, i_, tab, -k["scale"], BIG * 1e8, ALU.add, ALU.min, nmax[:, 2 * g + t:2 * g + t + 1])
                    if k["kind"] == "swa":
                        own.sig(ins)
                    else:
                        own.sig(ins, logits_ready if t == T - 1 else None)
                if k["kind"] == "swa":
                    own.settle()
                    m = nmax[:, 2 * g:2 * g + 2]
                    own.sig(V.tensor_scalar(m, m, col(NSINK + k["h"]), None, ALU.min), logits_ready)

            def recip(k):
                g = k["g"]
                e = esum[:, 2 * g:2 * g + 2]
                dve.wait_ge(probs_ready, g + 1)
                if k["kind"] == "swa":
                    link(V.tensor_tensor(e, e, col(ESINK + 2 * k["h"], 2), ALU.add))
                link(V.reciprocal(rsum[:, 2 * g:2 * g + 2], e))

            def outputs(k):
                recip(k)
                g, vd = k["g"], k["vd"]
                ps = condition(dve, ("Y", g))
                for t in range(T):
                    o = k["gate"](t)
                    ins = V.scalar_tensor_tensor(out=o, in0=ps[:, t * vd:(t + 1) * vd], scalar=rsum[:, 2 * g + t:2 * g + t + 1],
                                                 in1=o, op0=ALU.mult, op1=ALU.mult)
                    own.sig(ins, y_ready if t == T - 1 else None)

            def normalise(k):
                recip(k)
                g = k["g"]
                for t, (a, z) in enumerate(k["spans"]):
                    o = k["pb"][:, a:z]
                    ins = V.tensor_scalar(o, o, rsum[:, 2 * g + t:2 * g + t + 1], None, ALU.mult)
                    own.sig(ins, norm_ready if t == T - 1 else None)

            def y_lo(k, dst):
                ps = condition(dve, ("Y", k["g"]))
                dve.wait_ge(hiT_ready, lo_T[0] + 1)
                lo(dst[1][:, k["h"], :], ps[:, 0:S], dst[0][:, k["h"], :], None)

            def position_tables():
                dve.wait_ge(small_in, 16 * SMALL_LOADS)
                own.sig(V.tensor_scalar(col(NSINK, 8), col(SINK, 8), -1.0, None, ALU.mult))
                for n in range(2):
                    a = lam_in[:, 2 * n * HD:(2 * n + 1) * HD]
                    ins = V.tensor_tensor_reduce(arena[:, 5, 256 + n * HD:256 + (n + 1) * HD], a, lam_in[:, (2 * n + 1) * HD:(2 * n + 2) * HD],
                                                 1.0, 0.0, ALU.mult, ALU.add, col(LAM + n))
                    own.sig(ins, lam_sum if n else None)
                ang, turn, red = (arena[:, 4, n * S:(n + 1) * S] for n in (1, 2, 3))
                link(V.tensor_copy(red, pos_i))
                link(V.tensor_scalar(ang, red, col(INVF), None, ALU.mult))
                link(V.tensor_scalar(turn, ang, 1.0 / (2 * math.pi), col(TURN), ALU.mult, ALU.add))
                magic = 1.5 * 2.0 ** 23
                link(V.tensor_scalar(turn, turn, magic, None, ALU.add))
                link(V.tensor_scalar(turn, turn, -magic, None, ALU.add))
                hi_, mid_, low_ = two_pi_parts()
                link(V.scalar_tensor_tensor(out=red, in0=turn, scalar=-hi_, in1=ang, op0=ALU.mult, op1=ALU.add))
                link(V.scalar_tensor_tensor(out=red, in0=turn, scalar=-mid_, in1=red, op0=ALU.mult, op1=ALU.add))
                link(V.scalar_tensor_tensor(out=red, in0=turn, scalar=-low_, in1=red, op0=ALU.mult, op1=ALU.add))
                link(V.tensor_scalar(red, red, col(PHASE), None, ALU.add))
                own.sig(V.tensor_scalar(red, red, 3.1415925, -3.1415925, ALU.min, ALU.max), angle_ready)
                dve.wait_ge(sine_ready, 1)
                own.sig(V.tensor_scalar(rope[64:96, :], rope[64:96, :], -1.0, None, ALU.mult))
                dve.wait_ge(lam_exp, 1)
                link(V.tensor_scalar(col(NLAM), col(LAM + 1), -LAM_INIT, None, ALU.add))
                link(V.tensor_tensor(col(NLAM), col(NLAM), col(LAM), ALU.subtract))

            def front(q, k, v, g):
                used(names[k, 0])
                if q == "qa":
                    constants()
                qk_sums(q)
                used(names[q, 1])
                qk_scale(q)
                qk_sums(k)
                used(names[k, 1])
                qk_scale(k)
                used(names[v, 0])
                if q == "qa":
                    position_tables()
                plain(v)
                used(names[v, 1])
                gate_panel(g)
                used(names[g, 1])

            ps = condition(dve, "gains0")
            V.tensor_copy(gains[:, 0:first_rows], ps[:, 0:first_rows]).then_inc(read_of("gains0")[0], 1)
            own.last = read_of("gains0")
            own.settle()

            def constants():
                ps = condition(dve, "gains")
                V.tensor_copy(gains[:, first_rows:stage_rows], ps[:, first_rows:stage_rows]).then_inc(read_of("gains")[0], 1)
                own.last = read_of("gains")
                own.settle()
                for key, c in scaled.items():
                    own.sig(V.tensor_scalar(gains[:, c:c + 1], gain(key), scale_of.get(key, HD ** -0.5), None, ALU.mult), gains_ready)
                ps = condition(dve, "freq")
                V.tensor_copy(col(INVF), ps[:, 0:1]).then_inc(read_of("freq")[0], 1)
                own.last = read_of("freq")
                own.settle()

            def memory_rows():
                dve.wait_ge(*act_at["ssq", "mem", T - 1])
                rsqrt("mem", [("mem", T, D)])
                for t in range(T):
                    own.sig(V.tensor_scalar(mem[:, t, :], mem[:, t, :], rs("mem", t), None, ALU.mult), mem_ready)

            splits(2)
            x_turned(("n", 0), None, None, names["qa", 0])
            front("qa", "ka", "va", "ga")

            def pipeline(ks, after={}):
                for i in range(len(ks) + 3):
                    if i >= 3:
                        outputs(ks[i - 3])
                    if i < len(ks):
                        logits(ks[i])
                    for f in after.get(i, []):
                        f()

            def fox_z_():
                ps = condition(dve, "f")
                dve.wait_ge(small_in, 16 * SMALL_LOADS)
                dve.wait_ge(row_ready, row_no["n", 0])
                V.tensor_tensor(fox_z, ps[0:ROWS, 0:S], row[0:ROWS, :], ALU.mult).then_inc(read_of("f")[0], 1)
                own.last = read_of("f")
                own.settle()
                link(V.tensor_scalar(fox_z, fox_z, col(BF)[0:ROWS], None, ALU.add))
                own.sig(V.memset(fox_one, 1.0), fox_gate)

            def fox_rows():
                dve.wait_ge(fox_log, 1)
                link(V.scalar_tensor_tensor(out=fox_l, in0=fox_z, scalar=0.0, in1=fox_l, op0=ALU.min, op1=ALU.subtract))
                link(V.tensor_tensor_scan(fox_c, fox_one, fox_l, 0.0, ALU.mult, ALU.add))

            gate_rows = lambda lo_: fox_c[lo_:lo_ + HEADS].unsqueeze(1).to_broadcast([HEADS, HEADS, S])

            def fox_left():
                dve.wait_ge(fox_const, 1)
                for r in (32, 96):
                    own.sig(V.tensor_copy(foxL[r:r + HEADS], gate_rows(r)))

            def fox_right():
                dve.wait_ge(fox_const, 2)
                for r in (0, 64):
                    own.sig(V.tensor_copy(foxR[r:r + HEADS], gate_rows(r)), fox_ready)

            U = names
            split_to = lambda *key: lambda: used(U[key])
            pipeline(heads_of("moba") + heads_of("fox"), {
                0: [split_to("qb", 0)], 1: [lambda: qk_sums("qb"), split_to("qb", 1)],
                2: [lambda: qk_scale("qb"), split_to("kb", 0)], 3: [lambda: qk_sums("kb"), split_to("kb", 1)],
                4: [lambda: qk_scale("kb"), fox_z_, split_to("f", 0)], 5: [fox_rows, fox_left, split_to("vb", 0)],
                6: [lambda: plain("vb"), split_to("vb", 1)], 7: [fox_right], 8: [split_to("gb", 0)],
                10: [lambda: gate_panel("gb"), split_to("gb", 1)],
                11: [memory_rows], 12: [lambda: lo_chunks("yab0", 4, X)], 14: [split_to("oab", 0, 0)], 17: [split_to("oab", 1, 0)]})
            lo_chunks("yab1", 4, X, 4)
            x_turned(("n", 1), "oab", U["oab", 1, 1], U["qc", 0])

            front("qc", "kc", "vc", "gc")
            dh = heads_of("diff")

            def combine(a, b):
                recip(a)
                recip(b)
                r = rsum[:, 2 * b["g"]:2 * b["g"] + 2]
                link(V.tensor_scalar(r, r, col(NLAM), None, ALU.mult))
                for t, (s, z) in enumerate(a["spans"]):
                    o = a["pb"][:, s:z]
                    own.sig(V.tensor_scalar(o, o, rsum[:, 2 * a["g"] + t:2 * a["g"] + t + 1], None, ALU.mult))
                own.settle()
                for t, (s, z) in enumerate(a["spans"]):
                    ins = V.scalar_tensor_tensor(out=b["nl"][:, s:z], in0=b["pb"][:, s:z], scalar=rsum[:, 2 * b["g"] + t:2 * b["g"] + t + 1],
                                                 in1=a["pb"][:, s:z], op0=ALU.mult, op1=ALU.add)
                    own.sig(ins, norm_ready if t == T - 1 else None)

            extra = {0: [lambda: used(U["qd", 0])], 1: [lambda: qk_sums("qd"), split_to("qd", 1)],
                     2: [lambda: qk_sums("kvd"), split_to("kvd", 0)], 3: [split_to("gd", 0)],
                     4: [lambda: gate_panel("gd"), split_to("gd", 1)]}
            for i in range(4 + 2):
                if i < 4:
                    logits(dh[2 * i])
                    logits(dh[2 * i + 1])
                    combine(dh[2 * i], dh[2 * i + 1])
                if i in (2, 3):
                    qk_scale(("qd", "kvd")[i - 2])
                if i >= 2:
                    h = i - 2
                    k = dh[2 * h + 1]
                    dve.wait_ge(*act_at["ssq", ("sub", h), T - 1])
                    rsqrt(("sub", h), [(("sub", h), T, P)])
                    ps = condition(dve, ("Y", k["g"]))
                    for t in range(T):
                        c = stat["sub", h] + t
                        o = k["gate"](t)
                        ins = V.scalar_tensor_tensor(out=o, in0=ps[:, t * P:(t + 1) * P], scalar=rstd[:, c:c + 1], in1=o, op0=ALU.mult, op1=ALU.mult)
                        own.sig(ins, y_ready if t == T - 1 else None)
                for f in extra.get(i, []):
                    f()
            pipeline(heads_of("swa"), {0: [lambda: lo_chunks(("m", 0), KC, X)], **{n + 2: [lambda n=n: used(U[("xkv", 0, n), 0])] for n in range(4)},
                                       7: [lambda: lo_chunks("ycd0", 4, X)], 8: [split_to("ocd", 0, 0)], 9: [split_to("ocd", 1, 0)]})
            lo_chunks("ycd1", 4, X, 4)

            x_turned(("x", 0), "ocd", U["ocd", 1, 1], U["dq", 0])
            used(U["dp", 0])
            for n, c, chunks in ((2, 3, 2), (0, 0, 2), (1, 2, 1)):
                ps = condition(dve, ("lat", n))
                dve.wait_ge(hiT_ready, lo_T[0] + chunks)
                for k in range(chunks):
                    lo(hT_lo[:, c + k, :], ps[:, k * S:(k + 1) * S], hT_hi[:, c + k, :], evac_gain(("lat", n), k))
            dve.wait_ge(row_ready, row_no["x", 0])
            own.sig(V.tensor_tensor(row_sq, row[:, :], row[:, :], ALU.mult))
            link(V.tensor_tensor(row_rope, rope[:, :], row[:, :], ALU.mult))
            ps = condition(dve, "dp")
            own.sig(V.tensor_tensor(ksum_in, ps[:, 0:S], row_rope, ALU.mult), roped)
            for n, (r0, c0) in enumerate([(0, 0), (64, 64), (0, 64), (64, 0)]):
                ins = V.tensor_copy(halves[r0:r0 + 64, c0:c0 + 64], ident[r0:r0 + 64, r0:r0 + 64])
                own.sig(ins, roped if n == 3 else None)
            ps = condition(dve, "lat_ss")
            V.tensor_tensor(two_halves(lat_var), two_halves(ps[:, :]), row_sq.unsqueeze(1).to_broadcast([P, 2, S]), ALU.mult).then_inc(read_of("lat_ss")[0], 1)
            own.last = read_of("lat_ss")
            own.settle()
            for n, w in enumerate((MLA_QL, MLA_KVL)):
                a = lat_var[:, n * S:(n + 1) * S]
                own.sig(V.tensor_scalar(a, a, 1.0 / w, EPS, ALU.mult, ALU.add), var_ready if n else None)
            used(U["dq", 1])
            chains[0] += 1
            dve.wait_ge(guess_ready, chains[0])
            link(V.tensor_tensor(lat_tmp, lat_guess, lat_guess, ALU.mult))
            link(V.tensor_tensor(lat_tmp, lat_tmp, lat_var, ALU.mult))
            link(V.tensor_scalar(lat_tmp, lat_tmp, -0.5, 1.5, ALU.mult, ALU.add))
            link(V.tensor_tensor(lat_tmp, lat_tmp, lat_guess, ALU.mult))
            own.sig(V.tensor_tensor(k_scale, lat_tmp[:, S:2 * S], row[:, :], ALU.mult), lat_scales)
            link(V.tensor_tensor(q_scale[:, 0:S], lat_tmp[:, 0:S], row[:, :], ALU.mult))
            link(V.tensor_tensor(q_scale[:, S:2 * S], q_scale[:, 0:S], rope[:, :], ALU.mult))
            ps = condition(dve, "v_scales")
            c = stat["latv"]
            own.sig(V.tensor_copy(rstd[:, c:c + T], ps[:, 0:T]), v_scales)

            def mla_inputs(h):
                ps = condition(dve, ("q", h))
                own.sig(V.tensor_tensor(arena[:, MLA_PANELS[h % 5], 0:2 * S], ps[:, :], q_scale, ALU.mult), q_ready)
                ps = condition(dve, ("kv", h))
                dve.wait_ge(v_ready, 2 * h + 2)
                own.sig(V.tensor_tensor(mla_buf(h, 2), ps[:, 0:S], k_scale, ALU.mult), q_ready)
                used(U["uh", h])

            def deep(ks, inputs, dst, after={}):
                for i in range(len(ks) + 3):
                    if i >= 3:
                        y_lo(ks[i - 3], dst)
                    if 1 <= i <= len(ks):
                        normalise(ks[i - 1])
                    if i < len(ks):
                        logits(ks[i])
                    inputs(i + 2)
                    for f in after.get(i, []):
                        f()

            mla_inputs(0)
            mla_inputs(1)
            deep(heads_of("mla"), lambda h: mla_inputs(h) if h < HEADS else None, X,
                 {8: [split_to("omla", 0, 0)], 9: [split_to("omla", 1, 0)]})

            def cross(i, last, before):
                x_turned(("c", i), last, before)
                dve.wait_ge(row_ready, row_no["c", i])
                for n in range(2):
                    ps = condition(dve, ("xq", i, n))
                    own.sig(V.tensor_tensor(two_halves(pan(0, n)), two_halves(ps[:, :]), row2, ALU.mult), xq_ready)
                used(U[("xq", i, 1), 0])
                deep(heads_of("xa", layer=i), lambda h: None, H)

            hb = hT_blocks(hT_hi), hT_blocks(hT_lo)

            def mlp(i):
                x_turned(("p", i), ("xo", i), U[("xo", i, 1), 0], U["mlp", i])
                u0, h0 = names["mlp", i], 2 * NBLK * i

                def step(blk, u, it=None):
                    odd = blk % 2
                    du, db = (0, 0) if it is None else (it * 8, it * 2)
                    if it is None:
                        splits(u + 6)
                    else:
                        split_one(u + 4, du)
                        split_one(u + 5, du)
                    for p in range(2):
                        dve.wait_ge(relu_ready, h0 + 2 * blk + p + 1 + 2 * db)
                        if p == 0 and (blk > 0 or i > 0):
                            dve.wait_ge(hT_ready, h0 + 2 * blk + 2 * db)
                        V.tensor_tensor(pan(5, p), pan(4, p), pan(4, p), ALU.mult).then_inc(h_ready, 1)
                    for p in range(2):
                        dve.wait_ge(hhi_ready, h0 + 2 * blk + p + 1 + 2 * db)
                        V.tensor_tensor(hb[1][:, 2 * odd + p, :], pan(5, p), hb[0][:, 2 * odd + p, :].bitcast(F32),
                                        ALU.subtract).then_inc(hT_ready, 1)
                    if it is not None:
                        split_one(u + 6, du)
                        split_one(u + 7, du)

                used(u0 - 1)
                step(0, u0)
                step(1, u0 + 2)
                splits(u0 + 10)
                with dve.Fori(0, (NBLK - 4) // 2) as it:
                    step(2, u0 + 6, it)
                    step(3, u0 + 10, it)
                done[0] = u0 + 6 + 8 * ((NBLK - 4) // 2) + RING
                for blk in (NBLK - 2, NBLK - 1):
                    u = u0 + 6 + 4 * (blk - 2)
                    step(blk, u)
                    splits(u + 8)

            cross(0, "omla", U["omla", 1, 1])
            mlp(0)

            x_turned(("x", 1), ("mlp", 0), U["mlp", 0] + 4 * NBLK - 1)
            for n in range(4):
                used(U[("sv", n), 0])
            for a, z in ((0, P), (2 * P, 3 * P)):
                own.sig(V.scalar_tensor_tensor(out=strict[:, a:z], in0=ident[:, :], scalar=-BIG, in1=causal[:, a:z], op0=ALU.mult, op1=ALU.add))
            link(V.tensor_copy(strict[:, P:2 * P], causal[:, P:2 * P]))
            dve.wait_ge(row_ready, row_no["x", 1])

            def sqk(h):
                ps = condition(dve, ("sqk", h))
                own.sig(V.tensor_tensor(two_halves(sb_qk(h)), two_halves(ps[:, :]), row2, ALU.mult), sqk_ready)
                used(U["sqk", h])

            sqk(0)
            sqk(1)
            ks = heads_of("sb")
            for i in range(HEADS + 3):
                if i >= 3:
                    y_lo(ks[i - 3], H)
                if 1 <= i <= HEADS:
                    g = ks[i - 1]["g"]
                    z, l, w, r = (sbuf_of(n, i - 1) for n in range(4))
                    dve.wait_ge(sb_log, i)
                    if i >= 3:
                        dve.wait_ge(probs_ready, g - 1)
                    link(V.scalar_tensor_tensor(out=w, in0=z, scalar=0.0, in1=l, op0=ALU.max, op1=ALU.add))
                    for a, e in ks[i - 1]["spans"]:
                        own.sig(V.tensor_tensor_scan(r[:, a:e][:, ::-1], w[:, a:e][:, ::-1], w[:, a:e][:, ::-1], 0.0, ALU.add, ALU.bypass))
                    own.settle()
                    own.sig(V.tensor_tensor(w, z, r, ALU.subtract), sb_w)
                if i < HEADS:
                    ps = condition(dve, ("S", ks[i]["g"]))
                    own.settle()
                    own.sig(V.scalar_tensor_tensor(out=sbuf_of(0, i), in0=ps[:, 0:384], scalar=ks[i]["scale"], in1=strict,
                                                   op0=ALU.mult, op1=ALU.add), logits_ready)
                if i + 2 < HEADS:
                    sqk(i + 2)
                if i == 4:
                    dve.wait_ge(mem_in, 32)
                    for t in range(T):
                        own.sig(V.tensor_scalar(mem[:, t, :], mem[:, t, :], rs("mem", t), None, ALU.mult), mem_ready)
                if i == 6:
                    lo_chunks(("m", 1), KC, X)
                if i >= 7:
                    used(U[("xkv", 1, i - 7), 0])
            cross(1, "osb", U["osb", 1, 1])
            mlp(1)
            for n in range(2):
                residual(("mlp", 1), n)

            dve.wait_ge(*act_at["ssq", "final", T - 1])
            rsqrt("final", [("final", T, D)])
            dve.wait_ge(final_in, 16)
            for t in range(T):
                c = stat["final"] + t
                own.sig(V.scalar_tensor_tensor(out=xn[:, t, :], in0=x[:, t, :], scalar=rstd[:, c:c + 1], in1=final_gain,
                                               op0=ALU.mult, op1=ALU.mult), out_ready)

        @block.gpsimd
        def _(pool):
            G = nc.gpsimd
            own = Order(pool, pool_chain)

            def link(ins, s=None):
                own.sig(ins, s)
                own.settle()

            link(G.memset(ident[:, :], 0.0))
            own.sig(G.memset(col(BF), 0.0))
            link(G.affine_select(out=ident[:, :], in_=ident[:, :], compare_op=ALU.not_equal, fill=1.0, base=0, pattern=[[-1, P]], channel_multiplier=1), setup_ready)
            link(G.memset(col(PHASE), 0.0))
            link(G.memset(col(TURN), 0.0))
            link(G.memset(small[0:64, PHASE:PHASE + 1], math.pi / 2))
            link(G.memset(small[0:64, TURN:TURN + 1], 0.25))
            for j in range(32):
                f = float(np.float32(10000.0 ** (-2.0 * j / ROPE)))
                own.sig(G.memset(arena[0:1, 9, j:j + 97:32], f))
            link(G.memset(arena[0:1, 9, P:P + 1], 1.0), setup_ready)
            rel_i = arena[:, 10, 512:896].bitcast(I32)
            own.sig(G.iota(rel_i[:, 0:P], [[-1, P]], base=0, channel_multiplier=1))
            link(G.iota(rel_i[:, P:384], [[-1, S]], base=P, channel_multiplier=1))
            link(G.tensor_copy(rel[:, :], rel_i))
            link(G.memset(causal[:, :], 0.0))
            for a, base in ((0, 0), (2 * P, 0)):
                for buf, fill in ((rel, BIG), (causal, -BIG)):
                    link(G.affine_select(out=buf[:, a:a + P], in_=buf[:, a:a + P], compare_op=ALU.is_ge, fill=fill, base=base, pattern=[[-1, P]], channel_multiplier=1))
            own.sig(G.memset(col(ONE), 1.0), setup_ready)
            done = []
            for n, (g, factor, kind) in enumerate(tables):
                if n in (2, 6):
                    buf, first, fill = (foxL, 0, -1.0) if n == 2 else (foxR, 32, 1.0)
                    if n == 2:
                        pool.wait_ge(qkT_ready, 1)
                    else:
                        pool.wait_ge(qkT_ready, 8)
                    for _ in range(1):
                        link(G.memset(buf, 0.0))
                        for half in range(2):
                            link(G.affine_select(out=buf, in_=buf, compare_op=ALU.not_equal, fill=fill, base=-first - HD * half,
                                                 pattern=[[-1, HEADS], [0, S]], channel_multiplier=1), fox_const if half else None)
                if kind == "window" and "window" not in done:
                    done.append("window")
                    own.settle()
                    m = rel[:, P:2 * P]
                    link(G.affine_select(out=m, in_=m, compare_op=ALU.is_gt, fill=BIG, base=0, pattern=[[1, P]], channel_multiplier=-1))
                if n >= 2:
                    pool.wait_ge(logits_ready, tables[n - 1][0])
                own.sig(G.tensor_scalar(alibi[:, n % 2, :], rel[:, :], factor, None, ALU.mult), table_ready)

        @block.sync
        def _(sp):
            def weight(u, src=None, du=0):
                if u >= RAW:
                    sp.wait_ge(lo_ready, u - RAW + 1 + du)
                width, pieces = units[u]
                for c0, chunks, cols, pitch, ap in pieces:
                    if src is not None:
                        ap = src
                    o = raw[:, u % RAW, :]
                    if cols == pitch:
                        o = o[:, c0:c0 + chunks * cols].rearrange("p (c n) -> p c n", c=chunks)
                    else:
                        first = c0 - c0 % pitch
                        o = o[:, first:first + chunks * pitch].rearrange("p (c n) -> p c n", c=chunks)[:, :, c0 % pitch:c0 % pitch + cols]
                    sp.dma_start(o, ap).then_inc(w_in[u % RAW], 16)

            tok = lambda ap: ap[0].rearrange("(t p) n -> p t n", p=P)
            def gain_rows(r0, n, ap):
                o = stage[r0:r0 + n, :]
                o = o if len(ap.shape) == 2 else o.rearrange("p (h d) -> p h d", h=2)
                sp.dma_start(o, ap).then_inc(stage_in if r0 else first_gains_in, 16)

            for t in range(T):
                sp.dma_start(x[:, t, :], tok(A["x"])[:, t, :]).then_inc(x_in, 16)
            gain_rows(*gain_loads[0])
            for u in range(RAW):
                weight(u)
            for load in gain_loads[1:]:
                gain_rows(*load)
            sp.wait_ge(setup_ready, 1)
            loads = [(pos_i, A["positions_2"].to_broadcast([P, S])), (col(SINK, 8), A["swa_sinks"].to_broadcast([P, HEADS])),
                     (lam_in, A["diff_lambda"].rearrange("a b c -> a (b c)").to_broadcast([P, 4 * HD])),
                     *((small[r:r + HEADS, BF:BF + 1], A["b_forget"].rearrange("a h -> h a")) for r in GATE_ROWS)]
            assert len(loads) == SMALL_LOADS
            for o, i_ in loads:
                sp.dma_start(o, i_).then_inc(small_in, 16)
            for u in range(RAW, names["va", 0]):
                weight(u)
            sp.dma_start(mem[:, :, :], tok(A["mem_2"])).then_inc(mem_in, 16)

            def mlp(i):
                u0 = names["mlp", i]
                for u in range(u0, u0 + 6):
                    weight(u)
                win = A["mlp_w_in_2"][i].rearrange("(c p) n -> p c n", p=P)
                wout = A["mlp_w_out_2"][i].rearrange("(c p) n -> p c n", p=P)
                loops = (NBLK - 2) // 2
                with sp.Fori(0, loops) as it:
                    for s in range(2):
                        u = u0 + 6 + 4 * s
                        for n in range(2):
                            weight(u + n, win[:, 4 * n:4 * n + 4, bass.ds(it * (2 * BLK) + (2 + s) * BLK, BLK)], it * 8)
                        for n in range(2):
                            weight(u + 2 + n, wout[:, bass.ds(it * 8 + 4 * (1 + s), 4), n * PANEL:(n + 1) * PANEL], it * 8)
                for u in range(u0 + 6 + 8 * loops, u0 + 4 * NBLK):
                    weight(u)

            for u in range(names["va", 0], names["mlp", 0]):
                weight(u)
            mlp(0)
            sp.wait_ge(x_ready, 16)
            sp.dma_start(mem[:, :, :], tok(A["mem_2"])).then_inc(mem_in, 16)
            for u in range(names["mlp", 0] + 4 * NBLK, names["mlp", 1]):
                weight(u)
            mlp(1)
            sp.dma_start(final_gain, A["norm_final_2"].rearrange("(a n) -> a n", a=1).to_broadcast([P, D])).then_inc(final_in, 16)
            o = tok(out)
            for t in range(T):
                sp.wait_ge(out_ready, t + 1)
                sp.dma_start(o[:, t, :], xn[:, t, :]).then_inc(out_done, 16)
            sp.wait_ge(out_done, 16 * T)


_NAMES = ["x", "norm_gain", "w_in_ab", "b_forget", "moba_q_gain", "moba_k_gain", "fox_q_gain", "fox_k_gain", "w_out_ab",
          "w_in_cd", "diff_q_gain", "diff_k_gain", "diff_lambda", "diff_subln_gain", "swa_q_gain", "swa_k_gain", "swa_sinks",
          "w_out_cd", "mem_2", "positions_2", "norm_mix_2", "norm_cross_2", "norm_mem_2", "norm_mlp_2", "norm_final_2",
          "mla_w_dkv_2", "mla_g_q_2", "mla_g_kv_2", "mla_w_uq_2", "mla_w_ukv_2", "mla_w_o_2", "sb_w_qkv_2", "sb_w_o_2",
          "xa_w_q_2", "xa_w_kv_2", "xa_w_o_2", "mlp_w_in_2", "mlp_w_out_2"]


def kernel(**inputs):
    import concourse.bacc as bacc
    from concourse.bass_utils import run_bass_kernel_spmd

    nc = bacc.Bacc("TRN2", target_bir_lowering=False, num_devices=1)
    arrays, aps = {}, {}
    for name in _NAMES:
        a = np.ascontiguousarray(inputs[name])
        arrays[f"in_{name}"] = a
        aps[name] = nc.dram_tensor(f"in_{name}", a.shape, mybir.dt.from_np(a.dtype), kind="ExternalInput").ap()
    out = nc.dram_tensor("out", (1, S, D), F32, kind="ExternalOutput").ap()
    build(nc, aps, out)
    result = run_bass_kernel_spmd(nc, [arrays], core_ids=[0])
    return result.results[0]["out"]
```
